# Optimizing a Trainium2 kernel written in Bass

```python
import math
import jax, jax.numpy as jnp
from jax import lax
import numpy as np

"""One inference step of a hybrid diffusion / flow-matching trunk, run on two request groups with shared weights.

Trunk: DEPTH interleaved layers. Layer i uses token mixer i % 3 (0 = multi-scale pooling, 1 = bidirectional HGRN2
gated linear recurrence, 2 = differential attention), then a gated MLP with a 3x3 depthwise convolution between the
up-projection and the activation. Every sub-layer is pre-RMSNorm, adaLN modulated (shift, scale, gate from SiLU(cond)
through a per-layer linear map) and added residually; one final RMSNorm. Context tokens are an un-noised prefix of
the same trunk, modulated by c_ctx, and read only context tokens; latent tokens read all context + latent tokens.

Inputs:
  x_prompt   (BATCH, SEQ, D_MODEL)           context tokens of new requests (group i)
  x_sample   (DEC_BATCH, DEC_SEQ, D_MODEL)   noisy latent tokens, grid (DEC_SEQ // GRID_W, GRID_W) (group ii)
  state_hgrn (DEC_BATCH, N_HGRN, 2, HGRN_HEADS, HGRN_DK, HGRN_DV)  final context scan states (fwd, bwd)
  cache_k    (DEC_BATCH, N_DIFF, PAST_LEN, DIFF_HEADS, 2, DIFF_HEAD_DIM)  context keys of both maps
  cache_v    (DEC_BATCH, N_DIFF, PAST_LEN, DIFF_HEADS, 2 * DIFF_HEAD_DIM) context values
  c          (DEC_BATCH, D_MODEL)   conditioning vectors of the denoising requests
  c_ctx      (D_MODEL,)             learned modulation vector for context tokens
  followed by the weights.
Returns (y_prompt, y_sample, new_state_hgrn, new_cache_k, new_cache_v):
  y_prompt       (BATCH, SEQ, D_MODEL)
  y_sample       (DEC_BATCH, DEC_SEQ, D_MODEL)
  new_state_hgrn (BATCH, N_HGRN, 2, HGRN_HEADS, HGRN_DK, HGRN_DV)
  new_cache_k    (BATCH, N_DIFF, SEQ, DIFF_HEADS, 2, DIFF_HEAD_DIM)
  new_cache_v    (BATCH, N_DIFF, SEQ, DIFF_HEADS, 2 * DIFF_HEAD_DIM)
"""

D_MODEL = 1024
BATCH = 1
SEQ = 128
DEPTH = 4
DEC_BATCH = 1
DEC_SEQ = 512
PAST_LEN = 256

GRID_W = 64
N_MIXERS = 3
N_POOL = (DEPTH + 2) // 3
N_HGRN = (DEPTH + 1) // 3
N_DIFF = DEPTH // 3

POOL_WINDOWS = (2, 4, 8, 16)
POOL_GROUP = D_MODEL // len(POOL_WINDOWS)

HGRN_EXPAND = 128
HGRN_HEADS = D_MODEL // HGRN_EXPAND
HGRN_DK = HGRN_EXPAND
HGRN_DV = D_MODEL // HGRN_HEADS
CHUNK = 32

DIFF_HEAD_DIM = 64
DIFF_HEADS = D_MODEL // (2 * DIFF_HEAD_DIM)
Q_BLOCK = 128
ROPE_BASE = 10000.0

D_FF = ((8 * D_MODEL // 3) + 127) // 128 * 128
CONV_W = 3
EPS = 1e-6

kernel_name = 'hybrid_diffusion_pool_hgrn2_diffattn_step'

F32 = jnp.float32

def rms_norm(x, g):
    xf = x.astype(F32)
    y = xf * lax.rsqrt(jnp.mean(xf * xf, axis=-1, keepdims=True) + EPS)
    return (y * g.astype(F32)).astype(x.dtype)

def modulation(cond, w, b, dtype):
    m = jax.nn.silu(cond.astype(F32)) @ w.astype(F32) + b.astype(F32)
    return [a[:, None, :].astype(dtype) for a in jnp.split(m, 6, axis=-1)]

def box_mean_1d(x, w, axis):
    n = x.shape[axis]
    cs = jnp.cumsum(x.astype(F32), axis=axis)
    cs = jnp.concatenate([jnp.zeros_like(lax.slice_in_dim(cs, 0, 1, axis=axis)), cs], axis=axis)
    t = jnp.arange(n)
    lo = jnp.clip(t - w // 2, 0, n)
    hi = jnp.clip(t + w // 2, 0, n)
    s = jnp.take(cs, hi, axis=axis) - jnp.take(cs, lo, axis=axis)
    shape = [1] * x.ndim
    shape[axis] = n
    return s / (hi - lo).astype(F32).reshape(shape)

def pool_mixer(h, rows, cols, w_pool, scale):
    bsz, n, _ = h.shape
    hg = h.reshape(bsz, rows, cols, len(POOL_WINDOWS), POOL_GROUP)
    outs = []
    for g, w in enumerate(POOL_WINDOWS):
        xg = hg[..., g, :]
        m = box_mean_1d(box_mean_1d(xg, w, 1), w, 2)
        outs.append(m - xg.astype(F32))
    d = jnp.stack(outs, axis=3)
    y = jnp.einsum('brwgi,gio->brwgo', d, w_pool.astype(F32))
    return (y.reshape(bsz, n, D_MODEL) * scale.astype(F32)).astype(h.dtype)

def conv_ffn(h, rows, cols, w_up, conv_w, conv_b, w_down):
    bsz, n, _ = h.shape
    u = (h @ w_up).reshape(bsz, rows, cols, 2 * D_FF)
    u = lax.conv_general_dilated(u, conv_w[:, :, None, :].astype(u.dtype), window_strides=(1, 1),
                                 padding='SAME', dimension_numbers=('NHWC', 'HWIO', 'NHWC'),
                                 feature_group_count=2 * D_FF) + conv_b
    a, v = jnp.split(u, 2, axis=-1)
    return (jax.nn.silu(a) * v).reshape(bsz, n, D_FF) @ w_down

def gla_scan(q, k, v, logf, s0):
    bsz, n, nh, _ = q.shape
    nc = n // CHUNK

    def chunks(a):
        return a.reshape(bsz, nc, CHUNK, nh, a.shape[-1]).transpose(1, 0, 3, 2, 4)

    lower = jnp.tril(jnp.ones((CHUNK, CHUNK), dtype=bool))[:, :, None]

    def step(state, inp):
        qc, kc, vc, fc = inp
        cum = jnp.cumsum(fc, axis=2)
        rel = cum[:, :, :, None, :] - cum[:, :, None, :, :]
        decay = jnp.exp(jnp.where(lower, rel, -jnp.inf))
        scores = jnp.einsum('bhtc,bhsc,bhtsc->bhts', qc, kc, decay)
        out = (jnp.einsum('bhts,bhsv->bhtv', scores, vc)
               + jnp.einsum('bhtc,bhcv->bhtv', qc * jnp.exp(cum), state))
        last = cum[:, :, -1:, :]
        state = (jnp.exp(last[:, :, 0, :])[..., None] * state
                 + jnp.einsum('bhsc,bhsv->bhcv', kc * jnp.exp(last - cum), vc))
        return state, out

    state, out = lax.scan(step, s0, (chunks(q), chunks(k), chunks(v), chunks(logf)))
    return out.transpose(1, 0, 3, 2, 4).reshape(bsz, n, nh, v.shape[-1]), state

def hgrn_mixer(h, w_in, lb_param, layer_idx, norm_g, w_out, s0):
    bsz, n, _ = h.shape
    q, iv, g, zf, zb = jnp.split((h @ w_in).astype(F32), 5, axis=-1)
    lbs = jax.nn.softmax(lb_param.astype(F32), axis=1)
    lbs = jnp.cumsum(lbs, axis=1) - lbs[:, :1]
    lb = lbs[:, layer_idx].reshape(2, HGRN_HEADS, HGRN_DK)

    def heads(a):
        return a.reshape(bsz, n, HGRN_HEADS, -1)

    q, iv, g = heads(q), heads(iv), heads(g)
    f_fw = lb[0] + (1.0 - lb[0]) * jax.nn.sigmoid(heads(zf))
    f_bw = lb[1] + (1.0 - lb[1]) * jax.nn.sigmoid(heads(zb))
    s0 = s0.astype(F32)
    o_fw, s_fw = gla_scan(q, 1.0 - f_fw, iv, jnp.log(f_fw), s0[:, 0])

    def rev(a):
        return a[:, ::-1]

    o_bw, s_bw = gla_scan(rev(q), rev(1.0 - f_bw), rev(iv), rev(jnp.log(f_bw)), s0[:, 1])
    o = rms_norm(o_fw + rev(o_bw), norm_g) * jax.nn.silu(g)
    y = o.reshape(bsz, n, D_MODEL) @ w_out.astype(F32)
    return y.astype(h.dtype), jnp.stack([s_fw, s_bw], axis=1)

def axial_rope(x):
    n = x.shape[1]
    t = jnp.arange(n)
    half = DIFF_HEAD_DIM // 2
    nf = half // 2
    inv = ROPE_BASE ** (-jnp.arange(nf, dtype=F32) / nf)

    def rot(xa, pos):
        ang = pos.astype(F32)[:, None] * inv
        cos = jnp.cos(ang)[None, :, None, None, :]
        sin = jnp.sin(ang)[None, :, None, None, :]
        x1, x2 = jnp.split(xa.astype(F32), 2, axis=-1)
        return jnp.concatenate([x1 * cos - x2 * sin, x2 * cos + x1 * sin], axis=-1)

    out = jnp.concatenate([rot(x[..., :half], t // GRID_W), rot(x[..., half:], t % GRID_W)], axis=-1)
    return out.astype(x.dtype)

def diff_attention(q, k, v, lam):
    bsz, nq = q.shape[:2]
    nb = nq // Q_BLOCK
    qb = q.astype(F32).reshape(bsz, nb, Q_BLOCK, DIFF_HEADS, 2, DIFF_HEAD_DIM).transpose(1, 0, 2, 3, 4, 5)
    kf, vf = k.astype(F32), v.astype(F32)
    scale = DIFF_HEAD_DIM ** -0.5

    def block(qi):
        p = jax.nn.softmax(jnp.einsum('bqhcd,bkhcd->bhcqk', qi, kf) * scale, axis=-1)
        w = p[:, :, 0] - lam * p[:, :, 1]
        return jnp.einsum('bhqk,bkhe->bqhe', w, vf)

    out = lax.map(block, qb)
    return out.transpose(1, 0, 2, 3, 4).reshape(bsz, nq, DIFF_HEADS, 2 * DIFF_HEAD_DIM)

def trunk_layer(x, cond, i, p, rows, cols, cache):
    sh1, sc1, gt1, sh2, sc2, gt2 = modulation(cond, p['ada_w'][i], p['ada_b'][i], x.dtype)
    h = rms_norm(x, p['norm1'][i]) * (1 + sc1) + sh1
    kind, j = i % N_MIXERS, i // N_MIXERS
    produced = None
    bsz, n, _ = x.shape
    if kind == 0:
        y = pool_mixer(h, rows, cols, p['pool_w'][j], p['pool_scale'][j])
    elif kind == 1:
        if cache is None:
            s0 = jnp.zeros((bsz, 2, HGRN_HEADS, HGRN_DK, HGRN_DV), F32)
        else:
            s0 = cache['state_hgrn'][:, j]
        y, produced = hgrn_mixer(h, p['hgrn_w_in'][j], p['hgrn_lb'], i, p['hgrn_norm'][j],
                                 p['hgrn_w_out'][j], s0)
    else:
        q, k, v = jnp.split(h @ p['diff_w_in'][j], 3, axis=-1)
        q = q.reshape(bsz, n, DIFF_HEADS, 2, DIFF_HEAD_DIM)
        k = k.reshape(bsz, n, DIFF_HEADS, 2, DIFF_HEAD_DIM)
        v = v.reshape(bsz, n, DIFF_HEADS, 2 * DIFF_HEAD_DIM)
        if cache is None:
            produced = (k, v)
        else:
            q, k = axial_rope(q), axial_rope(k)
            k = jnp.concatenate([cache['cache_k'][:, j].astype(k.dtype), k], axis=1)
            v = jnp.concatenate([cache['cache_v'][:, j].astype(v.dtype), v], axis=1)
        lam_init = 0.8 - 0.6 * math.exp(-0.3 * i)
        lp = p['diff_lambda'][j].astype(F32)
        lam = jnp.exp(jnp.sum(lp[0] * lp[1])) - jnp.exp(jnp.sum(lp[2] * lp[3])) + lam_init
        o = diff_attention(q, k, v, lam)
        o = rms_norm(o, p['diff_subln'][j]) * (1.0 - lam_init)
        y = o.reshape(bsz, n, D_MODEL) @ p['diff_w_out'][j].astype(F32)
    x = x + gt1 * y.astype(x.dtype)
    h = rms_norm(x, p['norm2'][i]) * (1 + sc2) + sh2
    f = conv_ffn(h, rows, cols, p['ffn_w_up'][i], p['ffn_conv_w'][i], p['ffn_conv_b'][i], p['ffn_w_down'][i])
    x = x + gt2 * f.astype(x.dtype)
    return x, produced

def setup_inputs(seed: int = 0) -> dict:
    key = jax.random.key(seed)
    ks = jax.random.split(key, 32)
    nrm = jax.random.normal
    d = D_MODEL
    return {
        'x_prompt': nrm(ks[0], (BATCH, SEQ, d), F32),
        'x_sample': nrm(ks[1], (DEC_BATCH, DEC_SEQ, d), F32),
        'state_hgrn': nrm(ks[2], (DEC_BATCH, N_HGRN, 2, HGRN_HEADS, HGRN_DK, HGRN_DV), F32),
        'cache_k': nrm(ks[3], (DEC_BATCH, N_DIFF, PAST_LEN, DIFF_HEADS, 2, DIFF_HEAD_DIM), F32),
        'cache_v': nrm(ks[4], (DEC_BATCH, N_DIFF, PAST_LEN, DIFF_HEADS, 2 * DIFF_HEAD_DIM), F32),
        'c': nrm(ks[5], (DEC_BATCH, d), F32),
        'c_ctx': nrm(ks[6], (d,), F32),
        'ada_w': nrm(ks[7], (DEPTH, d, 6 * d), F32) * (0.5 * d ** -0.5),
        'ada_b': nrm(ks[8], (DEPTH, 6 * d), F32) * 0.01,
        'norm1': 1.0 + 0.02 * nrm(ks[9], (DEPTH, d), F32),
        'norm2': 1.0 + 0.02 * nrm(ks[10], (DEPTH, d), F32),
        'final_norm': 1.0 + 0.02 * nrm(ks[11], (d,), F32),
        'pool_w': nrm(ks[12], (N_POOL, len(POOL_WINDOWS), POOL_GROUP, POOL_GROUP), F32) * POOL_GROUP ** -0.5,
        'pool_scale': 1.0 + 0.02 * nrm(ks[13], (N_POOL, d), F32),
        'hgrn_w_in': nrm(ks[14], (N_HGRN, d, 5 * d), F32) * d ** -0.5,
        'hgrn_lb': nrm(ks[15], (2, DEPTH, d), F32) * 0.5,
        'hgrn_norm': 1.0 + 0.02 * nrm(ks[16], (N_HGRN, HGRN_DV), F32),
        'hgrn_w_out': nrm(ks[17], (N_HGRN, d, d), F32) * d ** -0.5,
        'diff_w_in': nrm(ks[18], (N_DIFF, d, 3 * d), F32) * d ** -0.5,
        'diff_lambda': nrm(ks[19], (N_DIFF, 4, DIFF_HEAD_DIM), F32) * 0.1,
        'diff_subln': 1.0 + 0.02 * nrm(ks[20], (N_DIFF, 2 * DIFF_HEAD_DIM), F32),
        'diff_w_out': nrm(ks[21], (N_DIFF, d, d), F32) * d ** -0.5,
        'ffn_w_up': nrm(ks[22], (DEPTH, d, 2 * D_FF), F32) * d ** -0.5,
        'ffn_conv_w': nrm(ks[23], (DEPTH, CONV_W, CONV_W, 2 * D_FF), F32) * (1.0 / CONV_W),
        'ffn_conv_b': nrm(ks[24], (DEPTH, 2 * D_FF), F32) * 0.01,
        'ffn_w_down': nrm(ks[25], (DEPTH, D_FF, d), F32) * D_FF ** -0.5,
    }

def reference(x_prompt, x_sample, state_hgrn, cache_k, cache_v, c, c_ctx, ada_w, ada_b, norm1, norm2,
              final_norm, pool_w, pool_scale, hgrn_w_in, hgrn_lb, hgrn_norm, hgrn_w_out, diff_w_in,
              diff_lambda, diff_subln, diff_w_out, ffn_w_up, ffn_conv_w, ffn_conv_b, ffn_w_down):
    p = dict(ada_w=ada_w, ada_b=ada_b, norm1=norm1, norm2=norm2, pool_w=pool_w, pool_scale=pool_scale,
             hgrn_w_in=hgrn_w_in, hgrn_lb=hgrn_lb, hgrn_norm=hgrn_norm, hgrn_w_out=hgrn_w_out,
             diff_w_in=diff_w_in, diff_lambda=diff_lambda, diff_subln=diff_subln, diff_w_out=diff_w_out,
             ffn_w_up=ffn_w_up, ffn_conv_w=ffn_conv_w, ffn_conv_b=ffn_conv_b, ffn_w_down=ffn_w_down)
    cache = dict(state_hgrn=state_hgrn, cache_k=cache_k, cache_v=cache_v)
    ctx_cond = c_ctx[None, :]
    rows = x_sample.shape[1] // GRID_W
    xp, xs = x_prompt, x_sample
    states, keys, vals = [], [], []
    for i in range(DEPTH):
        xp, produced = trunk_layer(xp, ctx_cond, i, p, 1, xp.shape[1], None)
        if i % N_MIXERS == 1:
            states.append(produced)
        elif i % N_MIXERS == 2:
            keys.append(produced[0])
            vals.append(produced[1])
        xs, _ = trunk_layer(xs, c, i, p, rows, GRID_W, cache)
    y_prompt = rms_norm(xp, final_norm)
    y_sample = rms_norm(xs, final_norm)
    new_state_hgrn = jnp.stack(states, axis=1)
    new_cache_k = jnp.stack(keys, axis=1)
    new_cache_v = jnp.stack(vals, axis=1)
    return (y_prompt, y_sample, new_state_hgrn, new_cache_k, new_cache_v)


_drawn_inputs = setup_inputs


def setup_inputs(seed=0):
    import zlib

    import numpy as np

    out = dict(_drawn_inputs(seed))
    spreads = {}
    factors = {'state_hgrn': 3.899,
     'norm2': 5.27,
     'final_norm': 7.848,
     'pool_scale': 6.048,
     'hgrn_norm': 33.468,
     'diff_lambda': 4.461,
     'diff_subln': 63.87,
     'ffn_conv_b': 8.0}
    for name, (base, spread) in spreads.items():
        noise = np.random.default_rng([zlib.crc32(name.encode()), seed]).standard_normal(out[name].shape)
        drawn = base * np.exp(spread * noise) if base else spread * noise
        out[name] = __import__('jax').numpy.asarray(drawn.astype(out[name].dtype))
    for name, factor in factors.items():
        out[name] = (out[name] * factor).astype(out[name].dtype)
    return out
```

```python
from contextlib import ExitStack
import math

import concourse.bass as bass
from concourse import mybir

F32 = mybir.dt.float32
F32R = mybir.dt.float32r
U32 = mybir.dt.uint32
ACT = mybir.ActivationFunctionType
ALU = mybir.AluOpType
AX = mybir.AxisListType

P = 128
D_MODEL = 1024
KT = D_MODEL // P
N_SAMPLE, N_PROMPT = 512, 128
T = N_SAMPLE + N_PROMPT
GRID_W = 64
ROWS = N_SAMPLE // GRID_W
DEPTH = 4
D_FF = ((8 * D_MODEL // 3) + 127) // 128 * 128
NPAIR = D_FF // P
HEADS = 8
LEVELS = 7
PAST = 256
EPS = 1e-6
KINDS = [i % 3 for i in range(DEPTH)]
CHUNKS_MOD = 48
MOD_PIECES = CHUNKS_MOD // 4
RING_G = 10
SEGMENTS = [("up", 0, 8), ("up", 8, 2), ("down", 0, 8), ("up", 10, 6), ("up", 16, 2), ("down", 8, 8),
            ("up", 18, 2), ("up", 20, 2), ("down", 16, 6)]
RANGES = [(0, N_SAMPLE, 0), (N_SAMPLE, T, 1)]
SLOTS = 4
SCALE = 64 ** -0.5
POOL_WINDOWS = (2, 4, 8, 16)


def job_plan():
    jobs = []
    for layer, kind in enumerate(KINDS):
        if kind == 1:
            for h in range(HEADS):
                jobs += [("hgrn_in", layer, part * HEADS + h, KT) for part in (0, 3, 4, 1, 2)]
            jobs += [("hgrn_out", layer, o, KT) for o in range(KT)]
        elif kind == 2:
            for h in range(HEADS):
                jobs += [("diff_in", layer, part * HEADS + h, KT) for part in (0, 1, 2)]
            jobs += [("diff_out", layer, o, KT) for o in range(KT)]
        for what, p0, n in SEGMENTS:
            if what == "up":
                for p in range(p0, p0 + n):
                    jobs += [("up", layer, p, KT), ("up", layer, NPAIR + p, KT)]
            else:
                jobs += [("down", layer, (p0, n, o), n) for o in range(KT)]
    return jobs


JOBS = job_plan()
NJOBS = len(JOBS)


def trunk(nc, dram):
    ctx = ExitStack()
    with ctx:
        def sb(name, shape, dt=F32):
            return ctx.enter_context(nc.sbuf_tensor(name, shape, dt))

        def sem(name):
            return ctx.enter_context(nc.semaphore(name))

        x = sb("x", [P, KT, T])
        h_base = nc.sbuf_base
        h_hi = sb("h_hi", [P, KT, T], F32R)
        h_lo = sb("h_lo", [P, KT, T], F32R)
        w_raw = [sb(f"w_raw{j}", [P, KT * P]) for j in range(SLOTS)]
        w_hi = [sb(f"w_hi{j}", [P, KT * P], F32R) for j in range(SLOTS)]
        w_lo = [sb(f"w_lo{j}", [P, KT * P], F32R) for j in range(SLOTS)]
        g_base = nc.sbuf_base
        g_hi = sb("g_hi", [P, RING_G, T], F32R)
        g_lo = sb("g_lo", [P, RING_G, T], F32R)
        sil_cond = sb("sil_cond", [P, KT * 2])
        mod = sb("mod", [P, 2, CHUNKS_MOD * 2])
        mod_b = sb("mod_b", [P, DEPTH, CHUNKS_MOD * 2])
        norms = sb("norms", [P, 2 * DEPTH + 1, KT * 2])
        mod_a = sb("mod_a", [P, KT * 2])
        norms_h = sb("norms_h", [P, 2])
        small = sb("small", [P, 96])
        ones_d = sb("ones_d", [P, P])
        ones_h = sb("ones_h", [P, P])
        ident = sb("ident", [P, P])
        unit = T * 4
        arena_base = nc.sbuf_base
        arena_size = 45 * 1024
        sb("arena", [P, arena_size // 4])
        U = T

        class Region:

            def __init__(self, name, spare=True):
                self.name, self.at, self.n = name, arena_base, 0
                self.spare = [g_base + 8 * unit, g_base + 9 * unit, g_base + 18 * unit, g_base + 19 * unit] if spare else []

            def __call__(self, what, elems, dt=F32):
                if self.spare and elems == U:
                    return nc.alloc_sbuf_tensor_at(f"{self.name}_{what}", [P, elems], dt, offset=self.spare.pop())
                a = nc.alloc_sbuf_tensor_at(f"{self.name}_{what}", [P, elems], dt, offset=self.at)
                self.at += elems * 4
                assert self.at <= arena_base + arena_size, (self.name, what, self.at - arena_base - arena_size)
                return a

        ffn = Region("ffn", spare=False)
        rstd = ffn("rstd", U)
        sq = [ffn("sq0", U), ffn("sq1", U)]
        hf = [ffn("hf0", U), ffn("hf1", U)]
        kept = ffn.at
        conv = ffn("conv", 2 * NPAIR * 10)
        acc_a, acc_v, sil = ffn("acc_a", U), ffn("acc_v", U), ffn("sil", U)
        mod_w = [ffn(f"mod_w{j}", KT * 256) for j in range(2)]

        pool = Region("pool")
        pool.at = kept
        box_h = [pool(f"box_h{j}", ROWS * 80) for j in range(2)]
        box_v = [pool(f"box_v{j}", 24 * GRID_W) for j in range(2)]
        inv = pool("inv", 4 * T)
        pool_w = pool("pool_w", 4 * 2 * 256)
        box_m = pool("box_m", U)
        sg = pool("sg", KT * 2)
        pool_h = nc.alloc_sbuf_tensor_at("pool_h", [P, KT, T], F32, offset=h_base)
        pool_d = nc.alloc_sbuf_tensor_at("pool_d", [P, KT, T], F32, offset=h_base + KT * unit)

        hg = Region("hgrn")
        hg.at = kept
        q, f_f, f_b, v_t, v_tok, gate = [hg(n, U) for n in ("q", "f_f", "f_b", "v_t", "v_tok", "gate")]
        qf, qb, kf, kb, tot_f, tot_b, scores = [hg(n, U) for n in ("qf", "qb", "kf", "kb", "tot_f", "tot_b", "scores")]
        masks = hg("masks", 8 * P)
        states = hg("states", 8 * P)
        st_out = hg("st_out", 2 * P)
        lb_in = hg("lb_in", 2 * DEPTH * KT)
        lb = hg("lb", 4 * KT)

        df = Region("diff")
        df.at = kept
        dq, dk, dv_t, dv_tok = [df(n, U) for n in ("q", "k", "v_t", "v_tok")]
        cos, sin = df("cos", N_SAMPLE), df("sin", N_SAMPLE)
        turn = df("turn", P)
        kc, vc = df("kc", PAST), df("vc", PAST)
        qr, kr = df("qr", U), df("kr", U)
        NK = N_SAMPLE + PAST
        prob = [df("prob0", NK), df("prob1", NK)]
        prob_t = df("prob_t", NK)
        lam_in = df("lam_in", 4 * 64)

        acc = [ctx.enter_context(nc.psum_tensor(f"acc{j}", [P, 1024], F32)) for j in range(SLOTS)]

        loaded = sem("loaded")
        raw_landed = [sem(f"raw_landed{j}") for j in range(SLOTS)]
        hi_done, lo_done, job_done, job_used = sem("hi_done"), sem("lo_done"), sem("job_done"), sem("job_used")
        dve_step, act_step = sem("dve_step"), sem("act_step")
        sq_done, sq_used, ms_done = sem("sq_done"), sem("sq_used"), sem("ms_done")
        sqrt_done, rstd_done = sem("sqrt_done"), sem("rstd_done")
        scaled, h_full, h_rounded, h_ready = sem("scaled"), sem("h_full"), sem("h_rounded"), sem("h_ready")
        x_ready = sem("x_ready")
        silu_cond_done = sem("silu_cond_done")
        mod_landed = [sem("mod_landed0"), sem("mod_landed1")]
        mod_done, mod_ready, mod_a_ready = sem("mod_done"), sem("mod_ready"), sem("mod_a_ready")
        conv_landed = sem("conv_landed")
        center_done, silu_done, gated, g_rounded, g_ready = [
            sem(n) for n in ("center_done", "silu_done", "gated", "g_rounded", "g_ready")]
        mixer_landed = sem("mixer_landed")
        sig_done, v_turned, v_ready, level_ready, level_done, masked = [
            sem(n) for n in ("sig_done", "v_turned", "v_ready", "level_ready", "level_done", "masked")]
        kt_turned, kt_ready, ds_done, states_ready, o_done, st_ready, st_stored, s0_landed = [
            sem(n) for n in ("kt_turned", "kt_ready", "ds_done", "states_ready", "o_done", "st_ready", "st_stored", "s0_landed")]
        osq_done, oms_done, osqrt_done, o_full, o_rounded, o_ready = [
            sem(n) for n in ("osq_done", "oms_done", "osqrt_done", "o_full", "o_rounded", "o_ready")]
        pool_ready, pool_done = sem("pool_ready"), sem("pool_done")
        rot_done, qk_ready, cache_landed, sc_done, mx_ready, exp_done, w_ready, wt_done, wt_ready, kv_stored, lam_sem = [
            sem(n) for n in ("rot_done", "qk_ready", "cache_landed", "sc_done", "mx_ready", "exp_done", "w_ready",
                             "wt_done", "wt_ready", "kv_stored", "lam_sem")]
        lb_sem = sem("lb_sem")
        y_ready, y_stored = sem("y_ready"), sem("y_stored")

        first = {}
        for n, (what, layer, index, nk) in enumerate(JOBS):
            first.setdefault((what, layer), n)
        POOL_LAYERS = [layer for layer in range(DEPTH) if KINDS[layer] == 0]
        pools = {layer: i for i, layer in enumerate(POOL_LAYERS)}
        mixer_loads, at = {}, 0
        for layer in range(DEPTH):
            at += 16 * (3, 2, 4)[KINDS[layer]]
            mixer_loads[layer] = at
        plain_norms = {2 * layer for layer in POOL_LAYERS}
        split_norms = [sum(1 for m in range(k) if m not in plain_norms) for k in range(2 * DEPTH + 2)]
        N_CONST = 8

        def x_updates(k):
            if k % 2 and KINDS[k // 2] == 0:
                return x_ready, KT * pools[k // 2]
            if k % 2:
                return job_used, first[("hgrn_out" if KINDS[k // 2] == 1 else "diff_out", k // 2)]
            layer = k // 2
            return job_used, (first[("up", layer - 1)] + 2 * NPAIR + 2 * KT)

        wall, out_y = dram["wall"], dram["y"]

        def layer_parts():
            return [(layer, KINDS[layer]) for layer in range(DEPTH)]

        def up_iters():
            piece = 0
            for what, p0, n in SEGMENTS:
                yield what, p0, n, piece
                if what == "up":
                    piece += n // 2

        def loop(eng, iters, body):
            if iters == 1:
                body(0)
            else:
                with eng.Fori(0, iters) as i:
                    body(i)

        block = ctx.enter_context(nc.Block())

        @block.sync
        def _(sp):
            for dst, src in ((x[:], dram["x"]), (sil_cond[:], dram["cond"]), (mod_b[:], dram["ada_b"]),
                             (norms[:], dram["norms"]), (ones_d[:], dram["ones_d"]), (ones_h[:], dram["ones_h"]),
                             (ident[:], dram["ident"]), (norms_h[:], dram["norms_h"])):
                sp.dma_start(dst, src).then_inc(loaded, 16)

            for j in range(SLOTS):
                sp.dma_start(w_raw[j][:], wall[j]).then_inc(raw_landed[j], 16)
            with sp.Fori(0, NJOBS // SLOTS - 1) as i:
                for j in range(SLOTS):
                    sp.wait_ge(lo_done, i * SLOTS + (j + 1))
                    sp.dma_start(w_raw[j][:], wall[i * SLOTS + (SLOTS + j)]).then_inc(raw_landed[j], 16)
            for kt in range(KT):
                sp.wait_ge(y_ready, kt + 1)
                sp.dma_start(out_y[:, kt], pool_h[:, kt, :]).then_inc(y_stored, 16)
            sp.wait_ge(y_stored, 16 * KT)

        @block.gpsimd
        def _(pl):
            with pl.Fori(0, NJOBS // SLOTS) as i:
                for j in range(SLOTS):
                    pl.wait_ge(hi_done, i * SLOTS + (j + 1))
                    nc.gpsimd.tensor_tensor(w_lo[j][:], w_raw[j][:], w_hi[j][:].bitcast(F32),
                                            ALU.subtract).then_inc(lo_done, 1)

        @block.tensor
        def _(pe):
            def product(out, terms, skip=False):
                for k, (a, b) in enumerate(terms):
                    mm = nc.tensor.matmul(out, a, b, start=(k == 0), stop=(k == len(terms) - 1), skip_group_check=skip)
                return mm

            def job(n, j, nk, hi, lo, sides=None):
                pe.wait_ge(lo_done, n + 1)
                if not (isinstance(n, int) and n < SLOTS):
                    pe.wait_ge(job_used, n - (SLOTS - 1))
                if sides is not None:
                    sides()
                for c0, c1, _ in RANGES:
                    terms = []
                    for k in range(nk):
                        wk = slice(k * P, (k + 1) * P)
                        terms += [(w_hi[j][:, wk], hi(k)[:, c0:c1]), (w_hi[j][:, wk], lo(k)[:, c0:c1]),
                                  (w_lo[j][:, wk], hi(k)[:, c0:c1])]
                    mm = product(acc[j][:, c0:c1], terms)
                mm.then_inc(job_done, 1)

            def mod_piece(k, piece_free):
                piece_free()
                for half in range(2):
                    pe.wait_ge(mod_landed[half], k * 16 + 16)
                    for c in range(2):
                        at = 640 + 4 * half + 2 * c
                        mm = product(acc[3][:, at:at + 2],
                                     [(mod_w[half][:, kt * 256 + c * P:kt * 256 + (c + 1) * P],
                                       sil_cond[:, 2 * kt:2 * kt + 2]) for kt in range(KT)])
                mm.then_inc(mod_done, 1)

            def norm(k, n_used):
                if n_used:
                    pe.wait_ge(job_used, n_used)
                for kt in range(KT):
                    pe.wait_ge(sq_done, KT * k + kt + 1)
                    for c0, c1, _ in RANGES:
                        mm = nc.tensor.matmul(acc[0][:, c0:c1], ones_d[:], sq[kt % 2][:, c0:c1],
                                              start=(kt == 0), stop=(kt == KT - 1))
                    mm.then_inc(sq_used, 1)

            def head_norm(h0):
                pe.wait_ge(osq_done, h0 + 1)
                for c0, c1, _ in RANGES:
                    mm = nc.tensor.matmul(acc[0][:, c0:c1], ones_h[:], sq[0][:, c0:c1], start=True, stop=True)
                mm.then_inc(oms_done, 1)

            def tokens(dst, src, tiles):
                for c in range(tiles):
                    mm = nc.tensor.transpose(dst[:, c * P:(c + 1) * P], src[:, c * P:(c + 1) * P], ident[:])
                return mm

            pe.wait_ge(loaded, 16 * N_CONST)
            pe.wait_ge(silu_cond_done, 1)
            for k in range(MOD_PIECES):
                mod_piece(k, lambda: pe.wait_ge(mod_ready, k) if k else None)
            hd = 0
            for layer, kind in layer_parts():
                n_used = first.get(("up", layer), 0) if kind == 0 else first[("hgrn_in" if kind == 1 else "diff_in", layer)]
                norm(2 * layer, n_used)
                if kind == 0:
                    pe.wait_ge(mixer_landed, mixer_loads[layer])
                    for g in range(4):
                        pe.wait_ge(pool_ready, KT * pools[layer] + 2 * g + 2)
                        for o in range(2):
                            u = 2 * g + o
                            j = 1 + u % 3
                            if u >= 3:
                                pe.wait_ge(x_ready, KT * pools[layer] + u - 2)
                            for c0, c1, _ in RANGES:
                                mm = product(acc[j][:, c0:c1],
                                             [(pool_w[:, ((g * 2 + i) * 2 + o) * P:((g * 2 + i) * 2 + o + 1) * P],
                                               pool_d[:, 2 * g + i, c0:c1]) for i in range(2)])
                            mm.then_inc(pool_done, 1)
                elif kind == 1:
                    pe.wait_ge(h_ready, KT * split_norms[2 * layer + 1])
                    pe.wait_ge(mixer_landed, mixer_loads[layer])
                    n0 = first[("hgrn_in", layer)]
                    for h in range(HEADS):
                        for part in range(5):
                            n = n0 + 5 * h + part
                            if part == 0 and h:
                                pe.wait_ge(o_full, hd)
                            job(n, n % SLOTS, KT, lambda k: h_hi[:, k, :], lambda k: h_lo[:, k, :])
                        pe.wait_ge(job_used, n + 1)
                        tokens(acc[0], v_t, 5).then_inc(v_turned, 1)
                        for level in range(LEVELS + 1):
                            s = (level + 1) % SLOTS
                            pe.wait_ge(level_ready, h * (LEVELS + 2) + level + 1)
                            if level == 3:
                                pe.wait_ge(v_ready, h + 1)
                            if level >= 4:
                                pe.wait_ge(masked, h * (LEVELS + 1) + level - 3)
                            for c in range(5):
                                at = slice(c * P, (c + 1) * P)
                                if level == 0:
                                    mm = nc.tensor.matmul(acc[s][:, at], sq[0][:, at], q[:, at], start=True, stop=True)
                                    continue
                                m = 1 << (level - 1)

                                def halves(t, half):
                                    return t[:, at].rearrange("p (b h m) -> p b h m", h=2, m=m)[:, :, half, :]

                                nc.tensor.matmul(halves(acc[s], 1), kf[:, at], halves(qf, 1), start=True, stop=True)
                                mm = nc.tensor.matmul(halves(acc[s], 0), kb[:, at], halves(qb, 0), start=True, stop=True)
                            mm.then_inc(level_done, 1)
                        pe.wait_ge(level_ready, (h + 1) * (LEVELS + 2))
                        pe.wait_ge(masked, (h + 1) * (LEVELS + 1))
                        tokens(acc[0], kf, 5)
                        tokens(acc[1], kb, 5).then_inc(kt_turned, 1)
                        pe.wait_ge(kt_ready, h + 1)
                        for u, (keys, c) in enumerate([(f_f, 0), (f_f, 1), (f_f, 2), (f_f, 4),
                                                       (f_b, 3), (f_b, 2), (f_b, 1), (f_b, 4)]):
                            at = slice(c * P, (c + 1) * P)
                            mm = nc.tensor.matmul(acc[2][:, u * P:(u + 1) * P], keys[:, at], v_tok[:, at],
                                                  start=True, stop=True)
                        mm.then_inc(ds_done, 1)
                        pe.wait_ge(states_ready, h + 1)
                        for c in range(5):
                            at = slice(c * P, (c + 1) * P)
                            terms = [(v_tok[:, at], scores[:, at])]
                            if c < 4:
                                terms += [(states[:, c * P:(c + 1) * P], qf[:, at]),
                                          (states[:, (4 + c) * P:(5 + c) * P], qb[:, at])]
                            mm = product(acc[3][:, at], terms)
                        mm.then_inc(o_done, 1)
                        head_norm(hd)
                        hd += 1
                    pe.wait_ge(o_ready, hd)
                    n0 = first[("hgrn_out", layer)]
                    for o in range(KT):
                        job(n0 + o, (n0 + o) % SLOTS, KT, lambda k: g_hi[:, k, :], lambda k: g_lo[:, k, :])
                else:
                    pe.wait_ge(h_ready, KT * split_norms[2 * layer + 1])
                    pe.wait_ge(mixer_landed, mixer_loads[layer])
                    n0 = first[("diff_in", layer)]
                    qt = 0
                    for h in range(HEADS):
                        for part in range(3):
                            n = n0 + 3 * h + part
                            if part == 0 and h:
                                pe.wait_ge(o_full, hd)
                            job(n, n % SLOTS, KT, lambda k: h_hi[:, k, :], lambda k: h_lo[:, k, :])
                        pe.wait_ge(job_used, n + 1)
                        tokens(acc[0], dv_t, 5).then_inc(v_turned, 1)
                        nc.tensor.matmul(acc[1][:, 0:512], turn[:], dq[:, 0:512], start=True, stop=True)
                        nc.tensor.matmul(acc[1][:, 512:1024], turn[:], dk[:, 0:512], start=True, stop=True).then_inc(rot_done, 1)
                        pe.wait_ge(qk_ready, h + 1)
                        pe.wait_ge(v_ready, HEADS + h + 1)
                        pe.wait_ge(cache_landed, 32 * (h + 1))
                        for tile in range(5):
                            at = slice(tile * P, (tile + 1) * P)
                            for c in range(2):
                                rows = slice(64 * c, 64 * c + 64)
                                if tile < 4:
                                    nc.tensor.matmul(acc[c][:, 0:512], qr[rows, at], kr[rows, 0:512], start=True, stop=True)
                                    mm = nc.tensor.matmul(acc[c][:, 512:768], qr[rows, at], kc[rows, :], start=True, stop=True)
                                else:
                                    mm = nc.tensor.matmul(acc[c][:, 0:P], dq[rows, at], dk[rows, at], start=True, stop=True)
                            mm.then_inc(sc_done, 1)
                            pe.wait_ge(w_ready, qt + 1)
                            if tile == 0 and h:
                                pass
                            nkt = 6 if tile < 4 else 1
                            tokens(acc[2], prob[0], nkt).then_inc(wt_done, 1)
                            pe.wait_ge(wt_ready, qt + 1)
                            terms = []
                            for k in range(nkt):
                                if tile == 4:
                                    vals = dv_tok[:, 512:640]
                                elif k < 4:
                                    vals = dv_tok[:, k * P:(k + 1) * P]
                                else:
                                    vals = vc[:, (k - 4) * P:(k - 3) * P]
                                terms.append((vals, prob_t[:, k * P:(k + 1) * P]))
                            mm = product(acc[3][:, at], terms)
                            qt += 1
                        mm.then_inc(o_done, 1)
                        head_norm(hd)
                        hd += 1
                    pe.wait_ge(o_ready, hd)
                    n0 = first[("diff_out", layer)]
                    for o in range(KT):
                        job(n0 + o, (n0 + o) % SLOTS, KT, lambda k: g_hi[:, k, :], lambda k: g_lo[:, k, :])
                norm(2 * layer + 1, first[("up", layer)])
                pe.wait_ge(h_ready, KT * split_norms[2 * layer + 2])
                n = first[("up", layer)]
                g_at = NPAIR * layer
                for what, p0, count, piece in up_iters():
                    if what == "up":
                        def body(i, n=n, piece=piece):
                            for j in range(SLOTS):
                                def sides():
                                    k = i + ((layer + 1) * MOD_PIECES + piece)
                                    mod_piece(k, lambda: pe.wait_ge(mod_ready, k))
                                job(i * SLOTS + (n + j), j, KT, lambda k: h_hi[:, k, :], lambda k: h_lo[:, k, :],
                                    sides if j == 3 and layer + 1 < DEPTH else None)
                        if n == 0:
                            body(0)
                            with pe.Fori(1, count // 2) as i:
                                body(i)
                        else:
                            loop(pe, count // 2, body)
                        n += 2 * count
                    else:
                        pe.wait_ge(g_ready, g_at + p0 + count)

                        def body(i, n=n, last=(p0 + count == NPAIR and layer + 1 < DEPTH)):
                            for j in range(SLOTS):
                                job(i * SLOTS + (n + j), j, count, lambda k: g_hi[:, (p0 + k) % RING_G, :],
                                    lambda k: g_lo[:, (p0 + k) % RING_G, :])
                        if p0 + count == NPAIR and layer + 1 < DEPTH:
                            for i in range(2):
                                for j in range(SLOTS):
                                    piece = (layer + 2) * MOD_PIECES - 1
                                    job(n + 4 * i + j, j, count, lambda k: g_hi[:, (p0 + k) % RING_G, :],
                                        lambda k: g_lo[:, (p0 + k) % RING_G, :],
                                        (lambda: mod_piece(piece, lambda: pe.wait_ge(mod_ready, piece)))
                                        if i == 0 and j == 3 else None)
                        else:
                            loop(pe, 2, body)
                        n += KT
            norm(2 * DEPTH, NJOBS)

        @block.scalar
        def _(act):
            steps = [0]

            def link(ins):
                ins.then_inc(act_step, 1)
                steps[0] += 1
                act.wait_ge(act_step, steps[0])

            def high(n, j):
                act.wait_ge(raw_landed[j], (n - j) * 4 + 16)
                if not (isinstance(n, int) and n < SLOTS):
                    act.wait_ge(job_done, n - (SLOTS - 1))
                nc.scalar.activation(w_hi[j][:], w_raw[j][:], ACT.Copy).then_inc(hi_done, 1)

            def ahead(n, j):
                if isinstance(n, int) and n + 3 >= NJOBS:
                    return
                high(n + 3, (j + 3) % SLOTS)

            def load_mod(k, half, free):
                free()
                act.dma_start(mod_w[half][:], dram["ada_w"][k * 2 + half]).then_inc(mod_landed[half], 16)

            def mixer_constants(layer):
                if layer == 0:
                    act.wait_ge(mod_done, MOD_PIECES)
                what = {0: ((inv, dram["inv"]), (pool_w, dram["pool_w"][pools.get(layer, 0)]),
                            (sg, dram["pool_scale"][pools.get(layer, 0)])),
                        1: ((masks, dram["masks"]), (lb_in, dram["lb"])),
                        2: ((cos, dram["cos"]), (sin, dram["sin"]), (turn, dram["turn"]), (lam_in, dram["lam"]))}[KINDS[layer]]
                for dst, src in what:
                    act.dma_start(dst[:], src).then_inc(mixer_landed, 16)

            def norm(k, plain):
                for kt in range(KT):
                    if k:
                        updated, before = x_updates(k)
                        act.wait_ge(updated, before + kt + 1)
                    if KT * k + kt >= 2:
                        act.wait_ge(sq_used, KT * k + kt - 1)
                    nc.scalar.activation(sq[kt % 2][:], x[:, kt, :], ACT.Square).then_inc(sq_done, 1)
                act.wait_ge(sq_used, KT * (k + 1))
                if k % 2 == 0 and k < 2 * DEPTH:
                    mixer_constants(k // 2)
                nc.scalar.activation(rstd[:], acc[0][:, 0:T], ACT.Sqrt, bias=EPS).then_inc(sqrt_done, 1)
                if k == 2 * DEPTH:
                    return
                layer, c0_b = k // 2, 24 * (k % 2)
                for kt in range(KT):
                    act.wait_ge(scaled, KT * k + kt + 1)
                    dst = pool_h[:, kt, :] if plain else hf[kt % 2][:]
                    if not plain and kt >= 2:
                        act.wait_ge(h_ready, KT * split_norms[k] + kt - 1)
                    for c0, c1, row in RANGES:
                        b = 2 * (c0_b + kt) + row
                        ins = nc.scalar.activation(dst[:, c0:c1], sq[kt % 2][:, c0:c1], ACT.Identity,
                                                   bias=mod[:, layer % 2, b:b + 1])
                    ins.then_inc(h_full, 1)
                    if not plain:
                        act.wait_ge(h_full, KT * k + kt + 1)
                        nc.scalar.activation(h_hi[:, kt, :], dst, ACT.Copy).then_inc(h_rounded, 1)

            def head_norm(h0, h):
                act.wait_ge(o_done, h0 + 1)
                nc.scalar.activation(sq[0][:], acc[3][:, 0:T], ACT.Square).then_inc(osq_done, 1)
                act.wait_ge(oms_done, h0 + 1)
                nc.scalar.activation(rstd[:], acc[0][:, 0:T], ACT.Sqrt, bias=EPS).then_inc(osqrt_done, 1)
                act.wait_ge(o_full, h0 + 1)
                nc.scalar.activation(g_hi[:, h, :], sq[1][:], ACT.Copy).then_inc(o_rounded, 1)

            act.wait_ge(loaded, 16 * N_CONST)
            nc.scalar.activation(sq[0][:, 0:2 * KT], sil_cond[:], ACT.Sigmoid).then_inc(act_step, 1)
            steps[0] = 1
            for k in range(MOD_PIECES):
                for half in range(2):
                    load_mod(k, half, lambda: act.wait_ge(mod_done, k) if k else None)
            for n in range(3):
                high(n, n)
            hd = 0
            for layer, kind in layer_parts():
                norm(2 * layer, kind == 0)
                if kind == 1:
                    n0 = first[("hgrn_in", layer)]
                    act.wait_ge(lb_sem, 1)
                    nc.scalar.activation(lb_in[:], lb_in[:], ACT.Exp).then_inc(lb_sem, 1)
                    for h in range(HEADS):
                        if h:
                            act.wait_ge(o_done, hd)
                        act.dma_start(states[:, 0:P], dram["s0"][0, h]).then_inc(s0_landed, 16)
                        act.dma_start(states[:, 7 * P:8 * P], dram["s0"][1, h]).then_inc(s0_landed, 16)
                        for part in range(5):
                            n = n0 + 5 * h + part
                            ahead(n, n % SLOTS)
                            if part in (1, 2, 4):
                                act.wait_ge(job_done, n + 1)
                                dst = {1: sq[0], 2: sq[1], 4: gate}[part]
                                if part == 1 and h:
                                    act.wait_ge(o_ready, hd)
                                if part == 4 and h:
                                    act.wait_ge(o_full, hd)
                                nc.scalar.activation(dst[:], acc[n % SLOTS][:, 0:T], ACT.Sigmoid).then_inc(sig_done, 1)
                        act.wait_ge(st_ready, h + 1)
                        act.dma_start(dram["new_state"][h], st_out[:]).then_inc(st_stored, 16)
                        head_norm(hd, h)
                        hd += 1
                    n0 = first[("hgrn_out", layer)]
                    for o in range(KT):
                        ahead(n0 + o, (n0 + o) % SLOTS)
                elif kind == 2:
                    act.wait_ge(lam_sem, 1)
                    nc.scalar.activation(small[:, 2:4], small[:, 0:2], ACT.Exp).then_inc(lam_sem, 1)
                    n0 = first[("diff_in", layer)]
                    qt = 0
                    for h in range(HEADS):
                        if h:
                            act.wait_ge(o_done, hd)
                        act.dma_start(kc[:], dram["cache_k"][h]).then_inc(cache_landed, 16)
                        act.dma_start(vc[:], dram["cache_v"][h]).then_inc(cache_landed, 16)
                        for part in range(3):
                            n = n0 + 3 * h + part
                            ahead(n, n % SLOTS)
                        act.wait_ge(job_used, n + 1)
                        act.dma_start(dram["new_k"][h], dk[:, N_SAMPLE:T]).then_inc(kv_stored, 16)
                        act.dma_start(dram["new_v"][h], dv_t[:, N_SAMPLE:T]).then_inc(kv_stored, 16)
                        for tile in range(5):
                            nk = NK if tile < 4 else P
                            act.wait_ge(mx_ready, qt + 1)
                            for c in range(2):
                                ins = nc.scalar.activation(prob[c][:, 0:nk], acc[c][:, 0:nk], ACT.Exp,
                                                           bias=small[:, 10 + c:11 + c], scale=SCALE,
                                                           accum_out=small[:, 12 + c:13 + c])
                                ins.then_inc(exp_done, 1)
                            act.wait_ge(wt_done, qt + 1)
                            nc.scalar.activation(prob_t[:, 0:nk], acc[2][:, 0:nk], ACT.Copy).then_inc(wt_ready, 1)
                            qt += 1
                        head_norm(hd, h)
                        hd += 1
                    n0 = first[("diff_out", layer)]
                    for o in range(KT):
                        ahead(n0 + o, (n0 + o) % SLOTS)
                norm(2 * layer + 1, False)
                act.dma_start(conv[:], dram["conv"][layer]).then_inc(conv_landed, 16)
                if layer + 1 < DEPTH:
                    for half in range(2):
                        load_mod((layer + 1) * MOD_PIECES, half, lambda: None)
                act.wait_ge(conv_landed, 16 * (layer + 1))
                n = first[("up", layer)]
                g_at = NPAIR * layer
                for what, p0, count, piece in up_iters():
                    if what == "up":
                        def body(i, n=n, p0=p0, piece=piece):
                            for pair in range(2):
                                p = i * 2 + (p0 + pair)
                                done = i * 2 + (g_at + p0 + pair)
                                for side in range(2):
                                    j = 2 * pair + side
                                    ahead(i * SLOTS + (n + j), j)
                                    act.wait_ge(job_done, i * SLOTS + (n + j + 1))
                                    if not (isinstance(i, int) and layer == 0 and p0 + pair + 2 * i == 0):
                                        act.wait_ge(gated, done)
                                    dst = acc_a if side == 0 else acc_v
                                    c10 = p * 20 + side * 10
                                    nc.scalar.activation(dst[:], acc[j][:, 0:T], ACT.Identity,
                                                         bias=conv[:, bass.ds(c10 + 9, 1)],
                                                         scale=conv[:, bass.ds(c10 + 4, 1)]).then_inc(center_done, 1)
                                act.wait_ge(job_used, i * SLOTS + (n + 2 * pair + 1))
                                if not (isinstance(i, int) and layer == 0 and p0 + pair + 2 * i == 0):
                                    act.wait_ge(g_ready, done)
                                nc.scalar.activation(sil[:], acc_a[:], ACT.Silu).then_inc(silu_done, 1)
                                act.wait_ge(gated, done + 1)
                                slot = (p0 + pair) % RING_G
                                dst = g_hi[:, i * 2 + slot, :]
                                nc.scalar.activation(dst, sil[:], ACT.Copy).then_inc(g_rounded, 1)
                            if layer + 1 < DEPTH:
                                k = i + ((layer + 1) * MOD_PIECES + piece)
                                for half in range(2):
                                    load_mod(k + 1, half, lambda: act.wait_ge(mod_done, k + 1))
                        if layer == 0 and p0 == 0:
                            body(0)
                            with act.Fori(1, count // 2) as i:
                                body(i)
                        else:
                            loop(act, count // 2, body)
                        n += 2 * count
                    else:
                        if n + KT + 3 > NJOBS:
                            for u in range(KT):
                                ahead(n + u, u % SLOTS)
                        else:
                            def body(i, n=n):
                                for j in range(SLOTS):
                                    ahead(i * SLOTS + (n + j), j)
                            loop(act, 2, body)
                        n += KT
            norm(2 * DEPTH, True)
            act.wait_ge(st_stored, 16 * HEADS)
            act.wait_ge(kv_stored, 32 * HEADS)

        @block.vector
        def _(dve):
            V = nc.vector
            steps = [0]

            def link(ins):
                ins.then_inc(dve_step, 1)
                steps[0] = steps[0] + 1
                dve.wait_ge(dve_step, steps[0])

            def linked_loop(iters, per, body, start=0):
                base = steps[0]
                if iters - start == 1:
                    body(start)
                    assert steps[0] == base + per
                    return
                with dve.Fori(start, iters) as i:
                    steps[0] = i * per + (base - start * per)
                    body(i)
                steps[0] = base + per * (iters - start)

            def mod_piece(k, layer):
                dve.wait_ge(mod_done, k + 1)
                c = (k - layer * MOD_PIECES) * 8
                V.tensor_tensor(mod[:, layer % 2, bass.ds(c, 8)], acc[3][:, 640:648], mod_b[:, layer, bass.ds(c, 8)],
                                ALU.add).then_inc(mod_ready, 1)

            def norm(k, plain):
                layer = k // 2
                if k < 2 * DEPTH:
                    dve.wait_ge(mod_ready, (layer + 1) * MOD_PIECES)
                    s0 = 2 * (24 * (k % 2) + 8)
                    V.scalar_tensor_tensor(out=mod_a[:], in0=mod[:, layer % 2, s0:s0 + 2 * KT], scalar=1.0,
                                           in1=norms[:, k, :], op0=ALU.add, op1=ALU.mult).then_inc(mod_a_ready, 1)
                    dve.wait_ge(mod_a_ready, k + 1)
                dve.wait_ge(sqrt_done, k + 1)
                V.reciprocal(rstd[:], rstd[:]).then_inc(rstd_done, 1)
                dve.wait_ge(rstd_done, k + 1)
                for kt in range(KT):
                    if k == 2 * DEPTH:
                        V.scalar_tensor_tensor(out=pool_h[:, kt, :], in0=x[:, kt, :], scalar=norms[:, k, 2 * kt:2 * kt + 1],
                                               in1=rstd[:], op0=ALU.mult, op1=ALU.mult).then_inc(y_ready, 1)
                        continue
                    if kt >= 2:
                        dve.wait_ge(h_full, KT * k + kt - 1)
                    for c0, c1, row in RANGES:
                        ins = V.scalar_tensor_tensor(out=sq[kt % 2][:, c0:c1], in0=x[:, kt, c0:c1],
                                                     scalar=mod_a[:, 2 * kt + row:2 * kt + row + 1],
                                                     in1=rstd[:, c0:c1], op0=ALU.mult, op1=ALU.mult)
                    ins.then_inc(scaled, 1)
                    if not plain and kt >= 1:
                        low_h(k, kt - 1)
                if k < 2 * DEPTH and not plain:
                    low_h(k, KT - 1)

            def low_h(k, kt):
                dve.wait_ge(h_rounded, KT * split_norms[k] + kt + 1)
                V.tensor_tensor(h_lo[:, kt, :], hf[kt % 2][:], h_hi[:, kt, :].bitcast(F32), ALU.subtract).then_inc(h_ready, 1)

            def add_x(o, src, scalars, at):
                for c0, c1, row in RANGES:
                    ins = V.scalar_tensor_tensor(out=x[:, o, c0:c1], in0=src[:, c0:c1],
                                                 scalar=scalars[:, bass.ds(at + row, 1)],
                                                 in1=x[:, o, c0:c1], op0=ALU.mult, op1=ALU.add)
                return ins

            def project(n, layer):
                for o in range(KT):
                    dve.wait_ge(job_done, n + o + 1)
                    add_x(o, acc[(n + o) % SLOTS], mod[:, layer % 2, :], 2 * (16 + o)).then_inc(job_used, 1)

            def head_norm(h0, h, gain, gated_by):
                dve.wait_ge(osqrt_done, h0 + 1)
                link(V.reciprocal(rstd[:], rstd[:]))
                link(V.tensor_tensor(sq[1][:], acc[3][:, 0:T], rstd[:], ALU.mult))
                if gated_by is not None:
                    V.scalar_tensor_tensor(out=sq[1][:], in0=sq[1][:], scalar=gain, in1=gated_by[:],
                                           op0=ALU.mult, op1=ALU.mult).then_inc(o_full, 1)
                else:
                    V.tensor_scalar(sq[1][:], sq[1][:], gain, None, ALU.mult).then_inc(o_full, 1)
                dve.wait_ge(o_rounded, h0 + 1)
                V.tensor_tensor(g_lo[:, h, :], sq[1][:], g_hi[:, h, :].bitcast(F32), ALU.subtract).then_inc(o_ready, 1)

            def lower_bounds(layer):
                v = lb_in[:].rearrange("p (d l k) -> p d l k", d=2, l=DEPTH)
                by_layer = [v[:, :, l, :] for l in range(DEPTH)]
                top = lb[:, 0:2 * KT].rearrange("p (d k) -> p d k", d=2)
                rest = lb[:, 2 * KT:4 * KT].rearrange("p (d k) -> p d k", d=2)
                link(V.tensor_tensor(top, by_layer[0], by_layer[1], ALU.max))
                for l in range(2, DEPTH):
                    link(V.tensor_tensor(top, top, by_layer[l], ALU.max))
                for l in range(DEPTH):
                    ins = V.tensor_tensor(by_layer[l], by_layer[l], top, ALU.subtract)
                ins.then_inc(lb_sem, 1)
                dve.wait_ge(lb_sem, 2)
                link(V.tensor_tensor(rest, by_layer[0], by_layer[1], ALU.add))
                for l in range(2, DEPTH):
                    link(V.tensor_tensor(rest, rest, by_layer[l], ALU.add))
                link(V.reciprocal(rest, rest))
                for l in range(2, layer + 1):
                    link(V.tensor_tensor(by_layer[1], by_layer[1], by_layer[l], ALU.add))
                link(V.tensor_tensor(top, by_layer[1], rest, ALU.mult))
                link(V.tensor_scalar(lb[:, 2 * KT:4 * KT], lb[:, 0:2 * KT], -1.0, 1.0, ALU.mult, ALU.add))

            link(V.memset(small[:], 0.0))
            dve.wait_ge(loaded, 16 * N_CONST)
            dve.wait_ge(act_step, 1)
            V.tensor_tensor(sil_cond[:], sil_cond[:], sq[0][:, 0:2 * KT], ALU.mult).then_inc(silu_cond_done, 1)
            for k in range(MOD_PIECES):
                mod_piece(k, 0)
            hd = 0
            for layer, kind in layer_parts():
                norm(2 * layer, kind == 0)
                if kind == 0:
                    dve.wait_ge(mixer_landed, mixer_loads[layer])
                    link(V.tensor_tensor(sg[:], sg[:], mod[:, layer % 2, 32:48], ALU.mult))
                    for b in box_v:
                        link(V.memset(b[:], 0.0))
                    for kt in range(KT):
                        g = kt // 2
                        w = POOL_WINDOWS[g]
                        dve.wait_ge(h_full, KT * 2 * layer + kt + 1)
                        H = [b[:].rearrange("p (r c) -> p r c", c=80) for b in box_h]
                        B = [b[:].rearrange("p (r c) -> p r c", c=GRID_W) for b in box_v]
                        hs = pool_h[:, kt, 0:N_SAMPLE].rearrange("p (r c) -> p r c", c=GRID_W)
                        link(V.memset(box_h[0][:], 0.0))
                        link(V.tensor_copy(H[0][:, :, 8:72], hs))
                        src, s = 0, 1
                        lo_c, hi_c = 8 - w // 2, 72 - w // 2
                        while s < w:
                            end = hi_c + w - 2 * s
                            if 2 * s == w:
                                out_ap = B[0][:, 8:16, :]
                            else:
                                out_ap = H[1 - src][:, :, lo_c:end]
                            link(V.tensor_tensor(out_ap, H[src][:, :, lo_c:end], H[src][:, :, lo_c + s:end + s], ALU.add))
                            src, s = 1 - src, 2 * s
                        m = box_m[:, 0:N_SAMPLE].rearrange("p (r c) -> p r c", c=GRID_W)
                        if w // 2 >= ROWS:
                            link(V.tensor_reduce(box_h[1][:, 0:GRID_W],
                                                 B[0][:, 8:16, :].rearrange("p r c -> p c r"), AX.X, ALU.add))
                            link(V.tensor_tensor(m, box_h[1][:, 0:GRID_W].rearrange("p (r c) -> p r c", r=1).broadcast_to([P, ROWS, GRID_W]),
                                                 inv[:, g * T:g * T + N_SAMPLE].rearrange("p (r c) -> p r c", c=GRID_W), ALU.mult))
                        else:
                            src, s = 0, 1
                            lo_r, hi_r = 8 - w // 2, 16 - w // 2
                            while s < w:
                                end = hi_r + w - 2 * s
                                link(V.tensor_tensor(B[1 - src][:, lo_r:end, :], B[src][:, lo_r:end, :],
                                                     B[src][:, lo_r + s:end + s, :], ALU.add))
                                src, s = 1 - src, 2 * s
                            link(V.tensor_tensor(m, B[src][:, lo_r:hi_r, :],
                                                 inv[:, g * T:g * T + N_SAMPLE].rearrange("p (r c) -> p r c", c=GRID_W), ALU.mult))
                            if w > 2:
                                link(V.memset(B[0][:, 0:8, :], 0.0))
                                link(V.memset(B[0][:, 16:24, :], 0.0))
                        link(V.memset(box_h[1][:, 0:144], 0.0))
                        link(V.tensor_copy(box_h[1][:, 8:136], pool_h[:, kt, N_SAMPLE:T]))
                        offs, src, s = (0, 160), 0, 1
                        lo_c, hi_c = 8 - w // 2, 136 - w // 2
                        while s < w:
                            end = hi_c + w - 2 * s
                            a, b = offs[src], offs[1 - src]
                            link(V.tensor_tensor(box_h[1][:, b + lo_c:b + end], box_h[1][:, a + lo_c:a + end],
                                                 box_h[1][:, a + lo_c + s:a + end + s], ALU.add))
                            src, s = 1 - src, 2 * s
                        a = offs[src]
                        link(V.tensor_tensor(box_m[:, N_SAMPLE:T], box_h[1][:, a + lo_c:a + hi_c],
                                             inv[:, g * T + N_SAMPLE:(g + 1) * T], ALU.mult))
                        V.tensor_tensor(pool_d[:, kt, :], box_m[:], pool_h[:, kt, :], ALU.subtract).then_inc(pool_ready, 1)
                    for u in range(KT):
                        dve.wait_ge(pool_done, KT * pools[layer] + u + 1)
                        add_x(u, acc[1 + u % 3], sg, 2 * u).then_inc(x_ready, 1)
                elif kind == 1:
                    n0 = first[("hgrn_in", layer)]
                    dve.wait_ge(mixer_landed, mixer_loads[layer])
                    lower_bounds(layer)
                    for h in range(HEADS):
                        n = n0 + 5 * h
                        dve.wait_ge(job_done, n + 1)
                        V.tensor_copy(q[:], acc[n % SLOTS][:, 0:T]).then_inc(job_used, 1)
                        for part, (f, k_) in enumerate(((f_f, kf), (f_b, kb))):
                            dve.wait_ge(sig_done, 3 * h + part + 1)
                            link(V.tensor_scalar(f[:], sq[part][:], lb[:, 2 * KT + part * KT + h:2 * KT + part * KT + h + 1],
                                                 lb[:, part * KT + h:part * KT + h + 1], ALU.mult, ALU.add))
                            V.tensor_scalar(k_[:], f[:], -1.0, 1.0, ALU.mult, ALU.add).then_inc(job_used, 1)
                        dve.wait_ge(job_done, n + 4)
                        V.tensor_copy(v_t[:], acc[(n + 3) % SLOTS][:, 0:T]).then_inc(job_used, 1)
                        dve.wait_ge(sig_done, 3 * h + 3)
                        V.tensor_tensor(gate[:], acc[(n + 4) % SLOTS][:, 0:T], gate[:], ALU.mult).then_inc(job_used, 1)
                        dve.wait_ge(v_turned, h + 1)
                        V.tensor_copy(v_tok[:], acc[0][:, 0:T]).then_inc(v_ready, 1)
                        dve.wait_ge(job_used, n + 3)
                        V.tensor_tensor(sq[0][:], kf[:], kb[:], ALU.add).then_inc(level_ready, 1)
                        link(V.tensor_tensor(qf[:], q[:], f_f[:], ALU.mult))
                        V.tensor_tensor(qb[:], q[:], f_b[:], ALU.mult).then_inc(level_ready, 1)
                        tf, tb = f_f[:, 0:T], f_b[:, 0:T]
                        t_at = 0
                        for level in range(LEVELS + 1):
                            s = (level + 1) % SLOTS
                            dve.wait_ge(level_done, h * (LEVELS + 1) + level + 1)
                            ps3 = acc[s][:, 0:T].rearrange("p (c t) -> p c t", t=P)
                            sc3 = scores[:].rearrange("p (c t) -> p c t", t=P)
                            mk = masks[:, level * P:(level + 1) * P].rearrange("p (c t) -> p c t", c=1).broadcast_to([P, 5, P])
                            if level == 0:
                                V.tensor_tensor(sc3, ps3, mk, ALU.mult).then_inc(masked, 1)
                                continue
                            m = 1 << (level - 1)
                            nb = T // (2 * m)

                            def halves(t, half):
                                return t[:, 0:T].rearrange("p (b h m) -> p b h m", h=2, m=m)[:, :, half, :]

                            def total(t, half):
                                return t.rearrange("p (b h) -> p b h", h=2)[:, :, half:half + 1]

                            for dst, half, t in ((qf, 1, tf), (kf, 0, tf), (qb, 0, tb), (kb, 1, tb)):
                                V.tensor_tensor(halves(dst, half), halves(dst, half),
                                                total(t, 1 - half).broadcast_to([P, nb, m]), ALU.mult)
                            new = []
                            for t, store in ((tf, tot_f), (tb, tot_b)):
                                out_t = store[:, t_at:t_at + nb]
                                ins = V.tensor_tensor(out_t.rearrange("p (b h) -> p b h", h=1), total(t, 0), total(t, 1), ALU.mult)
                                new.append(out_t)
                            ins.then_inc(level_ready, 1)
                            tf, tb = new
                            t_at += nb
                            dve.wait_ge(masked, h * (LEVELS + 1) + level)
                            V.copy_predicated(sc3, mk.bitcast(U32), ps3).then_inc(masked, 1)
                        dve.wait_ge(kt_turned, h + 1)
                        link(V.tensor_copy(f_f[:], acc[0][:, 0:T]))
                        V.tensor_copy(f_b[:], acc[1][:, 0:T]).then_inc(kt_ready, 1)
                        dve.wait_ge(ds_done, h + 1)
                        dve.wait_ge(s0_landed, 32 * (h + 1))
                        if h:
                            dve.wait_ge(st_stored, 16 * h)
                        V.tensor_copy(st_out[:, 0:P], acc[2][:, 3 * P:4 * P])
                        V.tensor_copy(st_out[:, P:2 * P], acc[2][:, 7 * P:8 * P]).then_inc(st_ready, 1)
                        for u in range(3):
                            for base, c, to, t, at in ((0, u, u + 1, tf, u), (4, 3 - u, 2 - u, tb, 4 + u)):
                                ins = V.scalar_tensor_tensor(out=states[:, (base + to) * P:(base + to + 1) * P],
                                                             in0=states[:, (base + c) * P:(base + c + 1) * P],
                                                             scalar=t[:, c:c + 1], in1=acc[2][:, at * P:(at + 1) * P],
                                                             op0=ALU.mult, op1=ALU.add)
                                if u < 2 or base == 0:
                                    link(ins)
                                else:
                                    ins.then_inc(states_ready, 1)
                        head_norm(hd, h, norms_h[:, 0:1], gate)
                        hd += 1
                    project(first[("hgrn_out", layer)], layer)
                else:
                    n0 = first[("diff_in", layer)]
                    dve.wait_ge(mixer_landed, mixer_loads[layer])
                    lam_init = 0.8 - 0.6 * math.exp(-0.3 * layer)
                    for u in range(2):
                        a = 128 * u
                        link(V.tensor_tensor(lam_in[:, a:a + 64], lam_in[:, a:a + 64], lam_in[:, a + 64:a + 128], ALU.mult))
                        link(V.tensor_reduce(small[:, u:u + 1], lam_in[:, a:a + 64], AX.X, ALU.add))
                    V.tensor_scalar(small[:, 7:8], small[:, 0:1], 1.0, None, ALU.mult).then_inc(lam_sem, 1)
                    dve.wait_ge(lam_sem, 2)
                    link(V.tensor_tensor(small[:, 4:5], small[:, 3:4], small[:, 2:3], ALU.subtract))
                    link(V.tensor_scalar(small[:, 5:6], small[:, 4:5], -lam_init, None, ALU.add))
                    link(V.tensor_scalar(small[:, 6:7], norms_h[:, 1:2], 1.0 - lam_init, None, ALU.mult))
                    qt = 0
                    for h in range(HEADS):
                        n = n0 + 3 * h
                        if h:
                            dve.wait_ge(kv_stored, 32 * h)
                        for part, dst in enumerate((dq, dk, dv_t)):
                            dve.wait_ge(job_done, n + part + 1)
                            V.tensor_copy(dst[:], acc[(n + part) % SLOTS][:, 0:T]).then_inc(job_used, 1)
                        dve.wait_ge(v_turned, HEADS + h + 1)
                        V.tensor_copy(dv_tok[:], acc[0][:, 0:T]).then_inc(v_ready, 1)
                        dve.wait_ge(rot_done, h + 1)
                        for part, (src, dst) in enumerate(((dq, qr), (dk, kr))):
                            link(V.tensor_tensor(dst[:, 0:512], src[:, 0:512], cos[:], ALU.mult))
                            link(V.tensor_tensor(sq[1][:, 0:512], acc[1][:, part * 512:(part + 1) * 512], sin[:], ALU.mult))
                            ins = V.tensor_tensor(dst[:, 0:512], dst[:, 0:512], sq[1][:, 0:512], ALU.add)
                            if part == 0:
                                link(ins)
                            else:
                                ins.then_inc(qk_ready, 1)
                        for tile in range(5):
                            nk = NK if tile < 4 else P
                            dve.wait_ge(sc_done, qt + 1)
                            for c in range(2):
                                V.tensor_reduce(small[:, 8 + c:9 + c], acc[c][:, 0:nk], AX.X, ALU.max) if c == 0 else \
                                    link(V.tensor_reduce(small[:, 8 + c:9 + c], acc[c][:, 0:nk], AX.X, ALU.max))
                            V.tensor_scalar(small[:, 10:12], small[:, 8:10], -SCALE, None, ALU.mult).then_inc(mx_ready, 1)
                            dve.wait_ge(exp_done, 2 * qt + 2)
                            link(V.reciprocal(small[:, 14:16], small[:, 12:14]))
                            link(V.tensor_tensor(small[:, 16:17], small[:, 15:16], small[:, 5:6], ALU.mult))
                            link(V.tensor_scalar(prob[0][:, 0:nk], prob[0][:, 0:nk], small[:, 14:15], None, ALU.mult))
                            V.scalar_tensor_tensor(out=prob[0][:, 0:nk], in0=prob[1][:, 0:nk], scalar=small[:, 16:17],
                                                   in1=prob[0][:, 0:nk], op0=ALU.mult, op1=ALU.add).then_inc(w_ready, 1)
                            qt += 1
                        head_norm(hd, h, small[:, 6:7], None)
                        hd += 1
                    project(first[("diff_out", layer)], layer)
                norm(2 * layer + 1, False)
                dve.wait_ge(conv_landed, 16 * (layer + 1))
                n = first[("up", layer)]
                g_at = NPAIR * layer
                for what, p0, count, piece in up_iters():
                    if what == "up":
                        def body(i, n=n, p0=p0, piece=piece):
                            for pair in range(2):
                                p = i * 2 + (p0 + pair)
                                done = i * 2 + (g_at + p0 + pair)
                                j = 2 * pair
                                views = []
                                for side, dst in enumerate((acc_a, acc_v)):
                                    u = acc[j + side]
                                    views.append((u[:, 0:N_SAMPLE].rearrange("p (r c) -> p r c", c=GRID_W),
                                                  dst[:, 0:N_SAMPLE].rearrange("p (r c) -> p r c", c=GRID_W),
                                                  u[:, N_SAMPLE:T], dst[:, N_SAMPLE:T], p * 20 + side * 10))
                                taps = [(dy, dx) for dy in (-1, 0, 1) for dx in (-1, 0, 1) if (dy, dx) != (0, 0)]
                                for step, (dy, dx) in enumerate([("p", -1), ("p", 1)] + taps):
                                    for side in range(2):
                                        us, ds, up, dp, c10 = views[side]
                                        if step == 0:
                                            dve.wait_ge(center_done, i * 4 + (2 * (g_at + p0 + pair) + side + 1))
                                            if pair == 1 and side == 1 and layer + 1 < DEPTH:
                                                mod_piece(i + ((layer + 1) * MOD_PIECES + piece), layer + 1)
                                        if dy == "p":
                                            a, b = max(0, -dx), N_PROMPT - max(0, dx)
                                            src, out, w = up[:, a + dx:b + dx], dp[:, a:b], 4 + dx
                                        else:
                                            r0, r1 = max(0, -dy), ROWS - max(0, dy)
                                            a, b = max(0, -dx), GRID_W - max(0, dx)
                                            src, out, w = us[:, r0 + dy:r1 + dy, a + dx:b + dx], ds[:, r0:r1, a:b], 4 + 3 * dy + dx
                                        ins = V.scalar_tensor_tensor(out=out, in0=src, scalar=conv[:, bass.ds(c10 + w, 1)],
                                                                     in1=out, op0=ALU.mult, op1=ALU.add)
                                        if step == 9:
                                            ins.then_inc(job_used, 1)
                                        else:
                                            ins.then_inc(dve_step, 1)
                                            steps[0] = steps[0] + 1
                                        if step < 9 and not (step == 0 and side == 0):
                                            dve.wait_ge(dve_step, steps[0] - 1)
                                        if step == 8 and side == 1:
                                            dve.wait_ge(dve_step, steps[0])
                                dve.wait_ge(job_used, i * 4 + (n + j + 2))
                                dve.wait_ge(silu_done, done + 1)
                                V.tensor_tensor(sil[:], sil[:], acc_v[:], ALU.mult).then_inc(gated, 1)
                                dve.wait_ge(g_rounded, done + 1)
                                slot = (p0 + pair) % RING_G
                                V.tensor_tensor(g_lo[:, i * 2 + slot, :], sil[:], g_hi[:, i * 2 + slot, :].bitcast(F32),
                                                ALU.subtract).then_inc(g_ready, 1)
                        linked_loop(count // 2, 36, body)
                        n += 2 * count
                    else:
                        def body(i, n=n):
                            for j in range(SLOTS):
                                dve.wait_ge(job_done, i * 4 + (n + j + 1))
                                if j == 3 and p0 + count == NPAIR and layer + 1 < DEPTH and i == 0:
                                    mod_piece((layer + 2) * MOD_PIECES - 1, layer + 1)
                                for c0, c1, row in RANGES:
                                    ins = V.scalar_tensor_tensor(out=x[:, i * 4 + j, c0:c1], in0=acc[j][:, c0:c1],
                                                                 scalar=mod[:, layer % 2, bass.ds(i * 8 + (2 * (40 + j) + row), 1)],
                                                                 in1=x[:, i * 4 + j, c0:c1], op0=ALU.mult, op1=ALU.add)
                                ins.then_inc(job_used, 1)
                        dve.wait_ge(job_used, n)
                        if p0 + count == NPAIR:
                            body(0)
                            body(1)
                        else:
                            with dve.Fori(0, 2) as i:
                                body(i)
                        n += KT
            norm(2 * DEPTH, True)


def kernel(**inputs):
    import numpy as np
    import concourse.bacc as bacc
    from concourse.bass_utils import run_bass_kernel_spmd

    a = {k: np.asarray(v) for k, v in inputs.items()}

    def chan(v):
        return np.moveaxis(v.reshape(*v.shape[:-1], -1, P), -1, 0)

    def tiles(w):
        k, n = w.shape
        return w.reshape(k // P, P, n // P, P).transpose(2, 1, 0, 3).reshape(n // P, P, -1)

    f32 = np.float32
    weights = {}
    for layer, kind in enumerate(KINDS):
        if kind == 1:
            weights["hgrn_in", layer] = tiles(a["hgrn_w_in"][layer // 3])
            weights["hgrn_out", layer] = tiles(a["hgrn_w_out"][layer // 3])
        elif kind == 2:
            weights["diff_in", layer] = tiles(a["diff_w_in"][layer // 3])
            weights["diff_out", layer] = tiles(a["diff_w_out"][layer // 3])
        weights["up", layer] = tiles(a["ffn_w_up"][layer])
        weights["down", layer] = tiles(a["ffn_w_down"][layer])
    wall = np.zeros((NJOBS, P, KT * P), f32)
    for n, (what, layer, index, nk) in enumerate(JOBS):
        if what == "down":
            p0, count, o = index
            wall[n, :, :count * P] = weights[what, layer][o, :, p0 * P:(p0 + count) * P]
        else:
            wall[n] = weights[what, layer][index]
    twice = lambda v: np.repeat(v[..., None], 2, axis=-1)
    data = {
        "x": chan(np.concatenate([a["x_sample"][0], a["x_prompt"][0]])).transpose(0, 2, 1),
        "cond": chan(np.stack([a["c"][0], a["c_ctx"]])).transpose(0, 2, 1).reshape(P, -1),
        "ada_b": twice(chan(a["ada_b"])).reshape(P, DEPTH, -1),
        "norms": twice(chan(np.stack([v for i in range(DEPTH) for v in (a["norm1"][i], a["norm2"][i])]
                                     + [a["final_norm"]]))).reshape(P, 2 * DEPTH + 1, -1),
        "norms_h": np.stack([a["hgrn_norm"][0], a["diff_subln"][0]], axis=1),
        "ones_d": np.full((P, P), 1 / D_MODEL, f32),
        "ones_h": np.full((P, P), 1 / P, f32),
        "ident": np.eye(P, dtype=f32),
        "wall": wall,
        "ada_w": a["ada_w"].reshape(DEPTH, KT, P, CHUNKS_MOD // 2, 256).transpose(0, 3, 2, 1, 4).reshape(-1, P, KT * 256),
        "pool_w": a["pool_w"].reshape(-1, 4, 2, P, 2, P).transpose(0, 3, 1, 2, 4, 5).reshape(-1, P, 4 * 2 * 256),
        "pool_scale": twice(chan(a["pool_scale"])).transpose(1, 0, 2, 3).reshape(-1, P, 2 * KT),
        "lb": chan(a["hgrn_lb"]).reshape(P, -1),
        "s0": a["state_hgrn"][0, 0],
        "cache_k": a["cache_k"][0, 0].transpose(1, 2, 3, 0).reshape(HEADS, P, PAST),
        "cache_v": a["cache_v"][0, 0].reshape(2, P, HEADS, P).transpose(2, 1, 0, 3).reshape(HEADS, P, PAST),
        "lam": np.repeat(a["diff_lambda"].reshape(1, -1), P, axis=0),
    }
    taps = np.concatenate([a["ffn_conv_w"].reshape(DEPTH, 9, -1), a["ffn_conv_b"][:, None]], axis=1)
    data["conv"] = taps.reshape(DEPTH, 10, 2, NPAIR, P).transpose(0, 4, 3, 2, 1).reshape(DEPTH, P, -1)
    def sizes(n, w):
        i = np.arange(n)
        return np.clip(i + w // 2, 0, n) - np.clip(i - w // 2, 0, n)

    inv = np.zeros((4, T), f32)
    for g, w in enumerate(POOL_WINDOWS):
        inv[g, :N_SAMPLE] = 1.0 / np.outer(sizes(ROWS, w), sizes(GRID_W, w)).reshape(-1)
        inv[g, N_SAMPLE:] = 1.0 / sizes(N_PROMPT, w)
    data["inv"] = np.broadcast_to(inv.reshape(1, -1), (P, 4 * T))
    masks = np.zeros((P, LEVELS + 1, P), f32)
    s, t = np.arange(P)[:, None], np.arange(P)[None, :]
    masks[:, 0] = s == t
    for level in range(1, LEVELS + 1):
        m = 1 << (level - 1)
        masks[:, level] = (s // (2 * m) == t // (2 * m)) & (s // m != t // m)
    data["masks"] = masks.reshape(P, -1)
    half, nf = 32, 16
    freq = 10000.0 ** (-np.arange(nf, dtype=f32) / nf)
    tok = np.arange(N_SAMPLE)
    d = np.arange(P) % 64
    pos = np.where((d < half)[:, None], tok[None, :] // GRID_W, tok[None, :] % GRID_W)
    angle = pos.astype(f32) * freq[d % nf][:, None].astype(f32)
    data["cos"], data["sin"] = np.cos(angle).astype(f32), np.sin(angle).astype(f32)
    turn = np.zeros((P, P), f32)
    for p in range(P):
        if p % 32 < nf:
            turn[p + nf, p] = -1
        else:
            turn[p - nf, p] = 1
    data["turn"] = turn
    data = {k: np.ascontiguousarray(v) for k, v in data.items()}
    outs = {"y": (P, KT, T), "new_state": (HEADS, P, 2 * P), "new_k": (HEADS, P, N_PROMPT), "new_v": (HEADS, P, N_PROMPT)}

    nc = bacc.Bacc("TRN2", target_bir_lowering=False, num_devices=1)
    dram = {k: nc.dram_tensor(f"in_{k}", v.shape, F32, kind="ExternalInput").ap() for k, v in data.items()}
    dram |= {k: nc.dram_tensor(f"out_{k}", v, F32, kind="ExternalOutput").ap() for k, v in outs.items()}
    trunk(nc, dram)
    got = run_bass_kernel_spmd(nc, [{f"in_{k}": v for k, v in data.items()}], core_ids=[0]).results[0]
    y = got["out_y"].transpose(2, 1, 0).reshape(T, D_MODEL)
    state = got["out_new_state"].reshape(HEADS, P, 2, P).transpose(2, 0, 1, 3)
    new_k = got["out_new_k"].transpose(2, 0, 1).reshape(N_PROMPT, HEADS, 2, 64)
    new_v = got["out_new_v"].transpose(2, 0, 1)
    return (y[None, N_SAMPLE:], y[None, :N_SAMPLE], state[None, None], new_k[None, None], new_v[None, None])
```

```python
from contextlib import ExitStack
import math

import concourse.bass as bass
from concourse import mybir

F32 = mybir.dt.float32
F32R = mybir.dt.float32r
U32 = mybir.dt.uint32
ACT = mybir.ActivationFunctionType
ALU = mybir.AluOpType
AX = mybir.AxisListType

P = 128
D_MODEL = 1024
KT = D_MODEL // P
N_SAMPLE, N_PROMPT = 512, 128
T = N_SAMPLE + N_PROMPT
GRID_W = 64
ROWS = N_SAMPLE // GRID_W
DEPTH = 4
D_FF = ((8 * D_MODEL // 3) + 127) // 128 * 128
NPAIR = D_FF // P
HEADS = 8
LEVELS = 7
PAST = 256
EPS = 1e-6
KINDS = [i % 3 for i in range(DEPTH)]
CHUNKS_MOD = 48
MOD_PIECES = CHUNKS_MOD // 4
RING_G = 10
SEGMENTS = [("up", 0, 8), ("up", 8, 2), ("down", 0, 8), ("up", 10, 6), ("up", 16, 2), ("down", 8, 8),
            ("up", 18, 2), ("up", 20, 2), ("down", 16, 6)]
RANGES = [(0, N_SAMPLE, 0), (N_SAMPLE, T, 1)]
SLOTS = 4
SCALE = 64 ** -0.5
POOL_WINDOWS = (2, 4, 8, 16)


def job_plan():
    jobs = []
    for layer, kind in enumerate(KINDS):
        if kind == 1:
            for h in range(HEADS):
                jobs += [("hgrn_in", layer, part * HEADS + h, KT) for part in (0, 3, 4, 1, 2)]
            jobs += [("hgrn_out", layer, o, KT) for o in range(KT)]
        elif kind == 2:
            for h in range(HEADS):
                jobs += [("diff_in", layer, part * HEADS + h, KT) for part in (0, 1, 2)]
            jobs += [("diff_out", layer, o, KT) for o in range(KT)]
        for what, p0, n in SEGMENTS:
            if what == "up":
                for p in range(p0, p0 + n):
                    jobs += [("up", layer, p, KT), ("up", layer, NPAIR + p, KT)]
            else:
                jobs += [("down", layer, (p0, n, o), n) for o in range(KT)]
    return jobs


JOBS = job_plan()
NJOBS = len(JOBS)


def trunk(nc, dram):
    ctx = ExitStack()
    with ctx:
        def sb(name, shape, dt=F32):
            return ctx.enter_context(nc.sbuf_tensor(name, shape, dt))

        def sem(name):
            return ctx.enter_context(nc.semaphore(name))

        x = sb("x", [P, KT, T])
        h_base = nc.sbuf_base
        h_hi = sb("h_hi", [P, KT, T], F32R)
        h_lo = sb("h_lo", [P, KT, T], F32R)
        w_raw = [sb(f"w_raw{j}", [P, KT * P]) for j in range(SLOTS)]
        w_hi = [sb(f"w_hi{j}", [P, KT * P], F32R) for j in range(SLOTS)]
        w_lo = [sb(f"w_lo{j}", [P, KT * P], F32R) for j in range(SLOTS)]
        g_base = nc.sbuf_base
        g_hi = sb("g_hi", [P, RING_G, T], F32R)
        g_lo = sb("g_lo", [P, RING_G, T], F32R)
        sil_cond = sb("sil_cond", [P, KT * 2])
        mod = sb("mod", [P, 2, CHUNKS_MOD * 2])
        mod_b = sb("mod_b", [P, DEPTH, CHUNKS_MOD * 2])
        norms = sb("norms", [P, 2 * DEPTH + 1, KT * 2])
        mod_a = sb("mod_a", [P, KT * 2])
        norms_h = sb("norms_h", [P, 2])
        small = sb("small", [P, 96])
        ones_d = sb("ones_d", [P, P])
        ones_h = sb("ones_h", [P, P])
        ident = sb("ident", [P, P])
        unit = T * 4
        arena_base = nc.sbuf_base
        arena_size = 45 * 1024
        sb("arena", [P, arena_size // 4])
        U = T

        class Region:

            def __init__(self, name, spare=True):
                self.name, self.at, self.n = name, arena_base, 0
                self.spare = [g_base + 8 * unit, g_base + 9 * unit, g_base + 18 * unit, g_base + 19 * unit] if spare else []

            def __call__(self, what, elems, dt=F32):
                if self.spare and elems == U:
                    return nc.alloc_sbuf_tensor_at(f"{self.name}_{what}", [P, elems], dt, offset=self.spare.pop())
                a = nc.alloc_sbuf_tensor_at(f"{self.name}_{what}", [P, elems], dt, offset=self.at)
                self.at += elems * 4
                assert self.at <= arena_base + arena_size, (self.name, what, self.at - arena_base - arena_size)
                return a

        ffn = Region("ffn", spare=False)
        rstd = ffn("rstd", U)
        sq = [ffn("sq0", U), ffn("sq1", U)]
        hf = [ffn("hf0", U), ffn("hf1", U)]
        kept = ffn.at
        conv = ffn("conv", 2 * NPAIR * 10)
        acc_a, acc_v, sil = ffn("acc_a", U), ffn("acc_v", U), ffn("sil", U)
        mod_w = [ffn(f"mod_w{j}", KT * 256) for j in range(2)]

        pool = Region("pool")
        pool.at = kept
        box_h = [pool(f"box_h{j}", ROWS * 80) for j in range(2)]
        box_v = [pool(f"box_v{j}", 24 * GRID_W) for j in range(2)]
        inv = pool("inv", 4 * T)
        pool_w = pool("pool_w", 4 * 2 * 256)
        box_m = pool("box_m", U)
        sg = pool("sg", KT * 2)
        pool_h = nc.alloc_sbuf_tensor_at("pool_h", [P, KT, T], F32, offset=h_base)
        pool_d = nc.alloc_sbuf_tensor_at("pool_d", [P, KT, T], F32, offset=h_base + KT * unit)

        hg = Region("hgrn")
        hg.at = kept
        q, f_f, f_b, v_t, v_tok, gate0, gate1 = [hg(n, U) for n in ("q", "f_f", "f_b", "v_t", "v_tok", "gate0", "gate1")]
        gates = [gate0, gate1]
        qf, qb, kf, kb, tot_f, tot_b = [hg(n, U) for n in ("qf", "qb", "kf", "kb", "tot_f", "tot_b")]
        k_sum, scores = hf
        masks = hg("masks", 8 * P)
        states = hg("states", 8 * P)
        st_out = hg("st_out", 2 * P)
        lb_in = hg("lb_in", 2 * DEPTH * KT)
        lb = hg("lb", 4 * KT)

        df = Region("diff")
        df.at = kept
        dq, dk, dv_t, dv_tok = [df(n, U) for n in ("q", "k", "v_t", "v_tok")]
        cos, sin = df("cos", N_SAMPLE), df("sin", N_SAMPLE)
        turn = df("turn", P)
        kc, vc = [[df(f"{n}{j}", PAST) for j in range(2)] for n in ("kc", "vc")]
        qr, kr = df("qr", U), df("kr", U)
        NK = N_SAMPLE + PAST
        prob = [df("prob0", NK), df("prob1", NK)]
        prob_t = df("prob_t", NK)
        o_sb = hf[0]
        lam_in = df("lam_in", 4 * 64)

        acc = [ctx.enter_context(nc.psum_tensor(f"acc{j}", [P, 1024], F32)) for j in range(SLOTS)]

        loaded = sem("loaded")
        raw_landed = [sem(f"raw_landed{j}") for j in range(SLOTS)]
        hi_done, lo_done, job_done, job_used = sem("hi_done"), sem("lo_done"), sem("job_done"), sem("job_used")
        dve_step, act_step = sem("dve_step"), sem("act_step")
        sq_done, sq_used, ms_done = sem("sq_done"), sem("sq_used"), sem("ms_done")
        sqrt_done, rstd_done = sem("sqrt_done"), sem("rstd_done")
        scaled, h_full, h_rounded, h_ready = sem("scaled"), sem("h_full"), sem("h_rounded"), sem("h_ready")
        x_ready = sem("x_ready")
        silu_cond_done = sem("silu_cond_done")
        mod_landed = [sem("mod_landed0"), sem("mod_landed1")]
        mod_done, mod_ready, mod_a_ready = sem("mod_done"), sem("mod_ready"), sem("mod_a_ready")
        conv_landed = sem("conv_landed")
        center_done, silu_done, gated, g_rounded, g_ready = [
            sem(n) for n in ("center_done", "silu_done", "gated", "g_rounded", "g_ready")]
        mixer_landed = sem("mixer_landed")
        sig_done, v_turned, v_ready, level_ready, level_done, masked = [
            sem(n) for n in ("sig_done", "v_turned", "v_ready", "level_ready", "level_done", "masked")]
        kt_turned, kt_ready, ds_done, states_ready, o_done, st_ready, st_stored, s0_landed = [
            sem(n) for n in ("kt_turned", "kt_ready", "ds_done", "states_ready", "o_done", "st_ready", "st_stored", "s0_landed")]
        osq_done, oms_done, osqrt_done, o_full, o_rounded, o_ready = [
            sem(n) for n in ("osq_done", "oms_done", "osqrt_done", "o_full", "o_rounded", "o_ready")]
        pool_ready, pool_done = sem("pool_ready"), sem("pool_done")
        cache_landed = [sem("cache_landed0"), sem("cache_landed1")]
        rot_done, qk_ready, sc_done, mx_ready, exp_done, w_ready, wt_done, wt_ready, kv_stored, lam_sem = [
            sem(n) for n in ("rot_done", "qk_ready", "sc_done", "mx_ready", "exp_done", "w_ready",
                             "wt_done", "wt_ready", "kv_stored", "lam_sem")]
        pv_done, o_copied = sem("pv_done"), sem("o_copied")
        lb_sem = sem("lb_sem")
        y_ready, y_stored = sem("y_ready"), sem("y_stored")

        first = {}
        for n, (what, layer, index, nk) in enumerate(JOBS):
            first.setdefault((what, layer), n)
        POOL_LAYERS = [layer for layer in range(DEPTH) if KINDS[layer] == 0]
        pools = {layer: i for i, layer in enumerate(POOL_LAYERS)}
        mixer_loads, at = {}, 0
        for layer in range(DEPTH):
            at += 16 * (3, 2, 4)[KINDS[layer]]
            mixer_loads[layer] = at
        plain_norms = {2 * layer for layer in POOL_LAYERS}
        split_norms = [sum(1 for m in range(k) if m not in plain_norms) for k in range(2 * DEPTH + 2)]
        N_CONST = 8

        def x_updates(k):
            if k % 2 and KINDS[k // 2] == 0:
                return x_ready, KT * pools[k // 2]
            if k % 2:
                return job_used, first[("hgrn_out" if KINDS[k // 2] == 1 else "diff_out", k // 2)]
            layer = k // 2
            return job_used, (first[("up", layer - 1)] + 2 * NPAIR + 2 * KT)

        wall, out_y = dram["wall"], dram["y"]

        def layer_parts():
            return [(layer, KINDS[layer]) for layer in range(DEPTH)]

        def up_iters():
            piece = 0
            for what, p0, n in SEGMENTS:
                yield what, p0, n, piece
                if what == "up":
                    piece += n // 2

        def loop(eng, iters, body):
            if iters == 1:
                body(0)
            else:
                with eng.Fori(0, iters) as i:
                    body(i)

        block = ctx.enter_context(nc.Block())

        @block.sync
        def _(sp):
            for dst, src in ((x[:], dram["x"]), (sil_cond[:], dram["cond"]), (mod_b[:], dram["ada_b"]),
                             (norms[:], dram["norms"]), (ones_d[:], dram["ones_d"]), (ones_h[:], dram["ones_h"]),
                             (ident[:], dram["ident"]), (norms_h[:], dram["norms_h"])):
                sp.dma_start(dst, src).then_inc(loaded, 16)

            for j in range(SLOTS):
                sp.dma_start(w_raw[j][:], wall[j]).then_inc(raw_landed[j], 16)
            with sp.Fori(0, NJOBS // SLOTS - 1) as i:
                for j in range(SLOTS):
                    sp.wait_ge(lo_done, i * SLOTS + (j + 1))
                    sp.dma_start(w_raw[j][:], wall[i * SLOTS + (SLOTS + j)]).then_inc(raw_landed[j], 16)
            for kt in range(KT):
                sp.wait_ge(y_ready, kt + 1)
                sp.dma_start(out_y[:, kt], pool_h[:, kt, :]).then_inc(y_stored, 16)
            sp.wait_ge(y_stored, 16 * KT)

        @block.gpsimd
        def _(pl):
            with pl.Fori(0, NJOBS // SLOTS) as i:
                for j in range(SLOTS):
                    pl.wait_ge(hi_done, i * SLOTS + (j + 1))
                    nc.gpsimd.tensor_tensor(w_lo[j][:], w_raw[j][:], w_hi[j][:].bitcast(F32),
                                            ALU.subtract).then_inc(lo_done, 1)

        @block.tensor
        def _(pe):
            def product(out, terms, skip=False):
                for k, (a, b) in enumerate(terms):
                    mm = nc.tensor.matmul(out, a, b, start=(k == 0), stop=(k == len(terms) - 1), skip_group_check=skip)
                return mm

            def job(n, j, nk, hi, lo, sides=None):
                pe.wait_ge(lo_done, n + 1)
                if not (isinstance(n, int) and n < SLOTS):
                    pe.wait_ge(job_used, n - (SLOTS - 1))
                if sides is not None:
                    sides()
                for c0, c1, _ in RANGES:
                    terms = []
                    for k in range(nk):
                        wk = slice(k * P, (k + 1) * P)
                        terms += [(w_hi[j][:, wk], hi(k)[:, c0:c1]), (w_hi[j][:, wk], lo(k)[:, c0:c1]),
                                  (w_lo[j][:, wk], hi(k)[:, c0:c1])]
                    mm = product(acc[j][:, c0:c1], terms)
                mm.then_inc(job_done, 1)

            def job_steps(n0, a, b, depth):
                for step in range(a, b):
                    n, k = n0 + step // KT, step % KT
                    j, ps = n % SLOTS, acc[n % depth]
                    if k == 0:
                        pe.wait_ge(lo_done, n + 1)
                        pe.wait_ge(job_used, n + 1 - depth)
                    wk = slice(k * P, (k + 1) * P)
                    for c0, c1, _ in RANGES:
                        for u, (w, h) in enumerate(((w_hi, h_hi), (w_hi, h_lo), (w_lo, h_hi))):
                            mm = nc.tensor.matmul(ps[:, c0:c1], w[j][:, wk], h[:, k, c0:c1], start=(k == 0 and u == 0),
                                                  stop=(k == KT - 1 and u == 2), skip_group_check=True)
                    if k == KT - 1:
                        mm.then_inc(job_done, 1)

            def mod_piece(k, piece_free):
                piece_free()
                for half in range(2):
                    pe.wait_ge(mod_landed[half], k * 16 + 16)
                    for c in range(2):
                        at = 640 + 4 * half + 2 * c
                        mm = product(acc[3][:, at:at + 2],
                                     [(mod_w[half][:, kt * 256 + c * P:kt * 256 + (c + 1) * P],
                                       sil_cond[:, 2 * kt:2 * kt + 2]) for kt in range(KT)])
                mm.then_inc(mod_done, 1)

            def norm(k, n_used):
                if n_used:
                    pe.wait_ge(job_used, n_used)
                for kt in range(KT):
                    pe.wait_ge(sq_done, KT * k + kt + 1)
                    for c0, c1, _ in RANGES:
                        mm = nc.tensor.matmul(acc[0][:, c0:c1], ones_d[:], sq[kt % 2][:, c0:c1],
                                              start=(kt == 0), stop=(kt == KT - 1))
                    mm.then_inc(sq_used, 1)

            def head_norm(h0, ps):
                pe.wait_ge(osq_done, h0 + 1)
                for c0, c1, _ in RANGES:
                    mm = nc.tensor.matmul(ps[:, c0:c1], ones_h[:], sq[0][:, c0:c1], start=True, stop=True)
                mm.then_inc(oms_done, 1)

            def tokens(dst, src, tiles):
                for c in range(tiles):
                    mm = nc.tensor.transpose(dst[:, c * P:(c + 1) * P], src[:, c * P:(c + 1) * P], ident[:])
                return mm

            pe.wait_ge(loaded, 16 * N_CONST)
            pe.wait_ge(silu_cond_done, 1)
            for k in range(MOD_PIECES):
                mod_piece(k, lambda: pe.wait_ge(mod_ready, k) if k else None)
            hd = 0
            for layer, kind in layer_parts():
                n_used = first.get(("up", layer), 0) if kind == 0 else first[("hgrn_in" if kind == 1 else "diff_in", layer)]
                norm(2 * layer, n_used)
                if kind == 0:
                    pe.wait_ge(mixer_landed, mixer_loads[layer])
                    for g in range(4):
                        pe.wait_ge(pool_ready, KT * pools[layer] + 2 * g + 2)
                        for o in range(2):
                            u = 2 * g + o
                            j = 1 + u % 3
                            if u >= 3:
                                pe.wait_ge(x_ready, KT * pools[layer] + u - 2)
                            for c0, c1, _ in RANGES:
                                mm = product(acc[j][:, c0:c1],
                                             [(pool_w[:, ((g * 2 + i) * 2 + o) * P:((g * 2 + i) * 2 + o + 1) * P],
                                               pool_d[:, 2 * g + i, c0:c1]) for i in range(2)])
                            mm.then_inc(pool_done, 1)
                elif kind == 1:
                    pe.wait_ge(h_ready, KT * split_norms[2 * layer + 1])
                    pe.wait_ge(mixer_landed, mixer_loads[layer])
                    n0 = first[("hgrn_in", layer)]
                    job_steps(n0, 0, 5 * KT, 2)
                    for h in range(HEADS):
                        def next_steps(point):
                            if h + 1 < HEADS:
                                job_steps(n0 + 5 * (h + 1), 4 * point, 4 * point + 4, 2)

                        pe.wait_ge(job_used, n0 + 5 * h + 4)
                        if h:
                            pe.wait_ge(o_full, hd)
                        tokens(acc[2], v_t, 5).then_inc(v_turned, 1)
                        for level in range(LEVELS + 1):
                            next_steps(level)
                            s = 2 + (level + 1) % 2
                            pe.wait_ge(level_ready, h * (LEVELS + 2) + level + 1)
                            if level == 1:
                                pe.wait_ge(v_ready, h + 1)
                            if level >= 2:
                                pe.wait_ge(masked, h * (LEVELS + 1) + level - 1)
                            for c in range(5):
                                at = slice(c * P, (c + 1) * P)
                                if level == 0:
                                    mm = nc.tensor.matmul(acc[s][:, at], k_sum[:, at], q[:, at], start=True, stop=True)
                                    continue
                                m = 1 << (level - 1)

                                def halves(t, half):
                                    return t[:, at].rearrange("p (b h m) -> p b h m", h=2, m=m)[:, :, half, :]

                                nc.tensor.matmul(halves(acc[s], 1), kf[:, at], halves(qf, 1), start=True, stop=True)
                                mm = nc.tensor.matmul(halves(acc[s], 0), kb[:, at], halves(qb, 0), start=True, stop=True)
                            mm.then_inc(level_done, 1)
                        next_steps(8)
                        pe.wait_ge(level_ready, (h + 1) * (LEVELS + 2))
                        pe.wait_ge(masked, (h + 1) * (LEVELS + 1))
                        tokens(acc[2], kf, 5)
                        tokens(acc[3], kb, 5).then_inc(kt_turned, 1)
                        next_steps(9)
                        pe.wait_ge(kt_ready, h + 1)
                        for u, (keys, c) in enumerate([(kf, 0), (kf, 1), (kf, 2), (kf, 4),
                                                       (kb, 3), (kb, 2), (kb, 1), (kb, 4)]):
                            at = slice(c * P, (c + 1) * P)
                            mm = nc.tensor.matmul(acc[2][:, u * P:(u + 1) * P], keys[:, at], v_tok[:, at],
                                                  start=True, stop=True)
                        mm.then_inc(ds_done, 1)
                        pe.wait_ge(states_ready, h + 1)
                        for c in range(5):
                            at = slice(c * P, (c + 1) * P)
                            terms = [(v_tok[:, at], scores[:, at])]
                            if c < 4:
                                terms += [(states[:, c * P:(c + 1) * P], qf[:, at]),
                                          (states[:, (4 + c) * P:(5 + c) * P], qb[:, at])]
                            mm = product(acc[3][:, at], terms)
                        mm.then_inc(o_done, 1)
                        head_norm(hd, acc[2])
                        hd += 1
                    pe.wait_ge(o_ready, hd)
                    n0 = first[("hgrn_out", layer)]
                    for o in range(KT):
                        job(n0 + o, (n0 + o) % SLOTS, KT, lambda k: g_hi[:, k, :], lambda k: g_lo[:, k, :])
                else:
                    pe.wait_ge(h_ready, KT * split_norms[2 * layer + 1])
                    pe.wait_ge(mixer_landed, mixer_loads[layer])
                    n0 = first[("diff_in", layer)]
                    qt = 0
                    job_steps(n0, 0, 3 * KT, 1)

                    def scores_of(tile, kcache):
                        at = slice(tile * P, (tile + 1) * P)
                        for c in range(2):
                            rows = slice(64 * c, 64 * c + 64)
                            if tile < 4:
                                nc.tensor.matmul(acc[1 + c][:, 0:512], qr[rows, at], kr[rows, 0:512], start=True, stop=True)
                                mm = nc.tensor.matmul(acc[1 + c][:, 512:768], qr[rows, at], kcache[rows, :], start=True, stop=True)
                            else:
                                mm = nc.tensor.matmul(acc[1 + c][:, 0:P], qr[rows, at], kr[rows, at], start=True, stop=True)
                        mm.then_inc(sc_done, 1)

                    for h in range(HEADS):
                        pe.wait_ge(job_used, n0 + 3 * h + 3)
                        if h:
                            pe.wait_ge(exp_done, 2 * qt)
                        tokens(acc[2], dv_t, 5).then_inc(v_turned, 1)
                        nc.tensor.matmul(acc[1][:, 0:512], turn[:], dq[:, 0:512], start=True, stop=True)
                        nc.tensor.matmul(acc[1][:, 512:1024], turn[:], dk[:, 0:512], start=True, stop=True).then_inc(rot_done, 1)
                        pe.wait_ge(qk_ready, h + 1)
                        pe.wait_ge(v_ready, HEADS + h + 1)
                        pe.wait_ge(cache_landed[h % 2], 32 * (h // 2 + 1))
                        kcache, vcache = kc[h % 2], vc[h % 2]
                        scores_of(0, kcache)
                        for tile in range(5):
                            if tile < 4:
                                pe.wait_ge(exp_done, 2 * qt + 2)
                                scores_of(tile + 1, kcache)
                            pe.wait_ge(w_ready, qt + 1)
                            if qt:
                                pe.wait_ge(o_copied, qt)
                            if tile == 0 and h:
                                pe.wait_ge(osqrt_done, hd)
                            nkt = 6 if tile < 4 else 1
                            tokens(acc[3], prob[0], nkt).then_inc(wt_done, 1)
                            if h + 1 < HEADS:
                                job_steps(n0 + 3 * (h + 1), 4 * tile, 4 * tile + (4 if tile < 4 else 8), 1)
                            pe.wait_ge(wt_ready, qt + 1)
                            terms = []
                            for k in range(nkt):
                                if tile == 4:
                                    vals = dv_tok[:, 512:640]
                                elif k < 4:
                                    vals = dv_tok[:, k * P:(k + 1) * P]
                                else:
                                    vals = vcache[:, (k - 4) * P:(k - 3) * P]
                                terms.append((vals, prob_t[:, k * P:(k + 1) * P]))
                            product(acc[3][:, 768:896], terms).then_inc(pv_done, 1)
                            qt += 1
                        pe.wait_ge(o_copied, qt)
                        head_norm(hd, acc[3])
                        hd += 1
                    pe.wait_ge(o_ready, hd)
                    n0 = first[("diff_out", layer)]
                    for o in range(KT):
                        job(n0 + o, (n0 + o) % SLOTS, KT, lambda k: g_hi[:, k, :], lambda k: g_lo[:, k, :])
                norm(2 * layer + 1, first[("up", layer)])
                pe.wait_ge(h_ready, KT * split_norms[2 * layer + 2])
                n = first[("up", layer)]
                g_at = NPAIR * layer
                for what, p0, count, piece in up_iters():
                    if what == "up":
                        def body(i, n=n, piece=piece):
                            for j in range(SLOTS):
                                def sides():
                                    k = i + ((layer + 1) * MOD_PIECES + piece)
                                    mod_piece(k, lambda: pe.wait_ge(mod_ready, k))
                                job(i * SLOTS + (n + j), j, KT, lambda k: h_hi[:, k, :], lambda k: h_lo[:, k, :],
                                    sides if j == 3 and layer + 1 < DEPTH else None)
                        if n == 0:
                            body(0)
                            with pe.Fori(1, count // 2) as i:
                                body(i)
                        else:
                            loop(pe, count // 2, body)
                        n += 2 * count
                    else:
                        pe.wait_ge(g_ready, g_at + p0 + count)

                        def body(i, n=n, last=(p0 + count == NPAIR and layer + 1 < DEPTH)):
                            for j in range(SLOTS):
                                job(i * SLOTS + (n + j), j, count, lambda k: g_hi[:, (p0 + k) % RING_G, :],
                                    lambda k: g_lo[:, (p0 + k) % RING_G, :])
                        if p0 + count == NPAIR and layer + 1 < DEPTH:
                            for i in range(2):
                                for j in range(SLOTS):
                                    piece = (layer + 2) * MOD_PIECES - 1
                                    job(n + 4 * i + j, j, count, lambda k: g_hi[:, (p0 + k) % RING_G, :],
                                        lambda k: g_lo[:, (p0 + k) % RING_G, :],
                                        (lambda: mod_piece(piece, lambda: pe.wait_ge(mod_ready, piece)))
                                        if i == 0 and j == 3 else None)
                        else:
                            loop(pe, 2, body)
                        n += KT
            norm(2 * DEPTH, NJOBS)

        @block.scalar
        def _(act):
            steps = [0]

            def link(ins):
                ins.then_inc(act_step, 1)
                steps[0] += 1
                act.wait_ge(act_step, steps[0])

            def high(n, j):
                act.wait_ge(raw_landed[j], (n - j) * 4 + 16)
                if not (isinstance(n, int) and n < SLOTS):
                    act.wait_ge(job_done, n - (SLOTS - 1))
                nc.scalar.activation(w_hi[j][:], w_raw[j][:], ACT.Copy).then_inc(hi_done, 1)

            def ahead(n, j):
                if isinstance(n, int) and n + 3 >= NJOBS:
                    return
                high(n + 3, (j + 3) % SLOTS)

            def load_mod(k, half, free):
                free()
                act.dma_start(mod_w[half][:], dram["ada_w"][k * 2 + half]).then_inc(mod_landed[half], 16)

            def mixer_constants(layer):
                if layer == 0:
                    act.wait_ge(mod_done, MOD_PIECES)
                what = {0: ((inv, dram["inv"]), (pool_w, dram["pool_w"][pools.get(layer, 0)]),
                            (sg, dram["pool_scale"][pools.get(layer, 0)])),
                        1: ((masks, dram["masks"]), (lb_in, dram["lb"])),
                        2: ((cos, dram["cos"]), (sin, dram["sin"]), (turn, dram["turn"]), (lam_in, dram["lam"]))}[KINDS[layer]]
                for dst, src in what:
                    act.dma_start(dst[:], src).then_inc(mixer_landed, 16)

            def norm(k, plain):
                for kt in range(KT):
                    if k:
                        updated, before = x_updates(k)
                        act.wait_ge(updated, before + kt + 1)
                    if KT * k + kt >= 2:
                        act.wait_ge(sq_used, KT * k + kt - 1)
                    nc.scalar.activation(sq[kt % 2][:], x[:, kt, :], ACT.Square).then_inc(sq_done, 1)
                act.wait_ge(sq_used, KT * (k + 1))
                if k % 2 == 0 and k < 2 * DEPTH:
                    mixer_constants(k // 2)
                nc.scalar.activation(rstd[:], acc[0][:, 0:T], ACT.Sqrt, bias=EPS).then_inc(sqrt_done, 1)
                if k == 2 * DEPTH:
                    return
                layer, c0_b = k // 2, 24 * (k % 2)
                for kt in range(KT):
                    act.wait_ge(scaled, KT * k + kt + 1)
                    dst = pool_h[:, kt, :] if plain else hf[kt % 2][:]
                    if not plain and kt >= 2:
                        act.wait_ge(h_ready, KT * split_norms[k] + kt - 1)
                    for c0, c1, row in RANGES:
                        b = 2 * (c0_b + kt) + row
                        ins = nc.scalar.activation(dst[:, c0:c1], sq[kt % 2][:, c0:c1], ACT.Identity,
                                                   bias=mod[:, layer % 2, b:b + 1])
                    ins.then_inc(h_full, 1)
                    if not plain:
                        act.wait_ge(h_full, KT * k + kt + 1)
                        nc.scalar.activation(h_hi[:, kt, :], dst, ACT.Copy).then_inc(h_rounded, 1)

            def head_norm(h0, h, src, ps, last):
                act.wait_ge(*last)
                if h0:
                    act.wait_ge(o_ready, h0)
                nc.scalar.activation(sq[0][:], src[:, 0:T], ACT.Square).then_inc(osq_done, 1)
                act.wait_ge(oms_done, h0 + 1)
                nc.scalar.activation(rstd[:], ps[:, 0:T], ACT.Sqrt, bias=EPS).then_inc(osqrt_done, 1)
                act.wait_ge(o_full, h0 + 1)
                nc.scalar.activation(g_hi[:, h, :], sq[1][:], ACT.Copy).then_inc(o_rounded, 1)

            act.wait_ge(loaded, 16 * N_CONST)
            nc.scalar.activation(sq[0][:, 0:2 * KT], sil_cond[:], ACT.Sigmoid).then_inc(act_step, 1)
            steps[0] = 1
            for k in range(MOD_PIECES):
                for half in range(2):
                    load_mod(k, half, lambda: act.wait_ge(mod_done, k) if k else None)
            for n in range(3):
                high(n, n)
            hd = 0
            for layer, kind in layer_parts():
                norm(2 * layer, kind == 0)
                if kind == 1:
                    n0 = first[("hgrn_in", layer)]
                    act.wait_ge(lb_sem, 1)
                    nc.scalar.activation(lb_in[:], lb_in[:], ACT.Exp).then_inc(lb_sem, 1)
                    def project_head(h):
                        for part in range(5):
                            n = n0 + 5 * h + part
                            ahead(n, n % SLOTS)
                            if part in (1, 2, 4):
                                act.wait_ge(job_done, n + 1)
                                dst = {1: f_f, 2: f_b, 4: gates[h % 2]}[part]
                                if part == 1 and h:
                                    act.wait_ge(level_ready, (h - 1) * (LEVELS + 2) + 3)
                                nc.scalar.activation(dst[:], acc[n % 2][:, 0:T], ACT.Sigmoid).then_inc(sig_done, 1)

                    project_head(0)
                    for h in range(HEADS):
                        act.dma_start(states[:, 0:P], dram["s0"][0, h]).then_inc(s0_landed, 16)
                        act.dma_start(states[:, 7 * P:8 * P], dram["s0"][1, h]).then_inc(s0_landed, 16)
                        if h + 1 < HEADS:
                            project_head(h + 1)
                        act.wait_ge(st_ready, h + 1)
                        act.dma_start(dram["new_state"][h], st_out[:]).then_inc(st_stored, 16)
                        head_norm(hd, h, acc[3], acc[2], (o_done, h + 1))
                        hd += 1
                    n0 = first[("hgrn_out", layer)]
                    for o in range(KT):
                        ahead(n0 + o, (n0 + o) % SLOTS)
                elif kind == 2:
                    act.wait_ge(lam_sem, 1)
                    nc.scalar.activation(small[:, 2:4], small[:, 0:2], ACT.Exp).then_inc(lam_sem, 1)
                    n0 = first[("diff_in", layer)]
                    qt = 0
                    for h in range(2):
                        act.dma_start(kc[h][:], dram["cache_k"][h]).then_inc(cache_landed[h], 16)
                        act.dma_start(vc[h][:], dram["cache_v"][h]).then_inc(cache_landed[h], 16)
                    for part in range(3):
                        ahead(n0 + part, (n0 + part) % SLOTS)
                    for h in range(HEADS):
                        act.wait_ge(v_ready, HEADS + h + 1)
                        act.wait_ge(qk_ready, h + 1)
                        act.dma_start(dram["new_k"][h], kr[:, N_SAMPLE:T]).then_inc(kv_stored, 16)
                        act.dma_start(dram["new_v"][h], dv_tok[:, N_SAMPLE:T]).then_inc(kv_stored, 16)

                        def exps(tile):
                            nk = NK if tile < 4 else P
                            act.wait_ge(mx_ready, 5 * h + tile + 1)
                            for c in range(2):
                                nc.scalar.activation(prob[c][:, 0:nk], acc[1 + c][:, 0:nk], ACT.Exp,
                                                     bias=small[:, 10 + c:11 + c], scale=SCALE,
                                                     accum_out=small[:, 12 + c:13 + c]).then_inc(exp_done, 1)

                        exps(0)
                        for tile in range(5):
                            nk = NK if tile < 4 else P
                            if h + 1 < HEADS and tile % 2 == 0:
                                n = n0 + 3 * (h + 1) + tile // 2
                                ahead(n, n % SLOTS)
                            act.wait_ge(wt_done, qt + 1)
                            nc.scalar.activation(prob_t[:, 0:nk], acc[3][:, 0:nk], ACT.Copy).then_inc(wt_ready, 1)
                            if tile < 4:
                                exps(tile + 1)
                            qt += 1
                        head_norm(hd, h, o_sb, acc[3], (o_copied, qt))
                        hd += 1
                        if h + 2 < HEADS:
                            act.dma_start(kc[h % 2][:], dram["cache_k"][h + 2]).then_inc(cache_landed[h % 2], 16)
                            act.dma_start(vc[h % 2][:], dram["cache_v"][h + 2]).then_inc(cache_landed[h % 2], 16)
                    n0 = first[("diff_out", layer)]
                    for o in range(KT):
                        ahead(n0 + o, (n0 + o) % SLOTS)
                norm(2 * layer + 1, False)
                act.dma_start(conv[:], dram["conv"][layer]).then_inc(conv_landed, 16)
                if layer + 1 < DEPTH:
                    for half in range(2):
                        load_mod((layer + 1) * MOD_PIECES, half, lambda: None)
                act.wait_ge(conv_landed, 16 * (layer + 1))
                n = first[("up", layer)]
                g_at = NPAIR * layer
                for what, p0, count, piece in up_iters():
                    if what == "up":
                        def body(i, n=n, p0=p0, piece=piece):
                            for pair in range(2):
                                p = i * 2 + (p0 + pair)
                                done = i * 2 + (g_at + p0 + pair)
                                for side in range(2):
                                    j = 2 * pair + side
                                    ahead(i * SLOTS + (n + j), j)
                                    act.wait_ge(job_done, i * SLOTS + (n + j + 1))
                                    if not (isinstance(i, int) and layer == 0 and p0 + pair + 2 * i == 0):
                                        act.wait_ge(gated, done)
                                    dst = acc_a if side == 0 else acc_v
                                    c10 = p * 20 + side * 10
                                    nc.scalar.activation(dst[:], acc[j][:, 0:T], ACT.Identity,
                                                         bias=conv[:, bass.ds(c10 + 9, 1)],
                                                         scale=conv[:, bass.ds(c10 + 4, 1)]).then_inc(center_done, 1)
                                act.wait_ge(job_used, i * SLOTS + (n + 2 * pair + 1))
                                if not (isinstance(i, int) and layer == 0 and p0 + pair + 2 * i == 0):
                                    act.wait_ge(g_ready, done)
                                nc.scalar.activation(sil[:], acc_a[:], ACT.Silu).then_inc(silu_done, 1)
                                act.wait_ge(gated, done + 1)
                                slot = (p0 + pair) % RING_G
                                dst = g_hi[:, i * 2 + slot, :]
                                nc.scalar.activation(dst, sil[:], ACT.Copy).then_inc(g_rounded, 1)
                            if layer + 1 < DEPTH:
                                k = i + ((layer + 1) * MOD_PIECES + piece)
                                for half in range(2):
                                    load_mod(k + 1, half, lambda: act.wait_ge(mod_done, k + 1))
                        if layer == 0 and p0 == 0:
                            body(0)
                            with act.Fori(1, count // 2) as i:
                                body(i)
                        else:
                            loop(act, count // 2, body)
                        n += 2 * count
                    else:
                        if n + KT + 3 > NJOBS:
                            for u in range(KT):
                                ahead(n + u, u % SLOTS)
                        else:
                            def body(i, n=n):
                                for j in range(SLOTS):
                                    ahead(i * SLOTS + (n + j), j)
                            loop(act, 2, body)
                        n += KT
            norm(2 * DEPTH, True)
            act.wait_ge(st_stored, 16 * HEADS)
            act.wait_ge(kv_stored, 32 * HEADS)

        @block.vector
        def _(dve):
            V = nc.vector
            steps = [0]

            def link(ins):
                ins.then_inc(dve_step, 1)
                steps[0] = steps[0] + 1
                dve.wait_ge(dve_step, steps[0])

            def linked_loop(iters, per, body, start=0):
                base = steps[0]
                if iters - start == 1:
                    body(start)
                    assert steps[0] == base + per
                    return
                with dve.Fori(start, iters) as i:
                    steps[0] = i * per + (base - start * per)
                    body(i)
                steps[0] = base + per * (iters - start)

            def mod_piece(k, layer):
                dve.wait_ge(mod_done, k + 1)
                c = (k - layer * MOD_PIECES) * 8
                V.tensor_tensor(mod[:, layer % 2, bass.ds(c, 8)], acc[3][:, 640:648], mod_b[:, layer, bass.ds(c, 8)],
                                ALU.add).then_inc(mod_ready, 1)

            def norm(k, plain):
                layer = k // 2
                if k < 2 * DEPTH:
                    dve.wait_ge(mod_ready, (layer + 1) * MOD_PIECES)
                    s0 = 2 * (24 * (k % 2) + 8)
                    V.scalar_tensor_tensor(out=mod_a[:], in0=mod[:, layer % 2, s0:s0 + 2 * KT], scalar=1.0,
                                           in1=norms[:, k, :], op0=ALU.add, op1=ALU.mult).then_inc(mod_a_ready, 1)
                    dve.wait_ge(mod_a_ready, k + 1)
                dve.wait_ge(sqrt_done, k + 1)
                V.reciprocal(rstd[:], rstd[:]).then_inc(rstd_done, 1)
                dve.wait_ge(rstd_done, k + 1)
                for kt in range(KT):
                    if k == 2 * DEPTH:
                        V.scalar_tensor_tensor(out=pool_h[:, kt, :], in0=x[:, kt, :], scalar=norms[:, k, 2 * kt:2 * kt + 1],
                                               in1=rstd[:], op0=ALU.mult, op1=ALU.mult).then_inc(y_ready, 1)
                        continue
                    if kt >= 2:
                        dve.wait_ge(h_full, KT * k + kt - 1)
                    for c0, c1, row in RANGES:
                        ins = V.scalar_tensor_tensor(out=sq[kt % 2][:, c0:c1], in0=x[:, kt, c0:c1],
                                                     scalar=mod_a[:, 2 * kt + row:2 * kt + row + 1],
                                                     in1=rstd[:, c0:c1], op0=ALU.mult, op1=ALU.mult)
                    ins.then_inc(scaled, 1)
                    if not plain and kt >= 1:
                        low_h(k, kt - 1)
                if k < 2 * DEPTH and not plain:
                    low_h(k, KT - 1)

            def low_h(k, kt):
                dve.wait_ge(h_rounded, KT * split_norms[k] + kt + 1)
                V.tensor_tensor(h_lo[:, kt, :], hf[kt % 2][:], h_hi[:, kt, :].bitcast(F32), ALU.subtract).then_inc(h_ready, 1)

            def add_x(o, src, scalars, at):
                for c0, c1, row in RANGES:
                    ins = V.scalar_tensor_tensor(out=x[:, o, c0:c1], in0=src[:, c0:c1],
                                                 scalar=scalars[:, bass.ds(at + row, 1)],
                                                 in1=x[:, o, c0:c1], op0=ALU.mult, op1=ALU.add)
                return ins

            def project(n, layer):
                for o in range(KT):
                    dve.wait_ge(job_done, n + o + 1)
                    add_x(o, acc[(n + o) % SLOTS], mod[:, layer % 2, :], 2 * (16 + o)).then_inc(job_used, 1)

            def head_norm(h0, h, src, gain, gated_by):
                dve.wait_ge(osqrt_done, h0 + 1)
                link(V.reciprocal(rstd[:], rstd[:]))
                link(V.tensor_tensor(sq[1][:], src[:, 0:T], rstd[:], ALU.mult))
                if gated_by is not None:
                    V.scalar_tensor_tensor(out=sq[1][:], in0=sq[1][:], scalar=gain, in1=gated_by[:],
                                           op0=ALU.mult, op1=ALU.mult).then_inc(o_full, 1)
                else:
                    V.tensor_scalar(sq[1][:], sq[1][:], gain, None, ALU.mult).then_inc(o_full, 1)
                dve.wait_ge(o_rounded, h0 + 1)
                V.tensor_tensor(g_lo[:, h, :], sq[1][:], g_hi[:, h, :].bitcast(F32), ALU.subtract).then_inc(o_ready, 1)

            def lower_bounds(layer):
                v = lb_in[:].rearrange("p (d l k) -> p d l k", d=2, l=DEPTH)
                by_layer = [v[:, :, l, :] for l in range(DEPTH)]
                top = lb[:, 0:2 * KT].rearrange("p (d k) -> p d k", d=2)
                rest = lb[:, 2 * KT:4 * KT].rearrange("p (d k) -> p d k", d=2)
                link(V.tensor_tensor(top, by_layer[0], by_layer[1], ALU.max))
                for l in range(2, DEPTH):
                    link(V.tensor_tensor(top, top, by_layer[l], ALU.max))
                for l in range(DEPTH):
                    ins = V.tensor_tensor(by_layer[l], by_layer[l], top, ALU.subtract)
                ins.then_inc(lb_sem, 1)
                dve.wait_ge(lb_sem, 2)
                link(V.tensor_tensor(rest, by_layer[0], by_layer[1], ALU.add))
                for l in range(2, DEPTH):
                    link(V.tensor_tensor(rest, rest, by_layer[l], ALU.add))
                link(V.reciprocal(rest, rest))
                for l in range(2, layer + 1):
                    link(V.tensor_tensor(by_layer[1], by_layer[1], by_layer[l], ALU.add))
                link(V.tensor_tensor(top, by_layer[1], rest, ALU.mult))
                link(V.tensor_scalar(lb[:, 2 * KT:4 * KT], lb[:, 0:2 * KT], -1.0, 1.0, ALU.mult, ALU.add))

            link(V.memset(small[:], 0.0))
            dve.wait_ge(loaded, 16 * N_CONST)
            dve.wait_ge(act_step, 1)
            V.tensor_tensor(sil_cond[:], sil_cond[:], sq[0][:, 0:2 * KT], ALU.mult).then_inc(silu_cond_done, 1)
            for k in range(MOD_PIECES):
                mod_piece(k, 0)
            hd = 0
            for layer, kind in layer_parts():
                norm(2 * layer, kind == 0)
                if kind == 0:
                    dve.wait_ge(mixer_landed, mixer_loads[layer])
                    link(V.tensor_tensor(sg[:], sg[:], mod[:, layer % 2, 32:48], ALU.mult))
                    for b in box_v:
                        link(V.memset(b[:], 0.0))
                    for kt in range(KT):
                        g = kt // 2
                        w = POOL_WINDOWS[g]
                        dve.wait_ge(h_full, KT * 2 * layer + kt + 1)
                        H = [b[:].rearrange("p (r c) -> p r c", c=80) for b in box_h]
                        B = [b[:].rearrange("p (r c) -> p r c", c=GRID_W) for b in box_v]
                        hs = pool_h[:, kt, 0:N_SAMPLE].rearrange("p (r c) -> p r c", c=GRID_W)
                        link(V.memset(box_h[0][:], 0.0))
                        link(V.tensor_copy(H[0][:, :, 8:72], hs))
                        src, s = 0, 1
                        lo_c, hi_c = 8 - w // 2, 72 - w // 2
                        while s < w:
                            end = hi_c + w - 2 * s
                            if 2 * s == w:
                                out_ap = B[0][:, 8:16, :]
                            else:
                                out_ap = H[1 - src][:, :, lo_c:end]
                            link(V.tensor_tensor(out_ap, H[src][:, :, lo_c:end], H[src][:, :, lo_c + s:end + s], ALU.add))
                            src, s = 1 - src, 2 * s
                        m = box_m[:, 0:N_SAMPLE].rearrange("p (r c) -> p r c", c=GRID_W)
                        if w // 2 >= ROWS:
                            link(V.tensor_reduce(box_h[1][:, 0:GRID_W],
                                                 B[0][:, 8:16, :].rearrange("p r c -> p c r"), AX.X, ALU.add))
                            link(V.tensor_tensor(m, box_h[1][:, 0:GRID_W].rearrange("p (r c) -> p r c", r=1).broadcast_to([P, ROWS, GRID_W]),
                                                 inv[:, g * T:g * T + N_SAMPLE].rearrange("p (r c) -> p r c", c=GRID_W), ALU.mult))
                        else:
                            src, s = 0, 1
                            lo_r, hi_r = 8 - w // 2, 16 - w // 2
                            while s < w:
                                end = hi_r + w - 2 * s
                                link(V.tensor_tensor(B[1 - src][:, lo_r:end, :], B[src][:, lo_r:end, :],
                                                     B[src][:, lo_r + s:end + s, :], ALU.add))
                                src, s = 1 - src, 2 * s
                            link(V.tensor_tensor(m, B[src][:, lo_r:hi_r, :],
                                                 inv[:, g * T:g * T + N_SAMPLE].rearrange("p (r c) -> p r c", c=GRID_W), ALU.mult))
                            if w > 2:
                                link(V.memset(B[0][:, 0:8, :], 0.0))
                                link(V.memset(B[0][:, 16:24, :], 0.0))
                        link(V.memset(box_h[1][:, 0:144], 0.0))
                        link(V.tensor_copy(box_h[1][:, 8:136], pool_h[:, kt, N_SAMPLE:T]))
                        offs, src, s = (0, 160), 0, 1
                        lo_c, hi_c = 8 - w // 2, 136 - w // 2
                        while s < w:
                            end = hi_c + w - 2 * s
                            a, b = offs[src], offs[1 - src]
                            link(V.tensor_tensor(box_h[1][:, b + lo_c:b + end], box_h[1][:, a + lo_c:a + end],
                                                 box_h[1][:, a + lo_c + s:a + end + s], ALU.add))
                            src, s = 1 - src, 2 * s
                        a = offs[src]
                        link(V.tensor_tensor(box_m[:, N_SAMPLE:T], box_h[1][:, a + lo_c:a + hi_c],
                                             inv[:, g * T + N_SAMPLE:(g + 1) * T], ALU.mult))
                        V.tensor_tensor(pool_d[:, kt, :], box_m[:], pool_h[:, kt, :], ALU.subtract).then_inc(pool_ready, 1)
                    for u in range(KT):
                        dve.wait_ge(pool_done, KT * pools[layer] + u + 1)
                        add_x(u, acc[1 + u % 3], sg, 2 * u).then_inc(x_ready, 1)
                elif kind == 1:
                    n0 = first[("hgrn_in", layer)]
                    dve.wait_ge(mixer_landed, mixer_loads[layer])
                    lower_bounds(layer)
                    def take(h, part):
                        n = n0 + 5 * h + part
                        ps = acc[n % 2][:, 0:T]
                        if part == 0:
                            dve.wait_ge(job_done, n + 1)
                            if h:
                                dve.wait_ge(level_done, (h - 1) * (LEVELS + 1) + 1)
                            V.tensor_copy(q[:], ps).then_inc(job_used, 1)
                        elif part < 3:
                            dve.wait_ge(sig_done, 3 * h + part)
                            f, at = (f_f, f_b)[part - 1], (part - 1) * KT + h
                            V.tensor_scalar(f[:], f[:], lb[:, 2 * KT + at:2 * KT + at + 1], lb[:, at:at + 1],
                                            ALU.mult, ALU.add).then_inc(job_used, 1)
                        elif part == 3:
                            dve.wait_ge(job_done, n + 1)
                            V.tensor_copy(v_t[:], ps).then_inc(job_used, 1)
                        else:
                            dve.wait_ge(sig_done, 3 * h + 3)
                            V.tensor_tensor(gates[h % 2][:], ps, gates[h % 2][:], ALU.mult).then_inc(job_used, 1)

                    for part in range(5):
                        take(0, part)
                    for h in range(HEADS):
                        dve.wait_ge(job_used, n0 + 5 * (h + 1))
                        link(V.tensor_scalar(kf[:], f_f[:], -1.0, 1.0, ALU.mult, ALU.add))
                        link(V.tensor_scalar(kb[:], f_b[:], -1.0, 1.0, ALU.mult, ALU.add))
                        V.tensor_tensor(k_sum[:], kf[:], kb[:], ALU.add).then_inc(level_ready, 1)
                        link(V.tensor_tensor(qf[:], q[:], f_f[:], ALU.mult))
                        V.tensor_tensor(qb[:], q[:], f_b[:], ALU.mult).then_inc(level_ready, 1)
                        dve.wait_ge(v_turned, h + 1)
                        V.tensor_copy(v_tok[:], acc[2][:, 0:T]).then_inc(v_ready, 1)
                        tf, tb = f_f[:, 0:T], f_b[:, 0:T]
                        t_at = 0
                        for level in range(LEVELS + 1):
                            s = 2 + (level + 1) % 2
                            dve.wait_ge(level_done, h * (LEVELS + 1) + level + 1)
                            ps3 = acc[s][:, 0:T].rearrange("p (c t) -> p c t", t=P)
                            sc3 = scores[:].rearrange("p (c t) -> p c t", t=P)
                            mk = masks[:, level * P:(level + 1) * P].rearrange("p (c t) -> p c t", c=1).broadcast_to([P, 5, P])
                            if level == 0:
                                V.tensor_tensor(sc3, ps3, mk, ALU.mult).then_inc(masked, 1)
                                continue
                            m = 1 << (level - 1)
                            nb = T // (2 * m)

                            def halves(t, half):
                                return t[:, 0:T].rearrange("p (b h m) -> p b h m", h=2, m=m)[:, :, half, :]

                            def total(t, half):
                                return t.rearrange("p (b h) -> p b h", h=2)[:, :, half:half + 1]

                            for dst, half, t in ((qf, 1, tf), (kf, 0, tf), (qb, 0, tb), (kb, 1, tb)):
                                V.tensor_tensor(halves(dst, half), halves(dst, half),
                                                total(t, 1 - half).broadcast_to([P, nb, m]), ALU.mult)
                            new = []
                            for t, store in ((tf, tot_f), (tb, tot_b)):
                                out_t = store[:, t_at:t_at + nb]
                                ins = V.tensor_tensor(out_t.rearrange("p (b h) -> p b h", h=1), total(t, 0), total(t, 1), ALU.mult)
                                new.append(out_t)
                            ins.then_inc(level_ready, 1)
                            tf, tb = new
                            t_at += nb
                            dve.wait_ge(masked, h * (LEVELS + 1) + level)
                            V.copy_predicated(sc3, mk.bitcast(U32), ps3).then_inc(masked, 1)
                            if h + 1 < HEADS and level in (2, 4, 6, 7):
                                take(h + 1, (2, 4, 6, 7).index(level))
                        dve.wait_ge(kt_turned, h + 1)
                        link(V.tensor_copy(kf[:], acc[2][:, 0:T]))
                        V.tensor_copy(kb[:], acc[3][:, 0:T]).then_inc(kt_ready, 1)
                        dve.wait_ge(ds_done, h + 1)
                        dve.wait_ge(s0_landed, 32 * (h + 1))
                        if h:
                            dve.wait_ge(st_stored, 16 * h)
                        V.tensor_copy(st_out[:, 0:P], acc[2][:, 3 * P:4 * P])
                        V.tensor_copy(st_out[:, P:2 * P], acc[2][:, 7 * P:8 * P]).then_inc(st_ready, 1)
                        for u in range(3):
                            for base, c, to, t, at in ((0, u, u + 1, tf, u), (4, 3 - u, 2 - u, tb, 4 + u)):
                                ins = V.scalar_tensor_tensor(out=states[:, (base + to) * P:(base + to + 1) * P],
                                                             in0=states[:, (base + c) * P:(base + c + 1) * P],
                                                             scalar=t[:, c:c + 1], in1=acc[2][:, at * P:(at + 1) * P],
                                                             op0=ALU.mult, op1=ALU.add)
                                if u < 2 or base == 0:
                                    link(ins)
                                else:
                                    ins.then_inc(states_ready, 1)
                        if h + 1 < HEADS:
                            take(h + 1, 4)
                        head_norm(hd, h, acc[3], norms_h[:, 0:1], gates[h % 2])
                        hd += 1
                    project(first[("hgrn_out", layer)], layer)
                else:
                    n0 = first[("diff_in", layer)]
                    dve.wait_ge(mixer_landed, mixer_loads[layer])
                    lam_init = 0.8 - 0.6 * math.exp(-0.3 * layer)
                    for u in range(2):
                        a = 128 * u
                        link(V.tensor_tensor(lam_in[:, a:a + 64], lam_in[:, a:a + 64], lam_in[:, a + 64:a + 128], ALU.mult))
                        link(V.tensor_reduce(small[:, u:u + 1], lam_in[:, a:a + 64], AX.X, ALU.add))
                    V.tensor_scalar(small[:, 7:8], small[:, 0:1], 1.0, None, ALU.mult).then_inc(lam_sem, 1)
                    dve.wait_ge(lam_sem, 2)
                    link(V.tensor_tensor(small[:, 4:5], small[:, 3:4], small[:, 2:3], ALU.subtract))
                    link(V.tensor_scalar(small[:, 5:6], small[:, 4:5], -lam_init, None, ALU.add))
                    link(V.tensor_scalar(small[:, 6:7], norms_h[:, 1:2], 1.0 - lam_init, None, ALU.mult))
                    qt = 0
                    def take(h, part):
                        n = n0 + 3 * h + part
                        dve.wait_ge(job_done, n + 1)
                        V.tensor_copy((dq, dk, dv_t)[part][:], acc[0][:, 0:T]).then_inc(job_used, 1)

                    def maxima(tile):
                        nk = NK if tile < 4 else P
                        dve.wait_ge(sc_done, 5 * h + tile + 1)
                        V.tensor_reduce(small[:, 8:9], acc[1][:, 0:nk], AX.X, ALU.max)
                        link(V.tensor_reduce(small[:, 9:10], acc[2][:, 0:nk], AX.X, ALU.max))
                        V.tensor_scalar(small[:, 10:12], small[:, 8:10], -SCALE, None, ALU.mult).then_inc(mx_ready, 1)

                    for part in range(3):
                        take(0, part)
                    for h in range(HEADS):
                        if h:
                            dve.wait_ge(kv_stored, 32 * h)
                        dve.wait_ge(job_used, n0 + 3 * (h + 1))
                        dve.wait_ge(v_turned, HEADS + h + 1)
                        V.tensor_copy(dv_tok[:], acc[2][:, 0:T]).then_inc(v_ready, 1)
                        dve.wait_ge(rot_done, h + 1)
                        V.tensor_copy(qr[:, 512:T], dq[:, 512:T])
                        V.tensor_copy(kr[:, 512:T], dk[:, 512:T])
                        for part, (src, dst) in enumerate(((dq, qr), (dk, kr))):
                            link(V.tensor_tensor(dst[:, 0:512], src[:, 0:512], cos[:], ALU.mult))
                            link(V.tensor_tensor(sq[1][:, 0:512], acc[1][:, part * 512:(part + 1) * 512], sin[:], ALU.mult))
                            ins = V.tensor_tensor(dst[:, 0:512], dst[:, 0:512], sq[1][:, 0:512], ALU.add)
                            if part == 0:
                                link(ins)
                            else:
                                ins.then_inc(qk_ready, 1)
                        maxima(0)
                        for tile in range(5):
                            nk = NK if tile < 4 else P
                            dve.wait_ge(exp_done, 2 * qt + 2)
                            link(V.reciprocal(small[:, 14:16], small[:, 12:14]))
                            link(V.tensor_tensor(small[:, 16:17], small[:, 15:16], small[:, 5:6], ALU.mult))
                            link(V.tensor_scalar(prob[0][:, 0:nk], prob[0][:, 0:nk], small[:, 14:15], None, ALU.mult))
                            V.scalar_tensor_tensor(out=prob[0][:, 0:nk], in0=prob[1][:, 0:nk], scalar=small[:, 16:17],
                                                   in1=prob[0][:, 0:nk], op0=ALU.mult, op1=ALU.add).then_inc(w_ready, 1)
                            if tile < 4:
                                maxima(tile + 1)
                            if h + 1 < HEADS and tile in (1, 3, 4):
                                take(h + 1, tile // 2)
                            dve.wait_ge(pv_done, qt + 1)
                            if tile == 0 and h:
                                dve.wait_ge(o_ready, hd)
                            V.tensor_copy(o_sb[:, tile * P:(tile + 1) * P], acc[3][:, 768:896]).then_inc(o_copied, 1)
                            qt += 1
                        head_norm(hd, h, o_sb, small[:, 6:7], None)
                        hd += 1
                    project(first[("diff_out", layer)], layer)
                norm(2 * layer + 1, False)
                dve.wait_ge(conv_landed, 16 * (layer + 1))
                n = first[("up", layer)]
                g_at = NPAIR * layer
                for what, p0, count, piece in up_iters():
                    if what == "up":
                        def body(i, n=n, p0=p0, piece=piece):
                            for pair in range(2):
                                p = i * 2 + (p0 + pair)
                                done = i * 2 + (g_at + p0 + pair)
                                j = 2 * pair
                                views = []
                                for side, dst in enumerate((acc_a, acc_v)):
                                    u = acc[j + side]
                                    views.append((u[:, 0:N_SAMPLE].rearrange("p (r c) -> p r c", c=GRID_W),
                                                  dst[:, 0:N_SAMPLE].rearrange("p (r c) -> p r c", c=GRID_W),
                                                  u[:, N_SAMPLE:T], dst[:, N_SAMPLE:T], p * 20 + side * 10))
                                taps = [(dy, dx) for dy in (-1, 0, 1) for dx in (-1, 0, 1) if (dy, dx) != (0, 0)]
                                for step, (dy, dx) in enumerate([("p", -1), ("p", 1)] + taps):
                                    for side in range(2):
                                        us, ds, up, dp, c10 = views[side]
                                        if step == 0:
                                            dve.wait_ge(center_done, i * 4 + (2 * (g_at + p0 + pair) + side + 1))
                                            if pair == 1 and side == 1 and layer + 1 < DEPTH:
                                                mod_piece(i + ((layer + 1) * MOD_PIECES + piece), layer + 1)
                                        if dy == "p":
                                            a, b = max(0, -dx), N_PROMPT - max(0, dx)
                                            src, out, w = up[:, a + dx:b + dx], dp[:, a:b], 4 + dx
                                        else:
                                            r0, r1 = max(0, -dy), ROWS - max(0, dy)
                                            a, b = max(0, -dx), GRID_W - max(0, dx)
                                            src, out, w = us[:, r0 + dy:r1 + dy, a + dx:b + dx], ds[:, r0:r1, a:b], 4 + 3 * dy + dx
                                        ins = V.scalar_tensor_tensor(out=out, in0=src, scalar=conv[:, bass.ds(c10 + w, 1)],
                                                                     in1=out, op0=ALU.mult, op1=ALU.add)
                                        if step == 9:
                                            ins.then_inc(job_used, 1)
                                        else:
                                            ins.then_inc(dve_step, 1)
                                            steps[0] = steps[0] + 1
                                        if step < 9 and not (step == 0 and side == 0):
                                            dve.wait_ge(dve_step, steps[0] - 1)
                                        if step == 8 and side == 1:
                                            dve.wait_ge(dve_step, steps[0])
                                dve.wait_ge(job_used, i * 4 + (n + j + 2))
                                dve.wait_ge(silu_done, done + 1)
                                V.tensor_tensor(sil[:], sil[:], acc_v[:], ALU.mult).then_inc(gated, 1)
                                dve.wait_ge(g_rounded, done + 1)
                                slot = (p0 + pair) % RING_G
                                V.tensor_tensor(g_lo[:, i * 2 + slot, :], sil[:], g_hi[:, i * 2 + slot, :].bitcast(F32),
                                                ALU.subtract).then_inc(g_ready, 1)
                        linked_loop(count // 2, 36, body)
                        n += 2 * count
                    else:
                        def body(i, n=n):
                            for j in range(SLOTS):
                                dve.wait_ge(job_done, i * 4 + (n + j + 1))
                                if j == 3 and p0 + count == NPAIR and layer + 1 < DEPTH and i == 0:
                                    mod_piece((layer + 2) * MOD_PIECES - 1, layer + 1)
                                for c0, c1, row in RANGES:
                                    ins = V.scalar_tensor_tensor(out=x[:, i * 4 + j, c0:c1], in0=acc[j][:, c0:c1],
                                                                 scalar=mod[:, layer % 2, bass.ds(i * 8 + (2 * (40 + j) + row), 1)],
                                                                 in1=x[:, i * 4 + j, c0:c1], op0=ALU.mult, op1=ALU.add)
                                ins.then_inc(job_used, 1)
                        dve.wait_ge(job_used, n)
                        if p0 + count == NPAIR:
                            body(0)
                            body(1)
                        else:
                            with dve.Fori(0, 2) as i:
                                body(i)
                        n += KT
            norm(2 * DEPTH, True)


def kernel(**inputs):
    import numpy as np
    import concourse.bacc as bacc
    from concourse.bass_utils import run_bass_kernel_spmd

    a = {k: np.asarray(v) for k, v in inputs.items()}

    def chan(v):
        return np.moveaxis(v.reshape(*v.shape[:-1], -1, P), -1, 0)

    def tiles(w):
        k, n = w.shape
        return w.reshape(k // P, P, n // P, P).transpose(2, 1, 0, 3).reshape(n // P, P, -1)

    f32 = np.float32
    weights = {}
    for layer, kind in enumerate(KINDS):
        if kind == 1:
            weights["hgrn_in", layer] = tiles(a["hgrn_w_in"][layer // 3])
            weights["hgrn_out", layer] = tiles(a["hgrn_w_out"][layer // 3])
        elif kind == 2:
            weights["diff_in", layer] = tiles(a["diff_w_in"][layer // 3])
            weights["diff_out", layer] = tiles(a["diff_w_out"][layer // 3])
        weights["up", layer] = tiles(a["ffn_w_up"][layer])
        weights["down", layer] = tiles(a["ffn_w_down"][layer])
    wall = np.zeros((NJOBS, P, KT * P), f32)
    for n, (what, layer, index, nk) in enumerate(JOBS):
        if what == "down":
            p0, count, o = index
            wall[n, :, :count * P] = weights[what, layer][o, :, p0 * P:(p0 + count) * P]
        else:
            wall[n] = weights[what, layer][index]
    twice = lambda v: np.repeat(v[..., None], 2, axis=-1)
    data = {
        "x": chan(np.concatenate([a["x_sample"][0], a["x_prompt"][0]])).transpose(0, 2, 1),
        "cond": chan(np.stack([a["c"][0], a["c_ctx"]])).transpose(0, 2, 1).reshape(P, -1),
        "ada_b": twice(chan(a["ada_b"])).reshape(P, DEPTH, -1),
        "norms": twice(chan(np.stack([v for i in range(DEPTH) for v in (a["norm1"][i], a["norm2"][i])]
                                     + [a["final_norm"]]))).reshape(P, 2 * DEPTH + 1, -1),
        "norms_h": np.stack([a["hgrn_norm"][0], a["diff_subln"][0]], axis=1),
        "ones_d": np.full((P, P), 1 / D_MODEL, f32),
        "ones_h": np.full((P, P), 1 / P, f32),
        "ident": np.eye(P, dtype=f32),
        "wall": wall,
        "ada_w": a["ada_w"].reshape(DEPTH, KT, P, CHUNKS_MOD // 2, 256).transpose(0, 3, 2, 1, 4).reshape(-1, P, KT * 256),
        "pool_w": a["pool_w"].reshape(-1, 4, 2, P, 2, P).transpose(0, 3, 1, 2, 4, 5).reshape(-1, P, 4 * 2 * 256),
        "pool_scale": twice(chan(a["pool_scale"])).transpose(1, 0, 2, 3).reshape(-1, P, 2 * KT),
        "lb": chan(a["hgrn_lb"]).reshape(P, -1),
        "s0": a["state_hgrn"][0, 0],
        "cache_k": a["cache_k"][0, 0].transpose(1, 2, 3, 0).reshape(HEADS, P, PAST),
        "cache_v": a["cache_v"][0, 0].reshape(2, P, HEADS, P).transpose(2, 1, 0, 3).reshape(HEADS, P, PAST),
        "lam": np.repeat(a["diff_lambda"].reshape(1, -1), P, axis=0),
    }
    taps = np.concatenate([a["ffn_conv_w"].reshape(DEPTH, 9, -1), a["ffn_conv_b"][:, None]], axis=1)
    data["conv"] = taps.reshape(DEPTH, 10, 2, NPAIR, P).transpose(0, 4, 3, 2, 1).reshape(DEPTH, P, -1)
    def sizes(n, w):
        i = np.arange(n)
        return np.clip(i + w // 2, 0, n) - np.clip(i - w // 2, 0, n)

    inv = np.zeros((4, T), f32)
    for g, w in enumerate(POOL_WINDOWS):
        inv[g, :N_SAMPLE] = 1.0 / np.outer(sizes(ROWS, w), sizes(GRID_W, w)).reshape(-1)
        inv[g, N_SAMPLE:] = 1.0 / sizes(N_PROMPT, w)
    data["inv"] = np.broadcast_to(inv.reshape(1, -1), (P, 4 * T))
    masks = np.zeros((P, LEVELS + 1, P), f32)
    s, t = np.arange(P)[:, None], np.arange(P)[None, :]
    masks[:, 0] = s == t
    for level in range(1, LEVELS + 1):
        m = 1 << (level - 1)
        masks[:, level] = (s // (2 * m) == t // (2 * m)) & (s // m != t // m)
    data["masks"] = masks.reshape(P, -1)
    half, nf = 32, 16
    freq = 10000.0 ** (-np.arange(nf, dtype=f32) / nf)
    tok = np.arange(N_SAMPLE)
    d = np.arange(P) % 64
    pos = np.where((d < half)[:, None], tok[None, :] // GRID_W, tok[None, :] % GRID_W)
    angle = pos.astype(f32) * freq[d % nf][:, None].astype(f32)
    data["cos"], data["sin"] = np.cos(angle).astype(f32), np.sin(angle).astype(f32)
    turn = np.zeros((P, P), f32)
    for p in range(P):
        if p % 32 < nf:
            turn[p + nf, p] = -1
        else:
            turn[p - nf, p] = 1
    data["turn"] = turn
    data = {k: np.ascontiguousarray(v) for k, v in data.items()}
    outs = {"y": (P, KT, T), "new_state": (HEADS, P, 2 * P), "new_k": (HEADS, P, N_PROMPT), "new_v": (HEADS, P, N_PROMPT)}

    nc = bacc.Bacc("TRN2", target_bir_lowering=False, num_devices=1)
    dram = {k: nc.dram_tensor(f"in_{k}", v.shape, F32, kind="ExternalInput").ap() for k, v in data.items()}
    dram |= {k: nc.dram_tensor(f"out_{k}", v, F32, kind="ExternalOutput").ap() for k, v in outs.items()}
    trunk(nc, dram)
    got = run_bass_kernel_spmd(nc, [{f"in_{k}": v for k, v in data.items()}], core_ids=[0]).results[0]
    y = got["out_y"].transpose(2, 1, 0).reshape(T, D_MODEL)
    state = got["out_new_state"].reshape(HEADS, P, 2, P).transpose(2, 0, 1, 3)
    new_k = got["out_new_k"].transpose(2, 0, 1).reshape(N_PROMPT, HEADS, 2, 64)
    new_v = got["out_new_v"].transpose(1, 0, 2)
    return (y[None, N_SAMPLE:], y[None, :N_SAMPLE], state[None, None], new_k[None, None], new_v[None, None])
```

```python
from contextlib import ExitStack
import math

import concourse.bass as bass
from concourse import mybir

F32 = mybir.dt.float32
F32R = mybir.dt.float32r
U32 = mybir.dt.uint32
ACT = mybir.ActivationFunctionType
ALU = mybir.AluOpType
AX = mybir.AxisListType

P = 128
D_MODEL = 1024
KT = D_MODEL // P
N_SAMPLE, N_PROMPT = 512, 128
T = N_SAMPLE + N_PROMPT
GRID_W = 64
ROWS = N_SAMPLE // GRID_W
DEPTH = 4
D_FF = ((8 * D_MODEL // 3) + 127) // 128 * 128
NPAIR = D_FF // P
HEADS = 8
LEVELS = 7
PAST = 256
EPS = 1e-6
KINDS = [i % 3 for i in range(DEPTH)]
CHUNKS_MOD = 48
RING_G = 10
SEGMENTS = [("up", 0, 10), ("down", 0, 8), ("up", 10, 8), ("down", 8, 4), ("up", 18, 2), ("up", 20, 2),
            ("down", 12, 6), ("down", 18, 4)]
RANGES = [(0, N_SAMPLE, 0), (N_SAMPLE, T, 1)]
BANK = 512
OUT = BANK - T // 2
HALVES = [(0, T // 2), (T // 2, T)]
SLOTS = 4
SCALE = 64 ** -0.5
MOD_AT = OUT + T
LATE_AT = (MOD_AT, 0)
EARLY = CHUNKS_MOD // 3
POOL_WINDOWS = (2, 4, 8, 16)


def mods_in_ffn(layer):
    if layer + 1 == DEPTH:
        return 0
    return CHUNKS_MOD if KINDS[layer + 1] else CHUNKS_MOD // 2


def has_mods(layer, what, p0, n):
    if mods_in_ffn(layer) == CHUNKS_MOD:
        return what == "up" or (what, p0) == SEGMENTS[-1][:2]
    return mods_in_ffn(layer) > 0 and (what, p0) in (SEGMENTS[0][:2], SEGMENTS[-1][:2])


def tile_plan():
    plan = [("mod", 0, c, KT) for c in range(CHUNKS_MOD // 2)]
    for layer, kind in enumerate(KINDS):
        if kind == 0:
            plan += [("mod", layer, c, KT) for c in range(CHUNKS_MOD // 2, CHUNKS_MOD)]
        mods = [("mod", layer + 1, c, KT) for c in range(mods_in_ffn(layer))]
        if kind == 1:
            for h in range(HEADS):
                plan += [("hgrn_in", layer, part * HEADS + h, KT) for part in (0, 3, 4, 1, 2)]
            plan += [("hgrn_out", layer, o, KT) for o in range(KT)]
        elif kind == 2:
            for h in range(HEADS):
                plan += [("diff_in", layer, part * HEADS + h, KT) for part in (0, 1, 2)]
            plan += [("diff_out", layer, o, KT) for o in range(KT)]
        for what, p0, n in SEGMENTS:
            if what == "up":
                for p in range(p0, p0 + n):
                    for index in (p, NPAIR + p):
                        if has_mods(layer, what, p0, n):
                            plan.append(mods.pop(0))
                        plan.append(("up", layer, index, KT))
            else:
                for o in range(KT):
                    if has_mods(layer, what, p0, n) and mods:
                        plan.append(mods.pop(0))
                    plan.append(("down", layer, (p0, n, o), n))
        assert not mods
    return plan


PLAN = tile_plan()
NTILES = len(PLAN)
NJOBS = sum(what != "mod" for what, *_ in PLAN)


def trunk(nc, dram):
    ctx = ExitStack()
    with ctx:
        def sb(name, shape, dt=F32):
            return ctx.enter_context(nc.sbuf_tensor(name, shape, dt))

        def sem(name):
            return ctx.enter_context(nc.semaphore(name))

        x = sb("x", [P, KT, T])
        h_base = nc.sbuf_base
        h_hi = sb("h_hi", [P, KT, T], F32R)
        h_lo = sb("h_lo", [P, KT, T], F32R)
        w_raw = [sb(f"w_raw{j}", [P, KT * P]) for j in range(SLOTS)]
        w_hi = [sb(f"w_hi{j}", [P, KT * P], F32R) for j in range(SLOTS)]
        w_lo = [sb(f"w_lo{j}", [P, KT * P], F32R) for j in range(SLOTS)]
        g_base = nc.sbuf_base
        g_hi = sb("g_hi", [P, RING_G, T], F32R)
        g_lo = sb("g_lo", [P, RING_G, T], F32R)
        sil_cond = sb("sil_cond", [P, KT * 2])
        cond = sb("cond", [P, KT, 4], F32R)
        mod = sb("mod", [P, 2, CHUNKS_MOD * 2])
        mod_b = sb("mod_b", [P, DEPTH, CHUNKS_MOD * 2])
        norms = sb("norms", [P, 2 * DEPTH + 1, KT * 2])
        mod_a = sb("mod_a", [P, KT * 2])
        norms_h = sb("norms_h", [P, 2])
        small = sb("small", [P, 32])
        warm = small[:, 20:32]
        ones_d = sb("ones_d", [P, P])
        ones_h = sb("ones_h", [P, P])
        ident = sb("ident", [P, P])
        unit = T * 4
        arena_base = nc.sbuf_base
        arena_size = 45 * 1024
        sb("arena", [P, arena_size // 4])
        U = T

        class Region:

            def __init__(self, name, spare=True):
                self.name, self.at, self.n = name, arena_base, 0
                self.spare = [g_base + 8 * unit, g_base + 9 * unit, g_base + 18 * unit, g_base + 19 * unit] if spare else []

            def __call__(self, what, elems, dt=F32):
                if self.spare and elems == U:
                    return nc.alloc_sbuf_tensor_at(f"{self.name}_{what}", [P, elems], dt, offset=self.spare.pop())
                a = nc.alloc_sbuf_tensor_at(f"{self.name}_{what}", [P, elems], dt, offset=self.at)
                self.at += elems * 4
                assert self.at <= arena_base + arena_size, (self.name, what, self.at - arena_base - arena_size)
                return a

        ffn = Region("ffn", spare=False)
        rstd = ffn("rstd", U)
        sq = [ffn("sq0", U), ffn("sq1", U)]
        hf = [ffn("hf0", U), ffn("hf1", U)]
        kept = ffn.at
        conv = ffn("conv", 2 * NPAIR * 10)
        acc_a, acc_v, sil = [[ffn(f"{what}{u}", U) for u in range(2)] for what in ("acc_a", "acc_v", "sil")]

        pool = Region("pool")
        pool.at = kept
        box_h = [pool(f"box_h{j}", ROWS * 80) for j in range(2)]
        box_v = [pool(f"box_v{j}", 24 * GRID_W) for j in range(2)]
        inv = pool("inv", 4 * T)
        pool_w = pool("pool_w", 4 * 2 * 256)
        box_m = pool("box_m", U)
        sg = pool("sg", KT * 2)
        pool_h = nc.alloc_sbuf_tensor_at("pool_h", [P, KT, T], F32, offset=h_base)
        pool_d = nc.alloc_sbuf_tensor_at("pool_d", [P, KT, T], F32, offset=h_base + KT * unit)

        hg = Region("hgrn")
        hg.at = kept
        q, f_f, f_b, v_t, v_tok, gate0, gate1 = [hg(n, U) for n in ("q", "f_f", "f_b", "v_t", "v_tok", "gate0", "gate1")]
        gates = [gate0, gate1]
        qf, qb, kf, kb, tot_f, tot_b = [hg(n, U) for n in ("qf", "qb", "kf", "kb", "tot_f", "tot_b")]
        k_sum, scores = hf
        masks = hg("masks", 8 * P)
        states = hg("states", 8 * P)
        st_out = hg("st_out", 2 * P)
        lb_in = hg("lb_in", 2 * DEPTH * KT)
        lb = hg("lb", 4 * KT)

        df = Region("diff")
        df.at = kept
        dq, dk, dv_t, dv_tok = [df(n, U) for n in ("q", "k", "v_t", "v_tok")]
        cos, sin = df("cos", N_SAMPLE), df("sin", N_SAMPLE)
        turn = df("turn", P)
        kc, vc = [[df(f"{n}{j}", PAST) for j in range(2)] for n in ("kc", "vc")]
        qr, kr = df("qr", U), df("kr", U)
        NK = N_SAMPLE + PAST
        prob = [df("prob0", NK), df("prob1", NK)]
        prob_t = df("prob_t", NK)
        o_sb = hf[0]
        lam_in = df("lam_in", 4 * 64)

        acc = [ctx.enter_context(nc.psum_tensor(f"acc{j}", [P, 1024], F32)) for j in range(SLOTS)]

        result = [a[:, OUT:OUT + T] for a in acc]

        cond_landed, bias_landed = sem("cond_landed"), sem("bias_landed")
        loaded = sem("loaded")
        raw_landed = [sem(f"raw_landed{j}") for j in range(SLOTS)]
        hi_done, lo_done, job_done, job_used = sem("hi_done"), sem("lo_done"), sem("job_done"), sem("job_used")
        dve_step, act_step = sem("dve_step"), sem("act_step")
        sq_done, sq_used = sem("sq_done"), sem("sq_used")
        sqrt_done, rstd_done = sem("sqrt_done"), sem("rstd_done")
        scaled, h_full, h_ready = sem("scaled"), sem("h_full"), sem("h_ready")
        x_ready = sem("x_ready")
        silu_cond_done = sem("silu_cond_done")
        mod_ready, mod_a_ready = sem("mod_ready"), sem("mod_a_ready")
        conv_landed = sem("conv_landed")
        center_done, silu_done, gated, g_rounded, g_ready = [
            sem(n) for n in ("center_done", "silu_done", "gated", "g_rounded", "g_ready")]
        mixer_landed = sem("mixer_landed")
        sig_done, v_turned, v_ready, level_ready, level_done, masked = [
            sem(n) for n in ("sig_done", "v_turned", "v_ready", "level_ready", "level_done", "masked")]
        kt_turned, kt_ready, ds_done, states_ready, o_done, st_ready, st_stored, s0_landed = [
            sem(n) for n in ("kt_turned", "kt_ready", "ds_done", "states_ready", "o_done", "st_ready", "st_stored", "s0_landed")]
        osq_done, o_moved, oms_done, osqrt_done, o_full, o_rounded, o_ready = [
            sem(n) for n in ("osq_done", "o_moved", "oms_done", "osqrt_done", "o_full", "o_rounded", "o_ready")]
        pool_ready, pool_done = sem("pool_ready"), sem("pool_done")
        cache_landed = [sem("cache_landed0"), sem("cache_landed1")]
        rot_done, qk_ready, sc_done, mx_ready, exp_done, w_ready, wt_done, wt_ready, kv_stored, lam_sem = [
            sem(n) for n in ("rot_done", "qk_ready", "sc_done", "mx_ready", "exp_done", "w_ready",
                             "wt_done", "wt_ready", "kv_stored", "lam_sem")]
        pv_done, o_copied = sem("pv_done"), sem("o_copied")
        lb_sem = sem("lb_sem")
        y_ready, y_stored = sem("y_ready"), sem("y_stored")

        first, first_t, n = {}, {}, 0
        for t, (what, layer, index, nk) in enumerate(PLAN):
            if what != "mod":
                first.setdefault((what, layer), n)
                first_t.setdefault((what, layer), t)
                n += 1
        for layer in range(DEPTH):
            first_t["up", layer] -= layer + 1 < DEPTH

        POOL_LAYERS = [layer for layer in range(DEPTH) if KINDS[layer] == 0]
        pools = {layer: i for i, layer in enumerate(POOL_LAYERS)}
        mixer_loads, at = {}, 0
        for layer in range(DEPTH):
            at += 16 * (3, 2, 4)[KINDS[layer]]
            mixer_loads[layer] = at
        plain_norms = {2 * layer for layer in POOL_LAYERS}
        split_norms = [sum(1 for m in range(k) if m not in plain_norms) for k in range(2 * DEPTH + 2)]
        N_CONST = 6

        def x_updates(k):
            if k % 2 and KINDS[k // 2] == 0:
                return x_ready, KT * pools[k // 2]
            if k % 2:
                return job_used, first[("hgrn_out" if KINDS[k // 2] == 1 else "diff_out", k // 2)]
            layer = k // 2
            return job_used, first[("up", layer - 1)] + 2 * NPAIR + KT * (sum(what == "down" for what, *_ in SEGMENTS) - 1)

        def late_mods(layer):
            return first_t["up", layer] - CHUNKS_MOD // 2

        wall, out_y = dram["wall"], dram["y"]

        def segments(layer):
            n, t, k = first["up", layer], first_t["up", layer], (layer + 1) * CHUNKS_MOD
            for what, p0, count in SEGMENTS:
                mods = has_mods(layer, what, p0, count)
                yield what, p0, count, n, t, mods, k
                jobs = 2 * count if what == "up" else KT
                n, t = n + jobs, t + jobs
                if mods:
                    t, k = t + (jobs if what == "up" else 4), k + jobs

        def loop(eng, iters, body):
            if iters == 1:
                body(0)
            else:
                with eng.Fori(0, iters) as i:
                    body(i)

        block = ctx.enter_context(nc.Block())

        @block.sync
        def _(sp):
            sp.dma_start(sil_cond[:], dram["cond"]).then_inc(cond_landed, 16)
            for j in range(SLOTS):
                sp.dma_start(w_raw[j][:], wall[j]).then_inc(raw_landed[j], 16)
            sp.dma_start(mod_b[:], dram["ada_b"]).then_inc(bias_landed, 16)
            for dst, src in ((x[:], dram["x"]), (norms[:], dram["norms"]), (ones_d[:], dram["ones_d"]),
                             (ones_h[:], dram["ones_h"]), (ident[:], dram["ident"]), (norms_h[:], dram["norms_h"])):
                sp.dma_start(dst, src).then_inc(loaded, 16)
            with sp.Fori(0, NTILES // SLOTS - 1) as i:
                for j in range(SLOTS):
                    sp.wait_ge(lo_done, i * SLOTS + (j + 1))
                    sp.dma_start(w_raw[j][:], wall[i * SLOTS + (SLOTS + j)]).then_inc(raw_landed[j], 16)
            for kt in range(KT):
                sp.wait_ge(y_ready, kt + 1)
                sp.dma_start(out_y[:, kt], pool_h[:, kt, :]).then_inc(y_stored, 16)
            sp.wait_ge(y_stored, 16 * KT)

        @block.gpsimd
        def _(pl):
            with pl.Fori(0, NTILES // SLOTS) as i:
                for j in range(SLOTS):
                    pl.wait_ge(hi_done, i * SLOTS + (j + 1))
                    nc.gpsimd.tensor_tensor(w_lo[j][:], w_raw[j][:], w_hi[j][:].bitcast(F32),
                                            ALU.subtract).then_inc(lo_done, 1)

        @block.tensor
        def _(pe):
            def product(out, terms, skip=False):
                for k, (a, b) in enumerate(terms):
                    mm = nc.tensor.matmul(out, a, b, start=(k == 0), stop=(k == len(terms) - 1), skip_group_check=skip)
                return mm

            def job(n, t, ps, j, nk, hi, lo, h_at=None):
                pe.wait_ge(lo_done, t + 1)
                if not (isinstance(n, int) and n < SLOTS):
                    pe.wait_ge(job_used, n - (SLOTS - 1))
                for c0, c1 in HALVES:
                    for k in range(nk):
                        if h_at is not None and c0 == 0:
                            pe.wait_ge(h_ready, h_at + k + 1)
                        wk = slice(k * P, (k + 1) * P)
                        terms = [(w_hi[j][:, wk], hi(k)[:, c0:c1]), (w_hi[j][:, wk], lo(k)[:, c0:c1]),
                                 (w_lo[j][:, wk], hi(k)[:, c0:c1])]
                        for u, (w, h) in enumerate(terms):
                            mm = nc.tensor.matmul(result[ps][:, c0:c1], w, h, start=(k == 0 and u == 0),
                                                  stop=(k == nk - 1 and u == 2))
                mm.then_inc(job_done, 1)

            def job_steps(n0, t0, a, b, depth, h_at=None):
                for step in range(a, b):
                    n, t, k = n0 + step // KT, t0 + step // KT, step % KT
                    j, ps = t % SLOTS, result[n % depth]
                    if k == 0:
                        pe.wait_ge(lo_done, t + 1)
                        pe.wait_ge(job_used, n + 1 - depth)
                    if h_at is not None and step < KT:
                        pe.wait_ge(h_ready, h_at + k + 1)
                    wk = slice(k * P, (k + 1) * P)
                    for c0, c1 in HALVES:
                        for u, (w, h) in enumerate(((w_hi, h_hi), (w_hi, h_lo), (w_lo, h_hi))):
                            mm = nc.tensor.matmul(ps[:, c0:c1], w[j][:, wk], h[:, k, c0:c1], start=(k == 0 and u == 0),
                                                  stop=(k == KT - 1 and u == 2), skip_group_check=True)
                    if k == KT - 1:
                        mm.then_inc(job_done, 1)

            def mod_tile(t, j, ps, at=MOD_AT):
                pe.wait_ge(lo_done, t + 1)
                mm = product(acc[ps][:, at:at + 4], [(w[j][:, kt * P:(kt + 1) * P], cond[:, kt, :])
                                                             for kt in range(KT) for w in (w_hi, w_lo)])
                mm.then_inc(job_done, 1)

            def mod_tiles(i):
                for c in range(SLOTS):
                    if not (isinstance(i, int) and i == 0):
                        pe.wait_ge(mod_ready, i * SLOTS + (c - SLOTS + 1))
                    mod_tile(i * SLOTS + c, c, c)

            def norm(k, n_used):
                if n_used:
                    pe.wait_ge(job_used, n_used)
                for kt in range(KT):
                    pe.wait_ge(sq_done, KT * k + kt + 1)
                    for c0, c1 in HALVES:
                        mm = nc.tensor.matmul(result[0][:, c0:c1], ones_d[:], sq[kt % 2][:, c0:c1],
                                              start=(kt == 0), stop=(kt == KT - 1))
                    mm.then_inc(sq_used, 1)

            def head_norm(h0, ps):
                pe.wait_ge(osq_done, h0 + 1)
                for c0, c1, _ in RANGES:
                    mm = nc.tensor.matmul(ps[:, c0:c1], ones_h[:], sq[0][:, c0:c1], start=True, stop=True)
                mm.then_inc(oms_done, 1)

            def tokens(dst, src, tiles):
                for c in range(tiles):
                    mm = nc.tensor.transpose(dst[:, c * P:(c + 1) * P], src[:, c * P:(c + 1) * P], ident[:])
                return mm

            pe.wait_ge(silu_cond_done, 2)
            mod_tiles(0)
            with pe.Fori(1, EARLY // SLOTS) as i:
                mod_tiles(i)
            pe.wait_ge(mod_ready, EARLY)
            pe.wait_ge(loaded, 16 * N_CONST)
            hd = 0
            for layer, kind in enumerate(KINDS):
                n_used = first.get(("up", layer), 0) if kind == 0 else first[("hgrn_in" if kind == 1 else "diff_in", layer)]
                norm(2 * layer, n_used)
                if kind == 0:
                    pe.wait_ge(sqrt_done, 2 * layer + 1)
                    if layer == 0:
                        for i in range(EARLY // SLOTS, CHUNKS_MOD // 8):
                            mod_tiles(i)
                    for g in range(4):
                        if g < 3:
                            for group in (2 * g, 2 * g + 1):
                                pe.wait_ge(mod_ready, layer * CHUNKS_MOD + CHUNKS_MOD // 2 + SLOTS * max(0, group - 1))
                                for c in range(SLOTS):
                                    mod_tile(late_mods(layer) + SLOTS * group + c, c, 0, LATE_AT[group % 2] + 4 * c)
                        if g == 0:
                            pe.wait_ge(mixer_landed, mixer_loads[layer])
                        pe.wait_ge(pool_ready, KT * pools[layer] + 2 * g + 2)
                        for o in range(2):
                            u = 2 * g + o
                            j = 1 + u % 3
                            if u >= 3:
                                pe.wait_ge(x_ready, KT * pools[layer] + u - 2)
                            for c0, c1 in HALVES:
                                mm = product(result[j][:, c0:c1],
                                             [(pool_w[:, ((g * 2 + i) * 2 + o) * P:((g * 2 + i) * 2 + o + 1) * P],
                                               pool_d[:, 2 * g + i, c0:c1]) for i in range(2)])
                            mm.then_inc(pool_done, 1)
                elif kind == 1:
                    pe.wait_ge(mixer_landed, mixer_loads[layer])
                    n0, t0 = first[("hgrn_in", layer)], first_t[("hgrn_in", layer)]
                    job_steps(n0, t0, 0, 5 * KT, 2, KT * split_norms[2 * layer])
                    for h in range(HEADS):
                        def next_steps(point):
                            if h + 1 < HEADS:
                                job_steps(n0 + 5 * (h + 1), t0 + 5 * (h + 1), 4 * point, 4 * point + 4, 2)

                        pe.wait_ge(job_used, n0 + 5 * h + 4)
                        if h:
                            pe.wait_ge(osqrt_done, hd)
                        tokens(acc[2], v_t, 5).then_inc(v_turned, 1)
                        for level in range(LEVELS + 1):
                            next_steps(level)
                            s = 2 + (level + 1) % 2
                            pe.wait_ge(level_ready, h * (LEVELS + 2) + level + 1)
                            if level == 0 and h:
                                pe.wait_ge(o_moved, h)
                            if level == 1:
                                pe.wait_ge(v_ready, h + 1)
                            if level >= 2:
                                pe.wait_ge(masked, h * (LEVELS + 1) + level - 1)
                            for c in range(5):
                                at = slice(c * P, (c + 1) * P)
                                if level == 0:
                                    mm = nc.tensor.matmul(acc[s][:, at], k_sum[:, at], q[:, at], start=True, stop=True)
                                    continue
                                m = 1 << (level - 1)

                                def halves(t, half):
                                    return t[:, at].rearrange("p (b h m) -> p b h m", h=2, m=m)[:, :, half, :]

                                nc.tensor.matmul(halves(acc[s], 1), kf[:, at], halves(qf, 1), start=True, stop=True)
                                mm = nc.tensor.matmul(halves(acc[s], 0), kb[:, at], halves(qb, 0), start=True, stop=True)
                            mm.then_inc(level_done, 1)
                        next_steps(8)
                        pe.wait_ge(level_ready, (h + 1) * (LEVELS + 2))
                        pe.wait_ge(masked, (h + 1) * (LEVELS + 1))
                        tokens(acc[2], kf, 5)
                        tokens(acc[3], kb, 5).then_inc(kt_turned, 1)
                        next_steps(9)
                        pe.wait_ge(kt_ready, h + 1)
                        for u, (keys, c) in enumerate([(kf, 0), (kf, 1), (kf, 2), (kf, 4),
                                                       (kb, 3), (kb, 2), (kb, 1), (kb, 4)]):
                            at = slice(c * P, (c + 1) * P)
                            mm = nc.tensor.matmul(acc[2][:, u * P:(u + 1) * P], keys[:, at], v_tok[:, at],
                                                  start=True, stop=True)
                        mm.then_inc(ds_done, 1)
                        pe.wait_ge(states_ready, h + 1)
                        for c in range(5):
                            at = slice(c * P, (c + 1) * P)
                            terms = [(v_tok[:, at], scores[:, at])]
                            if c < 4:
                                terms += [(states[:, c * P:(c + 1) * P], qf[:, at]),
                                          (states[:, (4 + c) * P:(5 + c) * P], qb[:, at])]
                            mm = product(acc[3][:, at], terms)
                        mm.then_inc(o_done, 1)
                        head_norm(hd, acc[2])
                        hd += 1
                    pe.wait_ge(o_ready, hd)
                    n0, t0 = first[("hgrn_out", layer)], first_t[("hgrn_out", layer)]
                    for o in range(KT):
                        job(n0 + o, t0 + o, (n0 + o) % SLOTS, (t0 + o) % SLOTS, KT, lambda k: g_hi[:, k, :], lambda k: g_lo[:, k, :])
                else:
                    pe.wait_ge(mixer_landed, mixer_loads[layer])
                    n0, t0 = first[("diff_in", layer)], first_t[("diff_in", layer)]
                    qt = 0
                    job_steps(n0, t0, 0, 3 * KT, 1, KT * split_norms[2 * layer])

                    def scores_of(tile, kcache):
                        at = slice(tile * P, (tile + 1) * P)
                        for c in range(2):
                            rows = slice(64 * c, 64 * c + 64)
                            if tile < 4:
                                nc.tensor.matmul(acc[1 + c][:, 0:512], qr[rows, at], kr[rows, 0:512], start=True, stop=True)
                                mm = nc.tensor.matmul(acc[1 + c][:, 512:768], qr[rows, at], kcache[rows, :], start=True, stop=True)
                            else:
                                mm = nc.tensor.matmul(acc[1 + c][:, 0:P], qr[rows, at], kr[rows, at], start=True, stop=True)
                        mm.then_inc(sc_done, 1)

                    for h in range(HEADS):
                        pe.wait_ge(job_used, n0 + 3 * h + 3)
                        if h:
                            pe.wait_ge(exp_done, 2 * qt)
                        tokens(acc[2], dv_t, 5).then_inc(v_turned, 1)
                        nc.tensor.matmul(acc[1][:, 0:512], turn[:], dq[:, 0:512], start=True, stop=True)
                        nc.tensor.matmul(acc[1][:, 512:1024], turn[:], dk[:, 0:512], start=True, stop=True).then_inc(rot_done, 1)
                        if h:
                            pe.wait_ge(o_copied, qt)
                            head_norm(hd, acc[3])
                            hd += 1
                        pe.wait_ge(qk_ready, h + 1)
                        pe.wait_ge(v_ready, HEADS + h + 1)
                        pe.wait_ge(cache_landed[h % 2], 32 * (h // 2 + 1))
                        kcache, vcache = kc[h % 2], vc[h % 2]
                        scores_of(0, kcache)
                        for tile in range(5):
                            if tile < 4:
                                pe.wait_ge(exp_done, 2 * qt + 2)
                                scores_of(tile + 1, kcache)
                            pe.wait_ge(w_ready, qt + 1)
                            if qt:
                                pe.wait_ge(o_copied, qt)
                            if tile == 0 and h:
                                pe.wait_ge(osqrt_done, hd)
                            nkt = 6 if tile < 4 else 1
                            tokens(acc[3], prob[0], nkt).then_inc(wt_done, 1)
                            if h + 1 < HEADS:
                                job_steps(n0 + 3 * (h + 1), t0 + 3 * (h + 1), 5 * tile, min(5 * tile + 5, 3 * KT), 1)
                            pe.wait_ge(wt_ready, qt + 1)
                            terms = []
                            for k in range(nkt):
                                if tile == 4:
                                    vals = dv_tok[:, 512:640]
                                elif k < 4:
                                    vals = dv_tok[:, k * P:(k + 1) * P]
                                else:
                                    vals = vcache[:, (k - 4) * P:(k - 3) * P]
                                terms.append((vals, prob_t[:, k * P:(k + 1) * P]))
                            product(acc[3][:, 768:896], terms).then_inc(pv_done, 1)
                            qt += 1
                    pe.wait_ge(o_copied, qt)
                    head_norm(hd, acc[3])
                    hd += 1
                    pe.wait_ge(o_ready, hd)
                    n0, t0 = first[("diff_out", layer)], first_t[("diff_out", layer)]
                    for o in range(KT):
                        job(n0 + o, t0 + o, (n0 + o) % SLOTS, (t0 + o) % SLOTS, KT, lambda k: g_hi[:, k, :], lambda k: g_lo[:, k, :])
                norm(2 * layer + 1, first[("up", layer)])
                g_at = NPAIR * layer
                for what, p0, count, n, t, mods, k in segments(layer):
                    def body(i, what=what, p0=p0, count=count, n=n, t=t, mods=mods, begins=False):
                        per = 1 + mods
                        for j in range(SLOTS):
                            tile = i * (SLOTS * per) + (t + per * j)
                            if mods:
                                if begins and j == 0:
                                    pe.wait_ge(sqrt_done, 2 * layer + 2)
                                if not (isinstance(i, int) and n == 0):
                                    pe.wait_ge(job_used, i * SLOTS + (n + j - (SLOTS - 1)))
                                mod_tile(tile, 2 * j % SLOTS, j)
                            if what == "up":
                                nk, hi, lo = KT, lambda k: h_hi[:, k, :], lambda k: h_lo[:, k, :]
                            else:
                                nk, hi, lo = count, lambda k: g_hi[:, (p0 + k) % RING_G, :], lambda k: g_lo[:, (p0 + k) % RING_G, :]
                            job(i * SLOTS + (n + j), tile + (per - 1), j, (per * j + per - 1) % SLOTS, nk, hi, lo,
                                KT * split_norms[2 * layer + 1] if begins and j == 0 else None)

                    if what == "up" and p0 == 0:
                        body(0, begins=True)
                        with pe.Fori(1, count // 2) as i:
                            body(i)
                    elif what == "up":
                        loop(pe, count // 2, body)
                    else:
                        pe.wait_ge(g_ready, g_at + p0 + count)
                        if mods:
                            body(0)
                            body(0, n=n + SLOTS, t=t + 2 * SLOTS, mods=False)
                        else:
                            loop(pe, 2, body)
            norm(2 * DEPTH, NJOBS)

        @block.scalar
        def _(act):
            steps = [0]

            def link(ins):
                ins.then_inc(act_step, 1)
                steps[0] += 1
                act.wait_ge(act_step, steps[0])

            def high(t, j):
                act.wait_ge(raw_landed[j], (t - j) * 4 + 16)
                if not (isinstance(t, int) and t < SLOTS):
                    act.wait_ge(job_done, t - (SLOTS - 1))
                nc.scalar.activation(w_hi[j][:], w_raw[j][:], ACT.Copy).then_inc(hi_done, 1)

            def ahead(t, j):
                if isinstance(t, int) and t + 3 >= NTILES:
                    return
                high(t + 3, (j + 3) % SLOTS)

            def ahead4(i, t):
                for j in range(SLOTS):
                    ahead(i * SLOTS + (t + j), j)

            def mixer_constants(layer):
                what = {0: ((inv, dram["inv"]), (pool_w, dram["pool_w"][pools.get(layer, 0)]),
                            (sg, dram["pool_scale"][pools.get(layer, 0)])),
                        1: ((masks, dram["masks"]), (lb_in, dram["lb"])),
                        2: ((cos, dram["cos"]), (sin, dram["sin"]), (turn, dram["turn"]), (lam_in, dram["lam"]))}[KINDS[layer]]
                for dst, src in what:
                    act.dma_start(dst[:], src).then_inc(mixer_landed, 16)

            def norm(k, plain):
                for kt in range(KT):
                    if k:
                        updated, before = x_updates(k)
                        if kt == 0:
                            act.wait_ge(h_full, KT * k)
                            if split_norms[k]:
                                act.wait_ge(h_ready, KT * split_norms[k])
                            nc.scalar.activation(warm[:, k:k + 1], ones_d[:, 0:1], ACT.Sqrt)
                        act.wait_ge(updated, before + kt + 1)
                    if KT * k + kt >= 2:
                        act.wait_ge(sq_used, KT * k + kt - 1)
                    nc.scalar.activation(sq[kt % 2][:], x[:, kt, :], ACT.Square).then_inc(sq_done, 1)
                act.wait_ge(sq_used, KT * (k + 1))
                if k % 2 == 0 and k < 2 * DEPTH:
                    mixer_constants(k // 2)
                nc.scalar.activation(rstd[:], result[0], ACT.Sqrt, bias=EPS).then_inc(sqrt_done, 1)
                if k == 2 * DEPTH:
                    return
                layer, c0_b = k // 2, 24 * (k % 2)
                for kt in range(KT):
                    act.wait_ge(scaled, KT * k + kt + 1)
                    dst = pool_h[:, kt, :] if plain else h_hi[:, kt, :]
                    for c0, c1, row in RANGES:
                        b = 2 * (c0_b + kt) + row
                        ins = nc.scalar.activation(dst[:, c0:c1], sq[kt % 2][:, c0:c1], ACT.Identity,
                                                   bias=mod[:, layer % 2, b:b + 1])
                    ins.then_inc(h_full, 1)
                    if k == 0 and kt < SLOTS:
                        ahead(EARLY + kt, kt)

            def head_norm(h0, src, ps, last, moved=False):
                act.wait_ge(*last)
                if h0:
                    act.wait_ge(o_ready, h0)
                nc.scalar.activation(sq[0][:], src[:, 0:T], ACT.Square).then_inc(osq_done, 1)
                if moved:
                    nc.scalar.activation(sq[1][:], src[:, 0:T], ACT.Copy).then_inc(o_moved, 1)
                act.wait_ge(oms_done, h0 + 1)
                nc.scalar.activation(rstd[:], ps[:, 0:T], ACT.Sqrt, bias=EPS).then_inc(osqrt_done, 1)

            def high_o(h0, h):
                act.wait_ge(o_full, h0 + 1)
                nc.scalar.activation(g_hi[:, h, :], sq[1][:], ACT.Copy).then_inc(o_rounded, 1)

            act.wait_ge(cond_landed, 16)
            nc.scalar.activation(sq[0][:, 0:2 * KT], sil_cond[:], ACT.Sigmoid).then_inc(act_step, 1)
            for j in range(3):
                high(j, j)
            act.wait_ge(silu_cond_done, 1)
            nc.scalar.activation(cond[:, :, 0:2], sil_cond[:].rearrange("p (k r) -> p k r", r=2), ACT.Copy).then_inc(act_step, 1)
            ahead4(0, 0)
            with act.Fori(1, EARLY // SLOTS) as i:
                ahead4(i, 0)
            act.wait_ge(loaded, 16 * N_CONST)
            hd = 0
            for layer, kind in enumerate(KINDS):
                norm(2 * layer, kind == 0)
                if kind == 0:
                    if layer == 0:
                        ahead4(0, EARLY + SLOTS)
                    with act.Fori(0, CHUNKS_MOD // 8) as i:
                        ahead4(i, late_mods(layer))
                if kind == 1:
                    n0, t0 = first[("hgrn_in", layer)], first_t[("hgrn_in", layer)]
                    act.wait_ge(lb_sem, 1)
                    nc.scalar.activation(lb_in[:], lb_in[:], ACT.Exp).then_inc(lb_sem, 1)
                    def project_head(h):
                        for part in range(5):
                            n, t = n0 + 5 * h + part, t0 + 5 * h + part
                            ahead(t, t % SLOTS)
                            if part in (1, 2, 4):
                                act.wait_ge(job_done, t + 1)
                                dst = {1: f_f, 2: f_b, 4: gates[h % 2]}[part]
                                if part == 1 and h:
                                    act.wait_ge(level_ready, (h - 1) * (LEVELS + 2) + 3)
                                nc.scalar.activation(dst[:], result[n % 2], ACT.Sigmoid).then_inc(sig_done, 1)

                    project_head(0)
                    for h in range(HEADS):
                        act.dma_start(states[:, 0:P], dram["s0"][0, h]).then_inc(s0_landed, 16)
                        act.dma_start(states[:, 7 * P:8 * P], dram["s0"][1, h]).then_inc(s0_landed, 16)
                        if h + 1 < HEADS:
                            project_head(h + 1)
                        act.wait_ge(st_ready, h + 1)
                        act.dma_start(dram["new_state"][h], st_out[:]).then_inc(st_stored, 16)
                        head_norm(hd, acc[3], acc[2], (o_done, h + 1), moved=True)
                        high_o(hd, h)
                        hd += 1
                    t0 = first_t[("hgrn_out", layer)]
                    for o in range(KT):
                        ahead(t0 + o, (t0 + o) % SLOTS)
                elif kind == 2:
                    act.wait_ge(lam_sem, 1)
                    nc.scalar.activation(small[:, 2:4], small[:, 0:2], ACT.Exp).then_inc(lam_sem, 1)
                    n0, t0 = first[("diff_in", layer)], first_t[("diff_in", layer)]
                    qt = 0
                    for h in range(2):
                        act.dma_start(kc[h][:], dram["cache_k"][h]).then_inc(cache_landed[h], 16)
                        act.dma_start(vc[h][:], dram["cache_v"][h]).then_inc(cache_landed[h], 16)
                    for part in range(3):
                        ahead(t0 + part, (t0 + part) % SLOTS)
                    for h in range(HEADS):
                        act.wait_ge(v_ready, HEADS + h + 1)
                        act.wait_ge(qk_ready, h + 1)
                        act.dma_start(dram["new_k"][h], kr[:, N_SAMPLE:T]).then_inc(kv_stored, 16)
                        act.dma_start(dram["new_v"][h], dv_tok[:, N_SAMPLE:T]).then_inc(kv_stored, 16)

                        def exps(tile):
                            nk = NK if tile < 4 else P
                            act.wait_ge(mx_ready, 5 * h + tile + 1)
                            for c in range(2):
                                nc.scalar.activation(prob[c][:, 0:nk], acc[1 + c][:, 0:nk], ACT.Exp,
                                                     bias=small[:, 10 + c:11 + c], scale=SCALE,
                                                     accum_out=small[:, 12 + c:13 + c]).then_inc(exp_done, 1)

                        if h:
                            high_o(hd, h - 1)
                            hd += 1
                        exps(0)
                        for tile in range(5):
                            nk = NK if tile < 4 else P
                            if h + 1 < HEADS and tile % 2 == 0:
                                t = t0 + 3 * (h + 1) + tile // 2
                                ahead(t, t % SLOTS)
                            act.wait_ge(wt_done, qt + 1)
                            nc.scalar.activation(prob_t[:, 0:nk], acc[3][:, 0:nk], ACT.Copy).then_inc(wt_ready, 1)
                            if tile < 4:
                                exps(tile + 1)
                            qt += 1
                        head_norm(hd, o_sb, acc[3], (o_copied, qt))
                        if h + 2 < HEADS:
                            act.dma_start(kc[h % 2][:], dram["cache_k"][h + 2]).then_inc(cache_landed[h % 2], 16)
                            act.dma_start(vc[h % 2][:], dram["cache_v"][h + 2]).then_inc(cache_landed[h % 2], 16)
                    high_o(hd, HEADS - 1)
                    hd += 1
                    t0 = first_t[("diff_out", layer)]
                    for o in range(KT):
                        ahead(t0 + o, (t0 + o) % SLOTS)
                norm(2 * layer + 1, False)
                act.dma_start(conv[:], dram["conv"][layer]).then_inc(conv_landed, 16)
                act.wait_ge(conv_landed, 16 * (layer + 1))
                g_at = NPAIR * layer
                for what, p0, count, n, t, mods, k in segments(layer):
                    per = 1 + mods
                    if what == "up":
                        def finish(d, side, slot):
                            if not (isinstance(d, int) and d < 2):
                                act.wait_ge(g_ready, d - 1)
                            nc.scalar.activation(sil[side][:], acc_a[side][:], ACT.Silu).then_inc(silu_done, 1)
                            act.wait_ge(gated, d + 1)
                            nc.scalar.activation(g_hi[:, slot, :], sil[side][:], ACT.Copy).then_inc(g_rounded, 1)

                        def body(i, fresh, n=n, t=t, p0=p0, per=per):
                            for pair in range(2):
                                p = i * 2 + (p0 + pair)
                                done = i * 2 + (g_at + p0 + pair)
                                for side in range(2):
                                    j = 2 * pair + side
                                    for u in range(per * j, per * j + per):
                                        tile = i * (SLOTS * per) + (t + u)
                                        ahead(tile, u % SLOTS)
                                    act.wait_ge(job_done, tile + 1)
                                    if not (isinstance(done, int) and done < 2):
                                        act.wait_ge(gated, done - 1)
                                    dst = (acc_a, acc_v)[side][pair]
                                    c10 = p * 20 + side * 10
                                    nc.scalar.activation(dst[:], result[j], ACT.Identity,
                                                         bias=conv[:, bass.ds(c10 + 9, 1)],
                                                         scale=conv[:, bass.ds(c10 + 4, 1)]).then_inc(center_done, 1)
                                if pair or not fresh:
                                    act.wait_ge(job_used, i * SLOTS + (n + 2 * pair - 1))
                                    slot = (p0 - 1) % RING_G if isinstance(i, int) and i + pair == 0 else \
                                        i * 2 + (p0 % RING_G + pair - 1)
                                    finish(done - 1, 1 - pair, slot)
                        fresh = p0 != 20
                        body(0, fresh)
                        start = 1
                        if layer == 0 and p0 == 0:
                            body(1, False)
                            start = 2
                        if count // 2 > start:
                            with act.Fori(start, count // 2) as i:
                                body(i, False)
                        if p0 != 18:
                            act.wait_ge(job_used, n + 2 * count - 1)
                            finish(g_at + p0 + count - 1, 1, (p0 + count - 1) % RING_G)
                    elif t + KT + 3 > NTILES:
                        for u in range(KT):
                            ahead(t + u, u % SLOTS)
                    else:
                        with act.Fori(0, 3 if mods else 2) as i:
                            ahead4(i, t)
            norm(2 * DEPTH, True)
            act.wait_ge(st_stored, 16 * HEADS)
            act.wait_ge(kv_stored, 32 * HEADS)

        @block.vector
        def _(dve):
            V = nc.vector
            steps = [0]

            def link(ins):
                ins.then_inc(dve_step, 1)
                steps[0] = steps[0] + 1
                dve.wait_ge(dve_step, steps[0])

            def linked_loop(iters, per, body, start=0):
                base = steps[0]
                if iters - start == 1:
                    body(start)
                    assert steps[0] == base + per
                    return
                with dve.Fori(start, iters) as i:
                    steps[0] = i * per + (base - start * per)
                    body(i)
                steps[0] = base + per * (iters - start)

            def mod_tile(k, ps, layer, at=MOD_AT):
                c = (k - layer * CHUNKS_MOD) * 2
                out = mod[:, layer % 2, bass.ds(c, 2)]
                link(V.tensor_tensor(out, acc[ps][:, at:at + 2], mod_b[:, layer, bass.ds(c, 2)], ALU.add))
                V.tensor_tensor(out, acc[ps][:, at + 2:at + 4], out, ALU.add).then_inc(mod_ready, 1)

            def norm(k, plain):
                layer = k // 2
                if k < 2 * DEPTH:
                    dve.wait_ge(mod_ready, (layer + 1) * CHUNKS_MOD - (CHUNKS_MOD // 2 if plain else 0) if k else EARLY)
                    s0 = 2 * (24 * (k % 2) + 8)
                    V.scalar_tensor_tensor(out=mod_a[:], in0=mod[:, layer % 2, s0:s0 + 2 * KT], scalar=1.0,
                                           in1=norms[:, k, :], op0=ALU.add, op1=ALU.mult).then_inc(mod_a_ready, 1)
                    dve.wait_ge(mod_a_ready, k + 1)
                dve.wait_ge(sqrt_done, k + 1)
                V.reciprocal(rstd[:], rstd[:]).then_inc(rstd_done, 1)
                dve.wait_ge(rstd_done, k + 1)
                for kt in range(KT):
                    if k == 2 * DEPTH:
                        V.scalar_tensor_tensor(out=pool_h[:, kt, :], in0=x[:, kt, :], scalar=norms[:, k, 2 * kt:2 * kt + 1],
                                               in1=rstd[:], op0=ALU.mult, op1=ALU.mult).then_inc(y_ready, 1)
                        continue
                    if kt >= 2 and plain:
                        dve.wait_ge(h_full, KT * k + kt - 1)
                    elif kt >= 2:
                        dve.wait_ge(h_ready, KT * split_norms[k] + kt - 1)
                    for c0, c1, row in RANGES:
                        ins = V.scalar_tensor_tensor(out=sq[kt % 2][:, c0:c1], in0=x[:, kt, c0:c1],
                                                     scalar=mod_a[:, 2 * kt + row:2 * kt + row + 1],
                                                     in1=rstd[:, c0:c1], op0=ALU.mult, op1=ALU.mult)
                    ins.then_inc(scaled, 1)
                    if not plain and kt >= 1:
                        low_h(k, kt - 1)
                if k < 2 * DEPTH and not plain:
                    low_h(k, KT - 1)

            def low_h(k, kt):
                dve.wait_ge(h_full, KT * k + kt + 1)
                layer, c0_b = k // 2, 24 * (k % 2)
                for c0, c1, row in RANGES:
                    b = 2 * (c0_b + kt) + row
                    ins = V.scalar_tensor_tensor(out=h_lo[:, kt, c0:c1], in0=sq[kt % 2][:, c0:c1],
                                                 scalar=mod[:, layer % 2, b:b + 1], in1=h_hi[:, kt, c0:c1].bitcast(F32),
                                                 op0=ALU.add, op1=ALU.subtract)
                ins.then_inc(h_ready, 1)

            def add_x(o, src, scalars, at):
                for c0, c1, row in RANGES:
                    ins = V.scalar_tensor_tensor(out=x[:, o, c0:c1], in0=src[:, c0:c1],
                                                 scalar=scalars[:, bass.ds(at + row, 1)],
                                                 in1=x[:, o, c0:c1], op0=ALU.mult, op1=ALU.add)
                return ins

            def project(n, t, layer):
                for o in range(KT):
                    dve.wait_ge(job_done, t + o + 1)
                    add_x(o, result[(n + o) % SLOTS], mod[:, layer % 2, :], 2 * (16 + o)).then_inc(job_used, 1)

            def head_norm(h0, src, gain, gated_by):
                dve.wait_ge(osqrt_done, h0 + 1)
                link(V.reciprocal(rstd[:], rstd[:]))
                link(V.tensor_tensor(sq[1][:], src[:, 0:T], rstd[:], ALU.mult))
                if gated_by is not None:
                    V.scalar_tensor_tensor(out=sq[1][:], in0=sq[1][:], scalar=gain, in1=gated_by[:],
                                           op0=ALU.mult, op1=ALU.mult).then_inc(o_full, 1)
                else:
                    V.tensor_scalar(sq[1][:], sq[1][:], gain, None, ALU.mult).then_inc(o_full, 1)

            def low_o(h0, h):
                dve.wait_ge(o_rounded, h0 + 1)
                V.tensor_tensor(g_lo[:, h, :], sq[1][:], g_hi[:, h, :].bitcast(F32), ALU.subtract).then_inc(o_ready, 1)

            def lower_bounds(layer):
                v = lb_in[:].rearrange("p (d l k) -> p d l k", d=2, l=DEPTH)
                by_layer = [v[:, :, l, :] for l in range(DEPTH)]
                top = lb[:, 0:2 * KT].rearrange("p (d k) -> p d k", d=2)
                rest = lb[:, 2 * KT:4 * KT].rearrange("p (d k) -> p d k", d=2)
                link(V.tensor_tensor(top, by_layer[0], by_layer[1], ALU.max))
                for l in range(2, DEPTH):
                    link(V.tensor_tensor(top, top, by_layer[l], ALU.max))
                for l in range(DEPTH):
                    ins = V.tensor_tensor(by_layer[l], by_layer[l], top, ALU.subtract)
                ins.then_inc(lb_sem, 1)
                dve.wait_ge(lb_sem, 2)
                link(V.tensor_tensor(rest, by_layer[0], by_layer[1], ALU.add))
                for l in range(2, DEPTH):
                    link(V.tensor_tensor(rest, rest, by_layer[l], ALU.add))
                link(V.reciprocal(rest, rest))
                for l in range(2, layer + 1):
                    link(V.tensor_tensor(by_layer[1], by_layer[1], by_layer[l], ALU.add))
                link(V.tensor_tensor(top, by_layer[1], rest, ALU.mult))
                link(V.tensor_scalar(lb[:, 2 * KT:4 * KT], lb[:, 0:2 * KT], -1.0, 1.0, ALU.mult, ALU.add))

            link(V.memset(small[:, 0:20], 0.0))
            dve.wait_ge(act_step, 1)
            V.tensor_tensor(sil_cond[:], sil_cond[:], sq[0][:, 0:2 * KT], ALU.mult).then_inc(silu_cond_done, 1)
            dve.wait_ge(act_step, 2)
            V.tensor_tensor(cond[:, :, 2:4], sil_cond[:].rearrange("p (k r) -> p k r", r=2), cond[:, :, 0:2].bitcast(F32),
                            ALU.subtract).then_inc(silu_cond_done, 1)

            def mod_tiles(i):
                for c in range(SLOTS):
                    dve.wait_ge(job_done, i * SLOTS + (c + 1))
                    mod_tile(i * SLOTS + c, c, 0)
            dve.wait_ge(bias_landed, 16)
            linked_loop(EARLY // SLOTS, SLOTS, mod_tiles)
            dve.wait_ge(loaded, 16 * N_CONST)
            hd = 0
            for layer, kind in enumerate(KINDS):
                norm(2 * layer, kind == 0)
                if kind == 0:
                    if layer == 0:
                        mod_tiles(EARLY // SLOTS)
                    dve.wait_ge(mixer_landed, mixer_loads[layer])
                    for b in box_v:
                        link(V.memset(b[:], 0.0))
                    for kt in range(KT):
                        g = kt // 2
                        w = POOL_WINDOWS[g]
                        dve.wait_ge(h_full, KT * 2 * layer + kt + 1)
                        H = [b[:].rearrange("p (r c) -> p r c", c=80) for b in box_h]
                        B = [b[:].rearrange("p (r c) -> p r c", c=GRID_W) for b in box_v]
                        hs = pool_h[:, kt, 0:N_SAMPLE].rearrange("p (r c) -> p r c", c=GRID_W)
                        link(V.memset(box_h[0][:], 0.0))
                        link(V.tensor_copy(H[0][:, :, 8:72], hs))
                        src, s = 0, 1
                        lo_c, hi_c = 8 - w // 2, 72 - w // 2
                        while s < w:
                            end = hi_c + w - 2 * s
                            if 2 * s == w:
                                out_ap = B[0][:, 8:16, :]
                            else:
                                out_ap = H[1 - src][:, :, lo_c:end]
                            link(V.tensor_tensor(out_ap, H[src][:, :, lo_c:end], H[src][:, :, lo_c + s:end + s], ALU.add))
                            src, s = 1 - src, 2 * s
                        m = box_m[:, 0:N_SAMPLE].rearrange("p (r c) -> p r c", c=GRID_W)
                        if w // 2 >= ROWS:
                            link(V.tensor_reduce(box_h[1][:, 0:GRID_W],
                                                 B[0][:, 8:16, :].rearrange("p r c -> p c r"), AX.X, ALU.add))
                            link(V.tensor_tensor(m, box_h[1][:, 0:GRID_W].rearrange("p (r c) -> p r c", r=1).broadcast_to([P, ROWS, GRID_W]),
                                                 inv[:, g * T:g * T + N_SAMPLE].rearrange("p (r c) -> p r c", c=GRID_W), ALU.mult))
                        else:
                            src, s = 0, 1
                            lo_r, hi_r = 8 - w // 2, 16 - w // 2
                            while s < w:
                                end = hi_r + w - 2 * s
                                link(V.tensor_tensor(B[1 - src][:, lo_r:end, :], B[src][:, lo_r:end, :],
                                                     B[src][:, lo_r + s:end + s, :], ALU.add))
                                src, s = 1 - src, 2 * s
                            link(V.tensor_tensor(m, B[src][:, lo_r:hi_r, :],
                                                 inv[:, g * T:g * T + N_SAMPLE].rearrange("p (r c) -> p r c", c=GRID_W), ALU.mult))
                            if w > 2:
                                link(V.memset(B[0][:, 0:8, :], 0.0))
                                link(V.memset(B[0][:, 16:24, :], 0.0))
                        link(V.memset(box_h[1][:, 0:144], 0.0))
                        link(V.tensor_copy(box_h[1][:, 8:136], pool_h[:, kt, N_SAMPLE:T]))
                        offs, src, s = (0, 160), 0, 1
                        lo_c, hi_c = 8 - w // 2, 136 - w // 2
                        while s < w:
                            end = hi_c + w - 2 * s
                            a, b = offs[src], offs[1 - src]
                            link(V.tensor_tensor(box_h[1][:, b + lo_c:b + end], box_h[1][:, a + lo_c:a + end],
                                                 box_h[1][:, a + lo_c + s:a + end + s], ALU.add))
                            src, s = 1 - src, 2 * s
                        a = offs[src]
                        link(V.tensor_tensor(box_m[:, N_SAMPLE:T], box_h[1][:, a + lo_c:a + hi_c],
                                             inv[:, g * T + N_SAMPLE:(g + 1) * T], ALU.mult))
                        V.tensor_tensor(pool_d[:, kt, :], box_m[:], pool_h[:, kt, :], ALU.subtract).then_inc(pool_ready, 1)
                        if layer == 0 and kt == 0:
                            mod_tiles(EARLY // SLOTS + 1)
                        if kt == 1:
                            link(V.tensor_tensor(sg[:], sg[:], mod[:, layer % 2, 32:48], ALU.mult))
                        for group in {1: (0,), 2: (1,), 3: (2,), 4: (3,), 5: (4,), 6: (5,)}.get(kt, ()):
                            dve.wait_ge(job_done, late_mods(layer) + SLOTS * (group + 1))
                            for c in range(SLOTS):
                                mod_tile(layer * CHUNKS_MOD + CHUNKS_MOD // 2 + SLOTS * group + c, 0, layer,
                                         LATE_AT[group % 2] + 4 * c)
                        for u in {3: (0, 1), 5: (2, 3), 7: (4, 5, 6, 7)}.get(kt, ()):
                            dve.wait_ge(pool_done, KT * pools[layer] + u + 1)
                            add_x(u, result[1 + u % 3], sg, 2 * u).then_inc(x_ready, 1)
                elif kind == 1:
                    n0, t0 = first[("hgrn_in", layer)], first_t[("hgrn_in", layer)]
                    dve.wait_ge(mixer_landed, mixer_loads[layer])
                    lower_bounds(layer)
                    def take(h, part):
                        n, t = n0 + 5 * h + part, t0 + 5 * h + part
                        ps = result[n % 2]
                        if part == 0:
                            dve.wait_ge(job_done, t + 1)
                            if h:
                                dve.wait_ge(level_done, (h - 1) * (LEVELS + 1) + 1)
                            V.tensor_copy(q[:], ps).then_inc(job_used, 1)
                        elif part < 3:
                            dve.wait_ge(sig_done, 3 * h + part)
                            f, at = (f_f, f_b)[part - 1], (part - 1) * KT + h
                            V.tensor_scalar(f[:], f[:], lb[:, 2 * KT + at:2 * KT + at + 1], lb[:, at:at + 1],
                                            ALU.mult, ALU.add).then_inc(job_used, 1)
                        elif part == 3:
                            dve.wait_ge(job_done, t + 1)
                            V.tensor_copy(v_t[:], ps).then_inc(job_used, 1)
                        else:
                            dve.wait_ge(sig_done, 3 * h + 3)
                            V.tensor_tensor(gates[h % 2][:], ps, gates[h % 2][:], ALU.mult).then_inc(job_used, 1)

                    def begin(h):
                        dve.wait_ge(job_used, n0 + 5 * (h + 1))
                        link(V.tensor_scalar(kf[:], f_f[:], -1.0, 1.0, ALU.mult, ALU.add))
                        link(V.tensor_scalar(kb[:], f_b[:], -1.0, 1.0, ALU.mult, ALU.add))
                        V.tensor_tensor(k_sum[:], kf[:], kb[:], ALU.add).then_inc(level_ready, 1)
                        if h:
                            dve.wait_ge(o_done, h)
                        link(V.tensor_tensor(qf[:], q[:], f_f[:], ALU.mult))
                        V.tensor_tensor(qb[:], q[:], f_b[:], ALU.mult).then_inc(level_ready, 1)

                    for part in range(5):
                        take(0, part)
                    for h in range(HEADS):
                        if h == 0:
                            begin(0)
                        dve.wait_ge(v_turned, h + 1)
                        V.tensor_copy(v_tok[:], acc[2][:, 0:T]).then_inc(v_ready, 1)
                        if h:
                            dve.wait_ge(o_moved, h)
                            head_norm(hd, sq[1], norms_h[:, 0:1], gates[(h - 1) % 2])
                        tf, tb = f_f[:, 0:T], f_b[:, 0:T]
                        t_at = 0
                        for level in range(LEVELS + 1):
                            s = 2 + (level + 1) % 2
                            dve.wait_ge(level_done, h * (LEVELS + 1) + level + 1)
                            ps3 = acc[s][:, 0:T].rearrange("p (c t) -> p c t", t=P)
                            sc3 = scores[:].rearrange("p (c t) -> p c t", t=P)
                            mk = masks[:, level * P:(level + 1) * P].rearrange("p (c t) -> p c t", c=1).broadcast_to([P, 5, P])
                            if level == 0:
                                V.tensor_tensor(sc3, ps3, mk, ALU.mult).then_inc(masked, 1)
                                continue
                            m = 1 << (level - 1)
                            nb = T // (2 * m)

                            def halves(t, half):
                                return t[:, 0:T].rearrange("p (b h m) -> p b h m", h=2, m=m)[:, :, half, :]

                            def total(t, half):
                                return t.rearrange("p (b h) -> p b h", h=2)[:, :, half:half + 1]

                            for dst, half, t in ((qf, 1, tf), (kf, 0, tf), (qb, 0, tb), (kb, 1, tb)):
                                V.tensor_tensor(halves(dst, half), halves(dst, half),
                                                total(t, 1 - half).broadcast_to([P, nb, m]), ALU.mult)
                            new = []
                            for t, store in ((tf, tot_f), (tb, tot_b)):
                                out_t = store[:, t_at:t_at + nb]
                                ins = V.tensor_tensor(out_t.rearrange("p (b h) -> p b h", h=1), total(t, 0), total(t, 1), ALU.mult)
                                new.append(out_t)
                            ins.then_inc(level_ready, 1)
                            tf, tb = new
                            t_at += nb
                            dve.wait_ge(masked, h * (LEVELS + 1) + level)
                            V.copy_predicated(sc3, mk.bitcast(U32), ps3).then_inc(masked, 1)
                            if level == 1 and h:
                                low_o(hd, h - 1)
                                hd += 1
                            if h + 1 < HEADS and level in (2, 4, 6, 7):
                                take(h + 1, (2, 4, 6, 7).index(level))
                        dve.wait_ge(kt_turned, h + 1)
                        link(V.tensor_copy(kf[:], acc[2][:, 0:T]))
                        V.tensor_copy(kb[:], acc[3][:, 0:T]).then_inc(kt_ready, 1)
                        dve.wait_ge(ds_done, h + 1)
                        dve.wait_ge(s0_landed, 32 * (h + 1))
                        if h:
                            dve.wait_ge(st_stored, 16 * h)
                        V.tensor_copy(st_out[:, 0:P], acc[2][:, 3 * P:4 * P])
                        V.tensor_copy(st_out[:, P:2 * P], acc[2][:, 7 * P:8 * P]).then_inc(st_ready, 1)
                        for u in range(3):
                            for base, c, to, t, at in ((0, u, u + 1, tf, u), (4, 3 - u, 2 - u, tb, 4 + u)):
                                ins = V.scalar_tensor_tensor(out=states[:, (base + to) * P:(base + to + 1) * P],
                                                             in0=states[:, (base + c) * P:(base + c + 1) * P],
                                                             scalar=t[:, c:c + 1], in1=acc[2][:, at * P:(at + 1) * P],
                                                             op0=ALU.mult, op1=ALU.add)
                                if u < 2 or base == 0:
                                    link(ins)
                                else:
                                    ins.then_inc(states_ready, 1)
                        if h + 1 < HEADS:
                            take(h + 1, 4)
                            begin(h + 1)
                    dve.wait_ge(o_moved, HEADS)
                    head_norm(hd, sq[1], norms_h[:, 0:1], gates[(HEADS - 1) % 2])
                    low_o(hd, HEADS - 1)
                    hd += 1
                    project(first[("hgrn_out", layer)], first_t[("hgrn_out", layer)], layer)
                else:
                    n0, t0 = first[("diff_in", layer)], first_t[("diff_in", layer)]
                    dve.wait_ge(mixer_landed, mixer_loads[layer])
                    lam_init = 0.8 - 0.6 * math.exp(-0.3 * layer)
                    for u in range(2):
                        a = 128 * u
                        link(V.tensor_tensor(lam_in[:, a:a + 64], lam_in[:, a:a + 64], lam_in[:, a + 64:a + 128], ALU.mult))
                        link(V.tensor_reduce(small[:, u:u + 1], lam_in[:, a:a + 64], AX.X, ALU.add))
                    V.tensor_scalar(small[:, 7:8], small[:, 0:1], 1.0, None, ALU.mult).then_inc(lam_sem, 1)
                    dve.wait_ge(lam_sem, 2)
                    link(V.tensor_tensor(small[:, 4:5], small[:, 3:4], small[:, 2:3], ALU.subtract))
                    link(V.tensor_scalar(small[:, 5:6], small[:, 4:5], -lam_init, None, ALU.add))
                    link(V.tensor_scalar(small[:, 6:7], norms_h[:, 1:2], 1.0 - lam_init, None, ALU.mult))
                    qt = 0
                    def take(h, part):
                        dve.wait_ge(job_done, t0 + 3 * h + part + 1)
                        V.tensor_copy((dq, dk, dv_t)[part][:], result[0]).then_inc(job_used, 1)

                    def maxima(tile):
                        nk = NK if tile < 4 else P
                        dve.wait_ge(sc_done, 5 * h + tile + 1)
                        V.tensor_reduce(small[:, 8:9], acc[1][:, 0:nk], AX.X, ALU.max)
                        link(V.tensor_reduce(small[:, 9:10], acc[2][:, 0:nk], AX.X, ALU.max))
                        V.tensor_scalar(small[:, 10:12], small[:, 8:10], -SCALE, None, ALU.mult).then_inc(mx_ready, 1)

                    for part in range(3):
                        take(0, part)
                    for h in range(HEADS):
                        if h:
                            dve.wait_ge(kv_stored, 32 * h)
                        dve.wait_ge(job_used, n0 + 3 * (h + 1))
                        dve.wait_ge(v_turned, HEADS + h + 1)
                        V.tensor_copy(dv_tok[:], acc[2][:, 0:T]).then_inc(v_ready, 1)
                        dve.wait_ge(rot_done, h + 1)
                        V.tensor_copy(qr[:, 512:T], dq[:, 512:T])
                        V.tensor_copy(kr[:, 512:T], dk[:, 512:T])
                        for part, (src, dst) in enumerate(((dq, qr), (dk, kr))):
                            link(V.tensor_tensor(dst[:, 0:512], src[:, 0:512], cos[:], ALU.mult))
                            link(V.tensor_tensor(sq[1][:, 0:512], acc[1][:, part * 512:(part + 1) * 512], sin[:], ALU.mult))
                            ins = V.tensor_tensor(dst[:, 0:512], dst[:, 0:512], sq[1][:, 0:512], ALU.add)
                            if part == 0:
                                link(ins)
                            else:
                                ins.then_inc(qk_ready, 1)
                        if h:
                            head_norm(hd, o_sb, small[:, 6:7], None)
                        maxima(0)
                        if h:
                            low_o(hd, h - 1)
                            hd += 1
                        for tile in range(5):
                            nk = NK if tile < 4 else P
                            dve.wait_ge(exp_done, 2 * qt + 2)
                            link(V.reciprocal(small[:, 14:16], small[:, 12:14]))
                            link(V.tensor_tensor(small[:, 16:17], small[:, 15:16], small[:, 5:6], ALU.mult))
                            link(V.tensor_scalar(prob[0][:, 0:nk], prob[0][:, 0:nk], small[:, 14:15], None, ALU.mult))
                            V.scalar_tensor_tensor(out=prob[0][:, 0:nk], in0=prob[1][:, 0:nk], scalar=small[:, 16:17],
                                                   in1=prob[0][:, 0:nk], op0=ALU.mult, op1=ALU.add).then_inc(w_ready, 1)
                            if tile < 4:
                                maxima(tile + 1)
                            if h + 1 < HEADS and tile in (1, 3, 4):
                                take(h + 1, tile // 2)
                            dve.wait_ge(pv_done, qt + 1)
                            if tile == 0 and h:
                                dve.wait_ge(o_ready, hd)
                            V.tensor_copy(o_sb[:, tile * P:(tile + 1) * P], acc[3][:, 768:896]).then_inc(o_copied, 1)
                            qt += 1
                    head_norm(hd, o_sb, small[:, 6:7], None)
                    low_o(hd, HEADS - 1)
                    hd += 1
                    project(first[("diff_out", layer)], first_t[("diff_out", layer)], layer)
                norm(2 * layer + 1, False)
                dve.wait_ge(conv_landed, 16 * (layer + 1))
                g_at = NPAIR * layer
                for what, p0, count, n, t, mods, k in segments(layer):
                    if what == "up":
                        def gate(d, side, used):
                            dve.wait_ge(job_used, used)
                            dve.wait_ge(silu_done, d + 1)
                            V.tensor_tensor(sil[side][:], sil[side][:], acc_v[side][:], ALU.mult).then_inc(gated, 1)

                        def low_g(d, side, slot):
                            dve.wait_ge(g_rounded, d + 1)
                            V.tensor_tensor(g_lo[:, slot, :], sil[side][:], g_hi[:, slot, :].bitcast(F32),
                                            ALU.subtract).then_inc(g_ready, 1)

                        def body(i, fresh, n=n, p0=p0, mods=mods, k=k):
                            for pair in range(2):
                                p = i * 2 + (p0 + pair)
                                done = i * 2 + (g_at + p0 + pair)
                                j = 2 * pair
                                views = []
                                for side, dst in enumerate((acc_a[pair], acc_v[pair])):
                                    u = result[j + side]
                                    views.append((u[:, 0:N_SAMPLE].rearrange("p (r c) -> p r c", c=GRID_W),
                                                  dst[:, 0:N_SAMPLE].rearrange("p (r c) -> p r c", c=GRID_W),
                                                  u[:, N_SAMPLE:T], dst[:, N_SAMPLE:T], p * 20 + side * 10))
                                prev = (1 - pair, (p0 - 1) % RING_G if isinstance(i, int) and i + pair == 0 else
                                        i * 2 + (p0 % RING_G + pair - 1))
                                taps = [(dy, dx) for dy in (-1, 0, 1) for dx in (-1, 0, 1) if (dy, dx) != (0, 0)]
                                for step, (dy, dx) in enumerate([("p", -1), ("p", 1)] + taps):
                                    if pair or not fresh:
                                        if step == 4:
                                            gate(done - 1, prev[0], i * SLOTS + (n + j))
                                        if step == 7:
                                            low_g(done - 1, *prev)
                                    for side in range(2):
                                        us, ds, up, dp, c10 = views[side]
                                        if step == 0:
                                            dve.wait_ge(center_done, i * 4 + (2 * (g_at + p0 + pair) + side + 1))
                                            if mods:
                                                mod_tile(i * 4 + (k + j + side), j + side, layer + 1)
                                        if dy == "p":
                                            a, b = max(0, -dx), N_PROMPT - max(0, dx)
                                            src, out, w = up[:, a + dx:b + dx], dp[:, a:b], 4 + dx
                                        else:
                                            r0, r1 = max(0, -dy), ROWS - max(0, dy)
                                            a, b = max(0, -dx), GRID_W - max(0, dx)
                                            src, out, w = us[:, r0 + dy:r1 + dy, a + dx:b + dx], ds[:, r0:r1, a:b], 4 + 3 * dy + dx
                                        ins = V.scalar_tensor_tensor(out=out, in0=src, scalar=conv[:, bass.ds(c10 + w, 1)],
                                                                     in1=out, op0=ALU.mult, op1=ALU.add)
                                        if step == 9:
                                            ins.then_inc(job_used, 1)
                                        else:
                                            ins.then_inc(dve_step, 1)
                                            steps[0] = steps[0] + 1
                                        if step < 9 and not (step == 0 and side == 0):
                                            dve.wait_ge(dve_step, steps[0] - 1)
                                        if step == 8 and side == 1:
                                            dve.wait_ge(dve_step, steps[0])
                        linked = 40 if mods else 36
                        base = steps[0]
                        body(0, p0 != 20)
                        assert steps[0] == base + linked
                        if count > 2:
                            linked_loop(count // 2, linked, lambda i: body(i, False), start=1)
                        if p0 != 18:
                            last = g_at + p0 + count - 1
                            gate(last, 1, n + 2 * count)
                            low_g(last, 1, (p0 + count - 1) % RING_G)
                    else:
                        def body(i, n=n, t=t, mods=mods, k=k):
                            for j in range(SLOTS):
                                if mods:
                                    dve.wait_ge(job_done, t + 2 * j + 2)
                                    mod_tile(k + j, j, layer + 1)
                                else:
                                    dve.wait_ge(job_done, i * SLOTS + (t + j + 1))
                                for c0, c1, row in RANGES:
                                    ins = V.scalar_tensor_tensor(out=x[:, i * 4 + j, c0:c1], in0=result[j][:, c0:c1],
                                                                 scalar=mod[:, layer % 2, bass.ds(i * 8 + (2 * (40 + j) + row), 1)],
                                                                 in1=x[:, i * 4 + j, c0:c1], op0=ALU.mult, op1=ALU.add)
                                ins.then_inc(job_used, 1)
                        dve.wait_ge(job_used, n)
                        if mods:
                            body(0)
                            body(1, t=t + SLOTS, mods=False)
                        else:
                            with dve.Fori(0, 2) as i:
                                body(i)
            norm(2 * DEPTH, True)


def kernel(**inputs):
    import numpy as np
    import concourse.bacc as bacc
    from concourse.bass_utils import run_bass_kernel_spmd

    a = {k: np.asarray(v) for k, v in inputs.items()}

    def chan(v):
        return np.moveaxis(v.reshape(*v.shape[:-1], -1, P), -1, 0)

    def tiles(w):
        k, n = w.shape
        return w.reshape(k // P, P, n // P, P).transpose(2, 1, 0, 3).reshape(n // P, P, -1)

    f32 = np.float32
    weights = {}
    for layer, kind in enumerate(KINDS):
        if kind == 1:
            weights["hgrn_in", layer] = tiles(a["hgrn_w_in"][layer // 3])
            weights["hgrn_out", layer] = tiles(a["hgrn_w_out"][layer // 3])
        elif kind == 2:
            weights["diff_in", layer] = tiles(a["diff_w_in"][layer // 3])
            weights["diff_out", layer] = tiles(a["diff_w_out"][layer // 3])
        weights["up", layer] = tiles(a["ffn_w_up"][layer])
        weights["down", layer] = tiles(a["ffn_w_down"][layer])
        weights["mod", layer] = tiles(a["ada_w"][layer])
    wall = np.zeros((NTILES, P, KT * P), f32)
    for n, (what, layer, index, nk) in enumerate(PLAN):
        if what == "down":
            p0, count, o = index
            wall[n, :, :count * P] = weights[what, layer][o, :, p0 * P:(p0 + count) * P]
        else:
            wall[n] = weights[what, layer][index]
    twice = lambda v: np.repeat(v[..., None], 2, axis=-1)
    data = {
        "x": chan(np.concatenate([a["x_sample"][0], a["x_prompt"][0]])).transpose(0, 2, 1),
        "cond": chan(np.stack([a["c"][0], a["c_ctx"]])).transpose(0, 2, 1).reshape(P, -1),
        "ada_b": twice(chan(a["ada_b"])).reshape(P, DEPTH, -1),
        "norms": twice(chan(np.stack([v for i in range(DEPTH) for v in (a["norm1"][i], a["norm2"][i])]
                                     + [a["final_norm"]]))).reshape(P, 2 * DEPTH + 1, -1),
        "norms_h": np.stack([a["hgrn_norm"][0], a["diff_subln"][0]], axis=1),
        "ones_d": np.full((P, P), 1 / D_MODEL, f32),
        "ones_h": np.full((P, P), 1 / P, f32),
        "ident": np.eye(P, dtype=f32),
        "wall": wall,
        "pool_w": a["pool_w"].reshape(-1, 4, 2, P, 2, P).transpose(0, 3, 1, 2, 4, 5).reshape(-1, P, 4 * 2 * 256),
        "pool_scale": twice(chan(a["pool_scale"])).transpose(1, 0, 2, 3).reshape(-1, P, 2 * KT),
        "lb": chan(a["hgrn_lb"]).reshape(P, -1),
        "s0": a["state_hgrn"][0, 0],
        "cache_k": a["cache_k"][0, 0].transpose(1, 2, 3, 0).reshape(HEADS, P, PAST),
        "cache_v": a["cache_v"][0, 0].reshape(2, P, HEADS, P).transpose(2, 1, 0, 3).reshape(HEADS, P, PAST),
        "lam": np.repeat(a["diff_lambda"].reshape(1, -1), P, axis=0),
    }
    taps = np.concatenate([a["ffn_conv_w"].reshape(DEPTH, 9, -1), a["ffn_conv_b"][:, None]], axis=1)
    data["conv"] = taps.reshape(DEPTH, 10, 2, NPAIR, P).transpose(0, 4, 3, 2, 1).reshape(DEPTH, P, -1)
    def sizes(n, w):
        i = np.arange(n)
        return np.clip(i + w // 2, 0, n) - np.clip(i - w // 2, 0, n)

    inv = np.zeros((4, T), f32)
    for g, w in enumerate(POOL_WINDOWS):
        inv[g, :N_SAMPLE] = 1.0 / np.outer(sizes(ROWS, w), sizes(GRID_W, w)).reshape(-1)
        inv[g, N_SAMPLE:] = 1.0 / sizes(N_PROMPT, w)
    data["inv"] = np.broadcast_to(inv.reshape(1, -1), (P, 4 * T))
    masks = np.zeros((P, LEVELS + 1, P), f32)
    s, t = np.arange(P)[:, None], np.arange(P)[None, :]
    masks[:, 0] = s == t
    for level in range(1, LEVELS + 1):
        m = 1 << (level - 1)
        masks[:, level] = (s // (2 * m) == t // (2 * m)) & (s // m != t // m)
    data["masks"] = masks.reshape(P, -1)
    half, nf = 32, 16
    freq = 10000.0 ** (-np.arange(nf, dtype=f32) / nf)
    tok = np.arange(N_SAMPLE)
    d = np.arange(P) % 64
    pos = np.where((d < half)[:, None], tok[None, :] // GRID_W, tok[None, :] % GRID_W)
    angle = pos.astype(f32) * freq[d % nf][:, None].astype(f32)
    data["cos"], data["sin"] = np.cos(angle).astype(f32), np.sin(angle).astype(f32)
    turn = np.zeros((P, P), f32)
    for p in range(P):
        if p % 32 < nf:
            turn[p + nf, p] = -1
        else:
            turn[p - nf, p] = 1
    data["turn"] = turn
    data = {k: np.ascontiguousarray(v) for k, v in data.items()}
    outs = {"y": (P, KT, T), "new_state": (HEADS, P, 2 * P), "new_k": (HEADS, P, N_PROMPT), "new_v": (HEADS, P, N_PROMPT)}

    nc = bacc.Bacc("TRN2", target_bir_lowering=False, num_devices=1)
    dram = {k: nc.dram_tensor(f"in_{k}", v.shape, F32, kind="ExternalInput").ap() for k, v in data.items()}
    dram |= {k: nc.dram_tensor(f"out_{k}", v, F32, kind="ExternalOutput").ap() for k, v in outs.items()}
    trunk(nc, dram)
    got = run_bass_kernel_spmd(nc, [{f"in_{k}": v for k, v in data.items()}], core_ids=[0]).results[0]
    y = got["out_y"].transpose(2, 1, 0).reshape(T, D_MODEL)
    state = got["out_new_state"].reshape(HEADS, P, 2, P).transpose(2, 0, 1, 3)
    new_k = got["out_new_k"].transpose(2, 0, 1).reshape(N_PROMPT, HEADS, 2, 64)
    new_v = got["out_new_v"].transpose(1, 0, 2)
    return (y[None, N_SAMPLE:], y[None, :N_SAMPLE], state[None, None], new_k[None, None], new_v[None, None])
```
